# Optimizing a Trainium2 kernel written in Bass

```python
import math
import jax, jax.numpy as jnp
from jax import lax
import numpy as np

D_MODEL = 1024
BATCH = 1
SEQ = 512
DEPTH = 1
DEC_BATCH = 8
DEC_SEQ = 1
PAST_LEN = 2048
PAGE_SIZE = 128

HEAD_DIM = 64
SB_HEADS = 8
NSA_HEADS = 8
NSA_KV_HEADS = 2
NSA_GROUP = NSA_HEADS // NSA_KV_HEADS
SB_WIDTH = SB_HEADS * HEAD_DIM
NSA_WIDTH = NSA_HEADS * HEAD_DIM
MIX_WIDTH = SB_WIDTH + NSA_WIDTH
KV_WIDTH = NSA_KV_HEADS * HEAD_DIM
IN_COLS = 3 * SB_WIDTH + NSA_WIDTH + 3 * 2 * KV_WIDTH + 3 * NSA_HEADS
CMP_STRIDE = 16
CMP_RATIO = 2
CMP_BLK = CMP_STRIDE * CMP_RATIO
CMP_HID = 2 * HEAD_DIM
SEL_BLK = 64
TOP_N = 16
N_LOCAL = 2
WINDOW = 512
D_FF = 4 * D_MODEL
Q_BLK = 128
ROPE_THETA = 10000.0
EPS = 1e-6
NEG = -1e30
TINY = 1e-30
FORCE = 1e9

kernel_name = "hymba_stickbreak_nsa_decoder_step"

def rmsnorm(x, g):
    xf = x.astype(jnp.float32)
    y = xf * lax.rsqrt(jnp.mean(xf * xf, axis=-1, keepdims=True) + EPS)
    return (y * g.astype(jnp.float32)).astype(x.dtype)

def rope(x, pos):
    half = HEAD_DIM // 2
    inv = ROPE_THETA ** (-jnp.arange(half, dtype=jnp.float32) / half)
    ang = pos.astype(jnp.float32)[:, None] * inv[None, :]
    cos = jnp.cos(ang)[None, :, None, :]
    sin = jnp.sin(ang)[None, :, None, :]
    xf = x.astype(jnp.float32)
    x1, x2 = xf[..., :half], xf[..., half:]
    return jnp.concatenate([x1 * cos - x2 * sin, x2 * cos + x1 * sin], axis=-1).astype(x.dtype)

def masked_probs(s, mask):
    s = jnp.where(mask, s, NEG)
    m = jnp.max(s, axis=-1, keepdims=True)
    p = jnp.exp(s - m) * mask
    return p / jnp.maximum(jnp.sum(p, axis=-1, keepdims=True), TINY)

def project(h, w_in, pos):
    B, T, _ = h.shape
    z = h @ w_in
    sizes = (SB_WIDTH, SB_WIDTH, SB_WIDTH, NSA_WIDTH, 2 * KV_WIDTH, 2 * KV_WIDTH, 2 * KV_WIDTH, 3 * NSA_HEADS)
    offs = [int(o) for o in np.cumsum(sizes)[:-1]]
    q_sb, k_sb, v_sb, q_n, kv_c, kv_s, kv_w, g = jnp.split(z, offs, axis=-1)

    def heads(t, n):
        return t.reshape(B, T, n, HEAD_DIM)

    def kv_pair(t):
        t = t.reshape(B, T, 2, NSA_KV_HEADS, HEAD_DIM)
        return jnp.stack([rope(t[:, :, 0], pos), t[:, :, 1]], axis=2)

    gates = jax.nn.sigmoid(g.astype(jnp.float32)).reshape(B, T, NSA_HEADS, 3)
    return (heads(q_sb, SB_HEADS), heads(k_sb, SB_HEADS), heads(v_sb, SB_HEADS),
            rope(heads(q_n, NSA_HEADS), pos), kv_pair(kv_c), kv_pair(kv_s), kv_pair(kv_w), gates)

def sb_attend(q, k, v, q_pos, k_pos):
    z = jnp.einsum('bqhd,bshd->bhqs', q.astype(jnp.float32), k.astype(jnp.float32)) / math.sqrt(HEAD_DIM)
    mask = k_pos[None, :] < q_pos[:, None]
    log_1m = jnp.where(mask, jax.nn.log_sigmoid(-z), 0.0)
    after = lax.cumsum(log_1m, axis=3, reverse=True) - log_1m
    a = jnp.where(mask, jnp.exp(jax.nn.log_sigmoid(z) + after), 0.0)
    return jnp.einsum('bhqs,bshd->bqhd', a, v.astype(jnp.float32)).astype(q.dtype)

def unblock(o):
    nb, B, Q, H, dh = o.shape
    return o.transpose(1, 0, 2, 3, 4).reshape(B, nb * Q, H, dh)

def sb_prompt(q, k, v):
    T = q.shape[1]
    pos = jnp.arange(T)

    def blk(i):
        qs = i * Q_BLK
        qb = lax.dynamic_slice_in_dim(q, qs, Q_BLK, axis=1)
        return sb_attend(qb, k, v, qs + jnp.arange(Q_BLK), pos)

    return unblock(lax.map(blk, jnp.arange(T // Q_BLK)))

def nsa_compress(kv, w_ck1, w_ck2, w_cv1, w_cv2, pe_k, pe_v):
    B, N = kv.shape[:2]
    n_chunks = N // CMP_STRIDE
    n_cmp = n_chunks - CMP_RATIO + 1
    ch = kv[:, :n_chunks * CMP_STRIDE].reshape(B, n_chunks, CMP_STRIDE, 2, NSA_KV_HEADS, HEAD_DIM)
    blocks = jnp.concatenate([ch[:, j:j + n_cmp] for j in range(CMP_RATIO)], axis=2)

    def mlp(x, pe, w1, w2):
        x = (x + pe[None, None, :, None, :]).transpose(0, 3, 1, 2, 4).reshape(B, NSA_KV_HEADS, n_cmp, CMP_BLK * HEAD_DIM)
        return jax.nn.silu(x @ w1) @ w2

    kc = mlp(blocks[:, :, :, 0], pe_k, w_ck1, w_ck2)
    vc = mlp(blocks[:, :, :, 1], pe_v, w_cv1, w_cv2)
    ends = jnp.arange(n_cmp) * CMP_STRIDE + CMP_BLK - 1
    return kc, vc, ends

def nsa_prepare(kv_cmp, kv_slc, cw):
    kc, vc, c_end = nsa_compress(kv_cmp, *cw)
    B, N = kv_slc.shape[:2]
    n_sel = -(-N // SEL_BLK)
    pad = n_sel * SEL_BLK - N
    kvs = jnp.pad(kv_slc, ((0, 0), (0, pad), (0, 0), (0, 0), (0, 0)))
    kvs = kvs.reshape(B, n_sel, SEL_BLK, 2, NSA_KV_HEADS, HEAD_DIM).transpose(3, 0, 4, 1, 2, 5)
    c_start = jnp.arange(kc.shape[2]) * CMP_STRIDE
    s_start = jnp.arange(n_sel) * SEL_BLK
    overlap = ((c_start[:, None] < s_start[None, :] + SEL_BLK)
               & (c_start[:, None] + CMP_BLK > s_start[None, :])).astype(jnp.float32)
    return kc, vc, c_end, kvs[0], kvs[1], overlap

def group_q(q):
    B, Q = q.shape[:2]
    return q.astype(jnp.float32).reshape(B, Q, NSA_KV_HEADS, NSA_GROUP, HEAD_DIM).transpose(0, 2, 3, 1, 4)

def ungroup(o):
    B, K, G, Q, dh = o.shape
    return o.transpose(0, 3, 1, 2, 4).reshape(B, Q, K * G, dh)

def nsa_cmp_slc(q, q_pos, kc, vc, c_end, k_sel, v_sel, overlap):
    B = q.shape[0]
    qg = group_q(q)
    scale = HEAD_DIM ** -0.5
    s_c = jnp.einsum('bkgqd,bkcd->bkgqc', qg, kc.astype(jnp.float32)) * scale
    p_c = masked_probs(s_c, c_end[None, :] <= q_pos[:, None])
    o_c = jnp.einsum('bkgqc,bkcd->bkgqd', p_c, vc.astype(jnp.float32))
    n_sel = k_sel.shape[2]
    imp = jnp.einsum('bkgqc,cj->bkqj', p_c, overlap)
    blk = jnp.arange(n_sel)[None, :]
    cur = (q_pos // SEL_BLK)[:, None]
    forced = (blk == 0) | ((blk <= cur) & (blk > cur - N_LOCAL))
    imp = jnp.where(forced, FORCE, imp)
    imp = jnp.where(blk * SEL_BLK <= q_pos[:, None], imp, NEG)
    _, idx = lax.top_k(imp, min(TOP_N, n_sel))
    bi = jnp.arange(B)[:, None, None, None]
    ki = jnp.arange(NSA_KV_HEADS)[None, :, None, None]
    kg = k_sel[bi, ki, idx].astype(jnp.float32)
    vg = v_sel[bi, ki, idx].astype(jnp.float32)
    s_s = jnp.einsum('bkgqd,bkqnld->bkgqnl', qg, kg) * scale
    key_pos = idx[..., None] * SEL_BLK + jnp.arange(SEL_BLK)
    m_s = key_pos <= q_pos[None, None, :, None, None]
    sh = s_s.shape
    p_s = masked_probs(s_s.reshape(sh[:4] + (-1,)), m_s[:, :, None].reshape(sh[0], sh[1], 1, sh[3], -1)).reshape(sh)
    o_s = jnp.einsum('bkgqnl,bkqnld->bkgqd', p_s, vg)
    return ungroup(o_c), ungroup(o_s)

def win_attend(q, q_pos, kv, k_pos):
    qg = group_q(q)
    k = kv[:, :, 0].astype(jnp.float32)
    v = kv[:, :, 1].astype(jnp.float32)
    s = jnp.einsum('bkgqd,bskd->bkgqs', qg, k) * HEAD_DIM ** -0.5
    kp, qp = k_pos[None, :], q_pos[:, None]
    m = (kp <= qp) & (kp > qp - WINDOW) & (kp >= 0)
    return ungroup(jnp.einsum('bkgqs,bskd->bkgqd', masked_probs(s, m), v))

def nsa_queries(q, q_pos, gates, prep, win_kv, win_pos):
    o_c, o_s = nsa_cmp_slc(q, q_pos, *prep)
    o_w = win_attend(q, q_pos, win_kv, win_pos)
    o = gates[..., 0:1] * o_c + gates[..., 1:2] * o_s + gates[..., 2:3] * o_w
    return o.astype(q.dtype)

def mixer_out(o_sb, o_n, g_sb, g_nsa, w_out):
    B, T = o_sb.shape[:2]
    a = rmsnorm(o_sb.reshape(B, T, SB_WIDTH), g_sb)
    b = rmsnorm(o_n.reshape(B, T, NSA_WIDTH), g_nsa)
    return jnp.concatenate([a, b], axis=-1) @ w_out

def mixer_prompt(h, w_in, cw, g_sb, g_nsa, w_out):
    B, T, _ = h.shape
    pos = jnp.arange(T)
    q_sb, k_sb, v_sb, q_n, kv_c, kv_s, kv_w, gates = project(h, w_in, pos)
    o_sb = sb_prompt(q_sb, k_sb, v_sb)
    prep = nsa_prepare(kv_c, kv_s, cw)
    kv_w_pad = jnp.pad(kv_w, ((0, 0), (WINDOW, 0), (0, 0), (0, 0), (0, 0)))

    def blk(i):
        qs = i * Q_BLK
        qb = lax.dynamic_slice_in_dim(q_n, qs, Q_BLK, axis=1)
        gb = lax.dynamic_slice_in_dim(gates, qs, Q_BLK, axis=1)
        wkv = lax.dynamic_slice_in_dim(kv_w_pad, qs, WINDOW + Q_BLK, axis=1)
        wpos = qs - WINDOW + jnp.arange(WINDOW + Q_BLK)
        return nsa_queries(qb, qs + jnp.arange(Q_BLK), gb, prep, wkv, wpos)

    o_n = unblock(lax.map(blk, jnp.arange(T // Q_BLK)))
    out = mixer_out(o_sb, o_n, g_sb, g_nsa, w_out)
    return out, jnp.stack([k_sb, v_sb], axis=2), kv_c, kv_s, kv_w[:, T - min(WINDOW, T):]

def gather_pages(cache, page_table):
    pages = cache[page_table]
    B, NP, PS = pages.shape[:3]
    return pages.reshape((B, NP * PS) + pages.shape[3:])

def mixer_sample(h, cache_sb, cache_cmp, cache_slc, win_buf, page_table, w_in, cw, g_sb, g_nsa, w_out):
    B, T, _ = h.shape
    past = page_table.shape[1] * cache_sb.shape[1]
    pos = past + jnp.arange(T)
    q_sb, k_sb, v_sb, q_n, kv_c, kv_s, kv_w, gates = project(h, w_in, pos)
    sb_past = gather_pages(cache_sb, page_table)
    k_all = jnp.concatenate([sb_past[:, :, 0], k_sb], axis=1)
    v_all = jnp.concatenate([sb_past[:, :, 1], v_sb], axis=1)
    o_sb = sb_attend(q_sb, k_all, v_all, pos, jnp.arange(past + T))
    kvc_all = jnp.concatenate([gather_pages(cache_cmp, page_table), kv_c], axis=1)
    kvs_all = jnp.concatenate([gather_pages(cache_slc, page_table), kv_s], axis=1)
    prep = nsa_prepare(kvc_all, kvs_all, cw)
    W = win_buf.shape[1]
    win_all = jnp.concatenate([win_buf, kv_w], axis=1)
    win_pos = past - W + jnp.arange(W + T)
    o_n = nsa_queries(q_n, pos, gates, prep, win_all, win_pos)
    out = mixer_out(o_sb, o_n, g_sb, g_nsa, w_out)
    n_keep = min(WINDOW, W + T)
    return out, jnp.stack([k_sb, v_sb], axis=2), kv_c, kv_s, win_all[:, W + T - n_keep:]

def sq_relu_mlp(h, w_up, w_down):
    return jnp.square(jax.nn.relu(h @ w_up)) @ w_down

def setup_inputs(seed: int = 0) -> dict:
    key = jax.random.key(seed)
    ks = jax.random.split(key, 24)
    n_pages = PAST_LEN // PAGE_SIZE
    n_used = DEC_BATCH * n_pages
    n_phys = n_used + max(1, n_used // 4)
    win_len = min(WINDOW, PAST_LEN)

    def nrm(k, shape, scale=1.0):
        return jax.random.normal(k, shape, jnp.float32) * scale

    def gain(k, shape):
        return 1.0 + 0.02 * jax.random.normal(k, shape, jnp.float32)

    page_table = jax.random.permutation(ks[6], n_phys)[:n_used].reshape(DEC_BATCH, n_pages).astype(jnp.int32)
    return {
        "x_prompt": nrm(ks[0], (BATCH, SEQ, D_MODEL)),
        "x_sample": nrm(ks[1], (DEC_BATCH, DEC_SEQ, D_MODEL)),
        "cache_sb_kv": nrm(ks[2], (DEPTH, n_phys, PAGE_SIZE, 2, SB_HEADS, HEAD_DIM)),
        "cache_nsa_cmp_kv": nrm(ks[3], (DEPTH, n_phys, PAGE_SIZE, 2, NSA_KV_HEADS, HEAD_DIM)),
        "cache_nsa_slc_kv": nrm(ks[4], (DEPTH, n_phys, PAGE_SIZE, 2, NSA_KV_HEADS, HEAD_DIM)),
        "state_nsa_win_kv": nrm(ks[5], (DEPTH, DEC_BATCH, win_len, 2, NSA_KV_HEADS, HEAD_DIM)),
        "page_table": page_table,
        "w_in": nrm(ks[7], (DEPTH, D_MODEL, IN_COLS), D_MODEL ** -0.5),
        "w_cmp_k1": nrm(ks[8], (DEPTH, CMP_BLK * HEAD_DIM, CMP_HID), (CMP_BLK * HEAD_DIM) ** -0.5),
        "w_cmp_k2": nrm(ks[9], (DEPTH, CMP_HID, HEAD_DIM), CMP_HID ** -0.5),
        "w_cmp_v1": nrm(ks[10], (DEPTH, CMP_BLK * HEAD_DIM, CMP_HID), (CMP_BLK * HEAD_DIM) ** -0.5),
        "w_cmp_v2": nrm(ks[11], (DEPTH, CMP_HID, HEAD_DIM), CMP_HID ** -0.5),
        "pe_cmp_k": nrm(ks[12], (DEPTH, CMP_BLK, HEAD_DIM), 0.1),
        "pe_cmp_v": nrm(ks[13], (DEPTH, CMP_BLK, HEAD_DIM), 0.1),
        "g_sb_out": gain(ks[14], (DEPTH, SB_WIDTH)),
        "g_nsa_out": gain(ks[15], (DEPTH, NSA_WIDTH)),
        "w_out": nrm(ks[16], (DEPTH, MIX_WIDTH, D_MODEL), MIX_WIDTH ** -0.5),
        "g_attn_norm": gain(ks[17], (DEPTH, D_MODEL)),
        "g_mlp_norm": gain(ks[18], (DEPTH, D_MODEL)),
        "w_up": nrm(ks[19], (DEPTH, D_MODEL, D_FF), D_MODEL ** -0.5),
        "w_down": nrm(ks[20], (DEPTH, D_FF, D_MODEL), D_FF ** -0.5),
        "g_final": gain(ks[21], (D_MODEL,)),
    }

def reference(x_prompt, x_sample, cache_sb_kv, cache_nsa_cmp_kv, cache_nsa_slc_kv, state_nsa_win_kv, page_table,
              w_in, w_cmp_k1, w_cmp_k2, w_cmp_v1, w_cmp_v2, pe_cmp_k, pe_cmp_v, g_sb_out, g_nsa_out, w_out,
              g_attn_norm, g_mlp_norm, w_up, w_down, g_final):
    xp, xs = x_prompt, x_sample
    sb_p, sb_s, cmp_p, cmp_s, slc_p, slc_s, win_p, win_s = [], [], [], [], [], [], [], []
    for l in range(DEPTH):
        cw = (w_cmp_k1[l], w_cmp_k2[l], w_cmp_v1[l], w_cmp_v2[l], pe_cmp_k[l], pe_cmp_v[l])
        mix, a, b, c, d = mixer_prompt(rmsnorm(xp, g_attn_norm[l]), w_in[l], cw, g_sb_out[l], g_nsa_out[l], w_out[l])
        xp = xp + mix
        xp = xp + sq_relu_mlp(rmsnorm(xp, g_mlp_norm[l]), w_up[l], w_down[l])
        sb_p.append(a); cmp_p.append(b); slc_p.append(c); win_p.append(d)
        mix, a, b, c, d = mixer_sample(rmsnorm(xs, g_attn_norm[l]), cache_sb_kv[l], cache_nsa_cmp_kv[l],
                                       cache_nsa_slc_kv[l], state_nsa_win_kv[l], page_table,
                                       w_in[l], cw, g_sb_out[l], g_nsa_out[l], w_out[l])
        xs = xs + mix
        xs = xs + sq_relu_mlp(rmsnorm(xs, g_mlp_norm[l]), w_up[l], w_down[l])
        sb_s.append(a); cmp_s.append(b); slc_s.append(c); win_s.append(d)
    y_prompt = rmsnorm(xp, g_final)
    y_sample = rmsnorm(xs, g_final)
    return (y_prompt, y_sample,
            jnp.stack(sb_p), jnp.stack(sb_s),
            jnp.stack(cmp_p), jnp.stack(cmp_s),
            jnp.stack(slc_p), jnp.stack(slc_s),
            jnp.stack(win_p), jnp.stack(win_s))


_drawn_inputs = setup_inputs


def setup_inputs(seed=0):
    import zlib

    import numpy as np

    out = dict(_drawn_inputs(seed))
    spreads = {}
    factors = {'pe_cmp_k': 2.71,
     'g_sb_out': 5.592,
     'g_nsa_out': 5.548,
     'g_attn_norm': 2.851,
     'g_mlp_norm': 3.82,
     'g_final': 2.763}
    for name, (base, spread) in spreads.items():
        noise = np.random.default_rng([zlib.crc32(name.encode()), seed]).standard_normal(out[name].shape)
        drawn = base * np.exp(spread * noise) if base else spread * noise
        out[name] = __import__('jax').numpy.asarray(drawn.astype(out[name].dtype))
    for name, factor in factors.items():
        out[name] = (out[name] * factor).astype(out[name].dtype)
    return out
```

```python
from contextlib import ExitStack

import numpy as np
import concourse.bass as bass
from concourse import mybir
from concourse.alu_op_type import AluOpType as ALU

ACT = mybir.ActivationFunctionType
AX = mybir.AxisListType
F32 = mybir.dt.float32
I32 = mybir.dt.int32
ds = bass.ds

P = 128
D = 1024
KD = D // P
SEQ, NT = 512, 4
B = 8
TOK = SEQ + B
T5 = NT + 1
H, DH, KVH, G = 8, 64, 2, 4
PAST, PAGE = 2048, 128
NPG = PAST // PAGE
NPHYS = 160
COLS = 2840
CB = COLS // 8
O_QS, O_KS, O_VS, O_QN, O_C, O_S, O_W, O_G = 0, 512, 1024, 1536, 2048, 2304, 2560, 2816
CH = 16
NCH = PAST // CH
NC = NCH - 1
NCP = SEQ // CH - 1
NSEL = 33
TOPN = 16
WIN = 512
NW = WIN // PAGE
DFF = 4096
FT = DFF // P
NEG, TINY, FORCE, EPS = -1e30, 1e-30, 1e9, 1e-6
SCALE = DH ** -0.5


class Fields:

    def __init__(self, start, end):
        self.at, self.end = start, end

    def take(self, n):
        lo = self.at
        self.at += n
        assert self.at <= self.end, (self.at, self.end)
        return lo


CONST_FIELDS = [("ident", P), ("ntri", P), ("nones", P), ("ones", P), ("causal", P), ("before", P),
                ("half", P), ("pagemap", (NPG + 1) * 16), ("overlap", NSEL), ("lower", NSEL * NSEL),
                ("cadd", NT * NCP), ("cmul", NT * NCP), ("cos", T5 * DH), ("sin", T5 * DH), ("eps", 1), ("one", 1)]
CONST_AT = {}
_n = 0
for _name, _w in CONST_FIELDS:
    CONST_AT[_name] = (_n, _w)
    _n += _w
NCONST = _n


def shape_constants():
    c = np.zeros((P, NCONST), np.float32)

    def put(name, a):
        lo, _ = CONST_AT[name]
        a = a.reshape(a.shape[0], -1)
        c[:a.shape[0], lo:lo + a.shape[1]] = a

    r = np.arange(P)
    put("ident", np.eye(P))
    put("ntri", -(r[:, None] >= r[None, :]).astype(np.float32))
    put("nones", -np.ones((P, P)))
    put("ones", np.ones((P, P)))
    put("causal", np.where(r[None, :] <= r[:, None], 0.0, NEG))
    put("before", (r[:, None] < r[None, :]).astype(np.float32))
    blk = np.arange(NSEL)
    put("half", (blk[:, None] % 2 == (r[None, :] >= P // 2)).astype(np.float32))
    put("pagemap", np.repeat((blk[:, None] // 2 == np.arange(NPG + 1)[None, :])[:, :, None], 16, 2).astype(np.float32))
    cs = np.arange(NC) * CH
    put("overlap", ((cs[:, None] < blk[None, :] * 64 + 64) & (cs[:, None] + 32 > blk[None, :] * 64)).astype(np.float32))
    put("lower", np.broadcast_to((blk[None, :] < blk[:, None])[None], (16, NSEL, NSEL)).astype(np.float32))
    q = np.arange(NT)[None, :, None] * P + r[:, None, None]
    ok = (np.arange(NCP) * CH + 31)[None, None, :] <= q
    put("cadd", np.where(ok, 0.0, NEG))
    put("cmul", ok.astype(np.float32))
    inv = np.float32(10000.0) ** (-np.arange(32, dtype=np.float32) / np.float32(32))
    pos = np.zeros((P, T5), np.float32)
    pos[:, :NT] = np.arange(NT)[None, :] * P + r[:, None]
    pos[:, NT] = PAST
    ang = pos[:, :, None] * inv[None, None, :].astype(np.float32)
    co, si = np.cos(ang), np.sin(ang)
    put("cos", np.concatenate([co, co], -1))
    put("sin", np.concatenate([-si, si], -1))
    put("eps", np.full((P, 1), EPS))
    put("one", np.full((P, 1), 1.0))
    return c


_MAX = ["m_max", "m_diag", "m_sub", "m_sum", "m_rec"]
SIGNALS = {
    "samples_pe": ["c_sc", "c_scT", "c_pT", "c_imp", "c_selT", "c_mask", "m_T", "m_b", "m_den", "m_T", "m_b", "m_den",
                   "s_c", "v_mm", "v_ss"],
    "samples_dve": ["att_done", "z_free", "c_s", "c_nm", "c_p", "c_pg", "c_sel", "c_selx", "c_selm"] + _MAX * 2
    + ["s_abs", "s_sp", "s_suf", "zero_set", "s_d", "v_sq", "v_st", "mix_ss"],
    "samples_act": ["c_e", "m_e", "m_e", "s_ln", "s_a", "v_rt", "mix_rt"],
}


PRIMED = {
    "pe": [f"{n}_mm{q}" for n in ("kq", "vq") for q in range(5)] + [f"ring_free{u}" for u in range(8)]
    + ["w2_mm0", "w2_mm1", "qs_mm", "up_free0", "up_free1", "dn_free0", "dn_free1", "y_mm0", "y_mm1"],
    "act": ["z_ev1", "z_ev3", "xT_ev0", "qs_ev", "up_ev0", "up_ev1"],
    "dve": ["win_free0", "win_free1", "z_ev0", "z_ev2", "z_ev4", "hid_ready0", "hid_ready1", "hid_ev0", "hid_ev1", "xT_ev1", "kvc_ev0", "kvc_ev1",
            "a_ready0", "a_ready1", "dn_ev0", "dn_ev1", "y_ev0", "y_ev1"],
    "pool": ["perm1_0", "perm1_1"],
}


class Chain:

    def __init__(self, eng, sem):
        self.eng, self.sem, self.n, self.off = eng, sem, 0, 0

    def __call__(self, ins):
        self.n += 1
        ins.then_inc(self.sem, 1)
        self.eng.wait_ge(self.sem, self.off + self.n)


class Turns:

    def __init__(self, chain, count, per):
        self.chain, self.count, self.per = chain, count, per

    def __enter__(self):
        c = self.chain
        self.first = c.n
        self.loop = c.eng.Fori(0, self.count)
        i = self.loop.__enter__()
        c.off = i * self.per
        return i

    def __exit__(self, *e):
        c = self.chain
        if e[0] is None:
            assert c.n - self.first == self.per, (c.n - self.first, self.per)
        c.off = 0
        c.n = self.first + self.count * self.per
        return self.loop.__exit__(*e)


def decoder_step(nc, A, O):
    with ExitStack() as ctx:
        sems = {}

        def signal(name, v):
            group = [g for g, order in SIGNALS.items() if name in order][0]
            return sem(group), [n for n, x in enumerate(SIGNALS[group], 1) if x == name][v - 1]

        def prime(eng, who):
            for name in PRIMED[who]:
                eng.sem_inc(sem(name), 1)

        def sem(name):
            if name not in sems:
                sems[name] = ctx.enter_context(nc.semaphore(name))
            return sems[name]

        TOTAL = 52900
        arena = ctx.enter_context(nc.sbuf_tensor("arena", [P, TOTAL], F32))
        pt = ctx.enter_context(nc.sbuf_tensor("page_ids", [1, B * NPG], I32))
        bank = [ctx.enter_context(nc.psum_tensor(f"bank{i}", [P, 512], F32)) for i in range(8)]
        sbq_dram = nc.dram_tensor("sb_queries", (B, 512), F32, kind="Internal").ap()

        def view(lo, *dims):
            n = int(np.prod(dims))
            a = arena[:, lo:lo + n]
            names = "abcd"[:len(dims)]
            if len(dims) > 1:
                a = a.rearrange(f"p ({' '.join(names)}) -> p {' '.join(names)}", **dict(zip(names, dims)))
            return a

        allr = Fields(0, TOTAL)
        const = view(allr.take(NCONST), NCONST)

        def K(name):
            lo, w = CONST_AT[name]
            return const[:, lo:lo + w]

        ident, ntri, nones, ones = K("ident"), K("ntri"), K("nones"), K("ones")
        vrow = view(allr.take(P), P)
        vcol = view(allr.take(56), 56)
        st = view(allr.take(256), 256)
        zero = view(allr.take(P), P)
        z = view(allr.take(T5 * COLS), T5, COLS)
        sbqT = view(allr.take(4 * SEQ), 4, SEQ)
        sbkT = view(allr.take(4 * SEQ), 4, SEQ)
        nqT = view(allr.take(4 * SEQ), 4, SEQ)
        ksT = view(allr.take(SEQ), SEQ)
        kwT = view(allr.take(SEQ), SEQ)
        hT_at = allr.take(KD * TOK)
        hT = view(hT_at, KD, TOK)
        x_at = allr.take(T5 * D)
        x = view(x_at, T5, D)
        r_at = allr.at

        r = Fields(r_at, TOTAL)
        h_at = r.take(T5 * D)
        h = view(h_at, T5, D)
        win = [view(r.take(KD * CB), KD, CB) for _ in range(2)]
        r = Fields(r_at, TOTAL)
        ropeA, ropeB = view(r.take(512), 512), view(r.take(512), 512)
        r = Fields(r_at + 1024, TOTAL)
        qbd = view(r.take(B * H), B, H)
        snew = view(r.take(2 * H), 2, H)
        qsc = view(r.take(512), 512)
        newrow = view(r.take(2 * B * H), 2, B, H)
        vnew = view(r.take(2 * B * P), 2, B, P)
        grow = view(r.take(B * 24), B, H, 3)
        kc = view(r.take((B + 1) * P), B + 1, P)
        vc = view(r.take((B + 1) * P), B + 1, P)
        slc = view(r.take(B * (NPG + 1) * H), B, NPG + 1, H)
        wsc = view(r.take(B * (NW + 1) * H), B, NW + 1, H)
        att_at = r.at
        w1 = [view(x_at + i * 2048, 16, P) for i in range(2)]
        w2 = [view(x_at + 4096 + i * DH, DH) for i in range(2)]
        pebias = view(x_at + 4224, 4)
        xT = [view(hT_at + i * 2048, KD, KVH, P) for i in range(2)]
        nat = [view(r.take(4096), CH, 2, KVH, DH) for _ in range(2)]
        hid = [view(r.take(256), KVH, P) for _ in range(4)]

        def per(kv, hh):
            return z[:, 2 * kv + hh, 0:1024].rearrange("p (t d) -> p t d", t=CH)

        a1 = Fields(x_at, r_at)
        r = Fields(att_at, TOTAL)
        ring = view(a1.take(8 * 512), 8, 512)
        qb = view(a1.take(2 * 512), 2, 512)
        quad = view(r.take(5 * 512), 5, 4, P)
        sbs = view(r.take(B * NPG * H), B, NPG, H)
        o_sb = view(r.take(NT * 512), NT, 512)
        o_n = view(r.take(NT * 512), NT, 512)
        wk_at = r.at
        kqT = view(wk_at, 5, 4, P)
        w = Fields(wk_at, TOTAL)
        prod = view(w.take(2 * 512), 2, 512)
        pbuf = view(w.take(2 * 512), 2, 512)
        ptb = view(w.take(2 * 512), 2, 512)
        w = Fields(hT_at, hT_at + KD * TOK)
        spb = view(w.take(2 * 512), 2, 512)
        ebuf = view(w.take(2 * 512), 2, 512)
        abuf = view(w.take(2 * 512), 2, 512)
        srun = view(w.take(512), 512)
        w = Fields(wk_at, TOTAL)
        sps = view(w.take(1024), B, NPG, H)
        suf = view(w.take(1024), B, NPG, H)
        ofs = view(w.take(12 * 64), 12, 64)
        w = Fields(hT_at, hT_at + KD * TOK)
        s64 = view(w.take(9 * P), 9, P)
        rankA = view(w.take(NSEL * NSEL), NSEL, NSEL)
        rankB = view(w.take(NSEL * NSEL), NSEL, NSEL)
        selx = view(w.take(272), NPG + 1, 16)
        selm = view(w.take(272), NPG + 1, 16)
        pcT = view(w.take(64), 64)
        aT_at = NCONST + P + 56 + 256 + P
        aT = view(aT_at, FT, TOK)
        wout = view(aT_at, KD, D)
        assert aT_at + FT * TOK <= hT_at
        r = Fields(r_at, TOTAL)
        h2 = view(r.take(T5 * D), T5, D)
        upw = [view(r.take(KD * P), KD, P) for _ in range(2)]
        dnw = [view(r.take(FT * P), FT, P) for _ in range(2)]
        yT = [view(r.take(TOK), TOK) for _ in range(2)]
        gfin = view(r.take(D), D)
        rows = [P] * NT + [B]

        def over(ap, axis, n):
            a = ap.unsqueeze(axis)
            shape = list(a.shape)
            shape[axis] = n
            return a.broadcast_to(shape)

        def place(hd):
            return (hd % G) * KVH + hd // G

        block = ctx.enter_context(nc.Block())
        xp, xs = A["x_prompt"][0], A["x_sample"].rearrange("b o d -> (b o) d")
        c_sb, c_cmp, c_slc = A["cache_sb_kv"][0], A["cache_nsa_cmp_kv"][0], A["cache_nsa_slc_kv"][0]
        w_in, w_up, w_down, w_out = A["w_in"][0], A["w_up"][0], A["w_down"][0], A["w_out"][0]

        @block.sync
        def _(sp):
            sp.dma_start(const, A["consts"]).then_inc(sem("const_in"), 16)
            sp.dma_start(x[:, 0:NT, :], xp.rearrange("(t p) d -> p t d", p=P)).then_inc(sem("x_in"), 16)
            sp.dma_start(x[0:B, NT, :], xs).then_inc(sem("x_in"), 16)
            for r0, n, src in ((0, 8, A["g_attn_norm"][0]), (8, 8, A["g_mlp_norm"][0]), (16, 4, A["g_sb_out"][0])):
                sp.dma_start(vrow[r0:r0 + n, :], src.rearrange("(r c) -> r c", c=P)).then_inc(sem("vrow_in"), 16)
            for two in range(2):
                sp.dma_start(vrow[20:24, two * DH:(two + 1) * DH],
                    A["g_nsa_out"][0].rearrange("(two t d) -> two t d", two=2, t=4)[two]).then_inc(sem("vrow_in"), 16)
            for r0, src in ((24, A["pe_cmp_k"][0]), (40, A["pe_cmp_v"][0])):
                sp.dma_start(vrow[r0:r0 + 16, :], src.rearrange("(m two) d -> m (two d)", two=2)).then_inc(sem("vrow_in"), 16)
            sp.dma_start(pt[:, :], A["page_table"].rearrange("(o b) n -> o (b n)", o=1)).then_inc(sem("pages_in"), 16)
            w_in_v = w_in.rearrange("(k p) c -> p k c", p=P)
            with sp.Fori(0, 4) as i:
                for u in range(2):
                    sp.wait_ge(sem(f"win_free{u}"), i + 1)
                    sp.dma_start(win[u][:, :, :], w_in_v[:, :, ds(i * (2 * CB) + u * CB, CB)]).then_inc(sem(f"win_in{u}"), 16)
            sp.wait_ge(sem("h_ready"), 1)
            for kv, n in enumerate(("w_cmp_k1", "w_cmp_v1")):
                sp.dma_start(w1[kv][:, :, :], A[n][0].rearrange("(m p) c -> p m c", p=P)).then_inc(sem("cmpw_in"), 16)
            for kv, n in enumerate(("w_cmp_k2", "w_cmp_v2")):
                sp.dma_start(w2[kv], A[n][0]).then_inc(sem("cmpw_in"), 16)
            sp.wait_ge(sem("pages_in"), 16)
            for t in range(T5):
                sp.wait_ge(sem(f"z_ev{t}"), 8 + 1)
            sp.wait_ge(sem("rope_done"), T5)
            with sp.Fori(0, 4) as i:
                for u in range(2):
                    sp.wait_ge(sem(f"perm1_{u}"), i + 1)
                    for p in range(NPG):
                        pg = sp.value_load(pt[0:1, ds(i * (2 * NPG) + u * NPG + p, 1)], min_val=0, max_val=NPHYS - 1)
                        sp.dma_start(nat[u][8 * p:8 * p + 8].rearrange("p t k h d -> p (t k h d)"),
                            c_cmp[ds(pg, 1)].rearrange("o (c t) k h d -> (o c) (t k h d)", t=CH)).then_inc(sem(f"nat_in{u}"), 16)
            sp.wait_ge(sem("cmp_stored"), 16)
            sp.wait_ge(sem("perm1_0"), 4 + 1)
            sp.dma_start(nat[0][0:NCP + 1].rearrange("p t k h d -> p (t k h d)"),
                O["cmp_p"][0, 0].rearrange("(c t) k h d -> c (t k h d)", t=CH)).then_inc(sem("nat_in0"), 16)
            sp.wait_ge(sem("kvc_ev0"), 9 + 1)
            sp.wait_ge(sem("kvc_ev1"), 9 + 1)
            win_v = A["state_nsa_win_kv"][0].rearrange("b (t p) k h d -> b p t k (h d)", p=P)

            def load_quads(kv):
                with sp.Fori(0, B) as b:
                    for q in range(5):
                        if kv == 0:
                            sp.wait_ge(sem(f"kq_mm{q}"), b + 1)
                        else:
                            sp.wait_ge(sem(f"vq_mm{q}"), b + 1)
                        for j in range(4 if q < 4 else 0):
                            pg = sp.value_load(pt[0:1, ds(b * NPG + 4 * q + j, 1)], min_val=0, max_val=NPHYS - 1)
                            sp.dma_start(quad[:, q, j, :], c_slc[ds(pg, 1), :, kv].rearrange("o s h d -> (o s) (h d)")).then_inc(sem(f"quad_in{q}"), 16)
                        if q == 4:
                            sp.dma_start(quad[:, 4], win_v[ds(b, 1), :, :, kv, :].rearrange("o p t c -> (o p) t c")).then_inc(sem("quad_in4"), 16)

            def load_pages(kv, b, r, first):
                for u in range(8):
                    sp.wait_ge(sem(f"ring_free{u}"), first + 2 * b + r + 1)
                    pg = sp.value_load(pt[0:1, ds(b * NPG + r * 8 + u, 1)], min_val=0, max_val=NPHYS - 1)
                    sp.dma_start(ring[:, u, :], c_sb[ds(pg, 1), :, kv].rearrange("o s h d -> (o s) (h d)")).then_inc(sem(f"ring_in{u}"), 16)

            load_quads(0)
            sp.wait_ge(sem("sbq_out"), 16)
            for b in range(B):
                if b >= 2:
                    sp.wait_ge(sem("k_red"), NPG * (b - 1))
                sp.dma_start(qb[:, b % 2, :], sbq_dram[b:b + 1, :].broadcast_to([P, 512])).then_inc(sem(f"qb_in{b % 2}"), 16)
                with sp.Fori(0, 2) as r:
                    load_pages(0, b, r, 0)
            with sp.Fori(0, B) as b:
                for r in range(2):
                    load_pages(1, b, r, 2 * B)
            for q in range(5):
                sp.wait_ge(sem(f"kq_mm{q}"), B + 1)
            load_quads(1)
            sp.wait_ge(*signal("z_free", 1))
            sp.wait_ge(sem("kv_out"), 16 * (B + 6))
            sp.wait_ge(sem("rows_in"), 96)
            for r0 in range(0, 4, 2):
                sp.dma_start(wout[:, r0:r0 + 2, :], w_out.rearrange("(k p) c -> p k c", p=P)[:, r0:r0 + 2, :]).then_inc(sem("wout_in"), 16)
            for two in range(2):
                sp.dma_start(wout[two * DH:(two + 1) * DH, 4:8, :],
                    w_out[512 + 256 * two:768 + 256 * two, :].rearrange("(t d) c -> d t c", d=DH)).then_inc(sem("wout_in"), 16)
            for u in range(8):
                sp.wait_ge(sem(f"ring_free{u}"), 4 * B + 1)
            sp.dma_start(x[:, 0:NT, :], xp.rearrange("(t p) d -> p t d", p=P)).then_inc(sem("x2_in"), 16)
            sp.dma_start(x[0:B, NT, :], xs).then_inc(sem("x2_in"), 16)
            sp.wait_ge(sem("mix_ready"), 2)
            sp.wait_ge(sem("mixT_mm"), 4)
            sp.dma_start(gfin, A["g_final"].rearrange("(o d) -> o d", o=1).broadcast_to([P, D])).then_inc(sem("gfin_in"), 16)
            w_up_v = w_up.rearrange("(k p) c -> p k c", p=P)
            with sp.Fori(0, FT // 2) as i:
                for u in range(2):
                    sp.wait_ge(sem(f"up_free{u}"), i + 1)
                    sp.dma_start(upw[u][:, :, :], w_up_v[:, :, ds(i * (2 * P) + u * P, P)]).then_inc(sem(f"up_in{u}"), 16)
            w_dn_v = w_down.rearrange("(k p) c -> p k c", p=P)
            with sp.Fori(0, KD // 2) as i:
                for u in range(2):
                    sp.wait_ge(sem(f"dn_free{u}"), i + 1)
                    sp.dma_start(dnw[u][:, :, :], w_dn_v[:, :, ds(i * (2 * P) + u * P, P)]).then_inc(sem(f"dn_in{u}"), 16)
            sp.wait_ge(sem("y_ready"), 1)
            sp.dma_start(O["y_p"][0].rearrange("(t p) d -> p t d", p=P), h2[:, 0:NT, :]).then_inc(sem("y_out"), 16)
            sp.dma_start(O["y_s"].rearrange("b o d -> (b o) d"), h2[0:B, NT, :]).then_inc(sem("y_out"), 16)
            sp.wait_ge(sem("y_out"), 32)

        @block.tensor
        def _(pe):
            T = nc.tensor
            prime(pe, "pe")

            def mm(out, l, r, start=True, stop=True, **k):
                return T.matmul(out, lhsT=l, rhs=r, start=start, stop=stop, **k)

            def tr(out, in_):
                n = in_.shape[0]
                return T.transpose(out, in_, ident[0:n, 0:n])

            def norm_transposes(src, turn):
                pe.wait_ge(sem("h_ready"), turn + 1)
                for k in range(KD):
                    if k >= 2:
                        pe.wait_ge(sem("hT_ev"), turn * 9 + k - 1)
                    for t in range(NT):
                        i = tr(bank[k % 2][:, t * P:(t + 1) * P], src[:, t, k * P:(k + 1) * P])
                    i.then_inc(sem("hT_mm"), 1)
                for k in range(KD):
                    i = tr(bank[2][:, k * B:(k + 1) * B], src[0:B, NT, k * P:(k + 1) * P])
                i.then_inc(sem("hT_mm"), 1)

            pe.wait_ge(sem("const_in"), 16)
            pe.wait_ge(sem("vrow_in"), 16 * 7)
            tr(bank[3][:, 0:56], vrow[0:56, :]).then_inc(sem("vcol_mm"), 1)
            norm_transposes(h, 0)
            pe.wait_ge(sem("vcol_ev"), 1)
            pe.wait_ge(sem("hT_ev"), 9)
            with pe.Fori(0, 4) as i:
                for u in range(2):
                    pe.wait_ge(sem(f"win_in{u}"), i * 16 + 16)
                    for t in range(T5):
                        pe.wait_ge(sem(f"z_ev{t}"), i * 2 + u + 1)
                        for k in range(KD):
                            ins = mm(bank[t][0:rows[t], 0:CB], hT[:, k, t * P:t * P + rows[t]], win[u][:, k, :],
                                     k == 0, k == KD - 1)
                        ins.then_inc(sem("z_mm"), 1)
            pe.wait_ge(sem("rope_done"), T5)
            for t in range(T5):
                pe.wait_ge(sem(f"z_ev{t}"), 8 + 1)
            src = [(lambda t, j=j: z[:, t, O_QS + j * P:O_QS + (j + 1) * P]) for j in range(4)]
            src += [(lambda t, j=j: z[:, t, O_KS + j * P:O_KS + (j + 1) * P]) for j in range(4)]
            src += [(lambda t, j=j: z[:, t, O_QN + j * P:O_QN + (j + 1) * P]) for j in range(4)]
            src += [(lambda t, o=o: z[:, t, o:o + P]) for o in (O_S, O_W)]
            for j, s in enumerate(src):
                if j >= 4:
                    pe.wait_ge(sem(f"qkT_ev{j % 2}"), (j - 4) // 2 + 1)
                for t in range(NT):
                    ins = tr(bank[j % 4][:, t * P:(t + 1) * P], s(t))
                ins.then_inc(sem("qkT_mm"), 1)
            for j in range(4):
                ins = tr(bank[4][:, j * B:(j + 1) * B], z[0:B, NT, O_QN + j * P:O_QN + (j + 1) * P])
            ins.then_inc(sem("qkT_mm"), 1)
            pe.wait_ge(sem("cmpw_in"), 64)
            for kv in range(2):
                for m in range(16):
                    ins = mm(bank[6][:, kv:kv + 1], w1[kv][:, m, :], vcol[:, 24 + 16 * kv + m:25 + 16 * kv + m],
                             m == 0, m == 15)
            ins.then_inc(sem("pe_mm"), 1)
            for j in range(2):
                pe.wait_ge(sem(f"qkT_ev{j}"), 7)
            pe.wait_ge(sem("qkT_ev0"), 8)
            pe.wait_ge(sem("pebias"), 2)

            def compress(c, u, i, n):
                nb = n - 1
                for kv in range(2):
                    if kv == 0:
                        pe.wait_ge(sem("perm0"), c + 1)
                    else:
                        pe.wait_ge(sem(f"perm1_{u}"), i + 1 + 1)
                    pe.wait_ge(sem(f"hid_ev{kv}"), c + 1)
                    for s in range(5):
                        if s < 4:
                            pe.wait_ge(sem(f"xT_ev{s % 2}"), c * 4 + kv * 2 + s // 2 + 1)
                            for j in range(2):
                                for hh in range(KVH):
                                    m = 2 * s + j
                                    ins = tr(bank[s % 2][:, (2 * j + hh) * P:(2 * j + hh) * P + n],
                                             per(kv, hh)[0:n, 2 * m:2 * m + 2, :].rearrange("p t d -> p (t d)"))
                            ins.then_inc(sem("xT_mm"), 1)
                        if s >= 1:
                            pe.wait_ge(sem(f"xT_ev{(s - 1) % 2}"), c * 4 + kv * 2 + (s - 1) // 2 + 1 + 1)
                            for m in (2 * s - 2, 2 * s - 1):
                                out = bank[2 + kv][:, 0:KVH * nb].rearrange("p (h c) -> p h c", h=KVH)
                                mm(out, w1[kv][:, m, :], xT[kv][:, m, :, 0:nb], m == 0, False)
                                ins = mm(out, w1[kv][:, 8 + m, :], xT[kv][:, m, :, 1:n], False, m == 7)
                            if kv == 1 and s == 4:
                                ins.then_inc(sem(f"hid_mm1"), 1)
                            elif s == 4:
                                ins.then_inc(sem("hid_mm0"), 1)
                pe.wait_ge(sem("hid_ready0"), c + 1 + 1)
                pe.wait_ge(sem("kvc_ev0"), c + 1)
                for hh in range(KVH):
                    ins = mm(bank[4][DH * hh:DH * (hh + 1), 0:nb], w2[0], hid[2][:, hh, 0:nb])
                ins.then_inc(sem("w2_mm0"), 1)
                pe.wait_ge(sem("hid_ready1"), c + 1 + 1)
                pe.wait_ge(sem("kvc_ev1"), c + 1)
                for hh in range(KVH):
                    ins = mm(bank[5][0:nb, DH * hh:DH * (hh + 1)], hid[3][:, hh, 0:nb], w2[1])
                ins.then_inc(sem("w2_mm1"), 1)

            with pe.Fori(0, 4) as i:
                for u in range(2):
                    compress(i * 2 + u, u, i, NCH)
            compress(B, 0, 4, NCP + 1)

            for kv in range(2):
                pe.wait_ge(sem(f"kvc_ev{kv}"), B + 1 + 1)
            with pe.Fori(0, B) as b:
                for q in range(5):
                    pe.wait_ge(sem(f"quad_in{q}"), (b + 1) * (64 if q < 4 else 16))
                    if q == 0:
                        pe.wait_ge(sem("qs_ev"), b + 1)
                    for j in range(4):
                        ins = tr(bank[q][:, j * P:(j + 1) * P], quad[:, q, j, :])
                    ins.then_inc(sem(f"kq_mm{q}"), 1)
                for q in range(5):
                    pe.wait_ge(sem("kq_ev"), b * 5 + q + 1)
                    for j in range(4):
                        c = (4 * q + j) * H
                        ins = mm(bank[5][:, c:c + H], kqT[:, q, j, :], qbd[:, ds(b, 1), :].rearrange("p o j -> p (o j)"))
                ins.then_inc(sem("qs_mm"), 1)
            pe.wait_ge(sem("qs_ev"), B + 1)

            for i in range(NT):
                if i >= 1:
                    pe.wait_ge(sem("cp_soft"), i)
                for n in range(H):
                    o = DH * (n // G)
                    ins = mm(bank[4 + n // G][:, (n % G) * NCP:(n % G + 1) * NCP], nqT[o:o + DH, n % G, i * P:(i + 1) * P],
                             kc[o:o + DH, B, 0:NCP])
                ins.then_inc(sem("cp_qk"), 1)
                pe.wait_ge(sem("cp_soft"), i + 1)
                for n in range(H):
                    if n == 0 and i >= 1:
                        pe.wait_ge(sem("cp_pT"), 2 * i)
                    ins = tr(bank[6 + n // 4][0:NCP, (n % 4) * P:(n % 4 + 1) * P], pbuf[:, 0, n * NCP:(n + 1) * NCP])
                    if n % 4 == 3:
                        ins.then_inc(sem("cp_tr"), 1)
                pe.wait_ge(sem("cp_pT"), 2 * i + 2)
                if i >= 2:
                    pe.wait_ge(sem("cp_out"), i - 1)
                for n in range(H):
                    o = DH * (n // G)
                    ins = mm(bank[i % 2][:, place(n) * DH:(place(n) + 1) * DH], ptb[0:NCP].rearrange("p a b -> p (a b)")[:, n * P:(n + 1) * P],
                             vc[0:NCP, B, o:o + DH])
                ins.then_inc(sem("cp_pv"), 1)
            pe.wait_ge(sem("cp_out"), NT)

            def sb_qk(hd, i):
                m = 4 * hd + 3 - i
                if m >= 2:
                    pe.wait_ge(sem("sb_a"), m - 1)
                if hd and i >= 2:
                    pe.wait_ge(sem("n_out"), 8 * hd)
                o = DH * (hd % 2)
                mm(bank[m % 2][:, 0:SEQ - i * P], sbkT[o:o + DH, hd // 2, i * P:(i + 1) * P],
                        sbqT[o:o + DH, hd // 2, i * P:SEQ], True, False, skip_group_check=True).then_inc(sem("sb_qk"), 1)

            def sb_sum(hd, i):
                m = 4 * hd + 3 - i
                pe.wait_ge(sem("sb_sp"), m + 1)
                n = SEQ - i * P
                ins = mm(bank[m % 2][:, 0:n], ntri, spb[:, m % 2, 0:n], False, i == 3, skip_group_check=True)
                if i < 3:
                    pe.wait_ge(sem("sb_run"), m)
                    ins = mm(bank[m % 2][:, P:n], nones, srun[:, (i + 1) * P:SEQ], False, True, skip_group_check=True)
                ins.then_inc(sem("sb_c"), 1)

            def sb_pv(hd, i):
                m = 4 * hd + 3 - i
                pe.wait_ge(sem("sb_am"), m + 1)
                if i == 3 and hd >= 2:
                    pe.wait_ge(sem("sb_out"), hd - 1)
                for j in range(i, NT):
                    ins = mm(bank[2 + hd % 2][:, j * DH:(j + 1) * DH], abuf[:, m % 2, (j - i) * P:(j - i + 1) * P],
                             z[:, i, O_VS + hd * DH:O_VS + (hd + 1) * DH], i == 3, i == 0, skip_group_check=True)
                ins.then_inc(sem("sb_pv"), 1)

            def n_unit(n):
                hd, br, i = n // 8, (n // 4) % 2, n % 4
                return hd, br, i, DH * (hd // G)

            def n_qk(n):
                hd, br, i, o = n_unit(n)
                if n >= 2:
                    pe.wait_ge(sem("n_exp"), n - 1)
                mm(bank[4 + n % 2][:, 0:(i + 1) * P], nqT[o:o + DH, hd % G, i * P:(i + 1) * P],
                        (ksT, kwT)[br][o:o + DH, 0:(i + 1) * P]).then_inc(sem("n_qk"), 1)

            def n_tr(n):
                hd, br, i, o = n_unit(n)
                pe.wait_ge(sem("n_exp"), n + 1)
                if n >= 2:
                    pe.wait_ge(sem("n_pT"), n - 1)
                for j in range(i + 1):
                    ins = tr(bank[6 + n % 2][:, j * P:(j + 1) * P], pbuf[:, n % 2, j * P:(j + 1) * P])
                ins.then_inc(sem("n_tr"), 1)

            def n_pv(n):
                hd, br, i, o = n_unit(n)
                pe.wait_ge(sem("n_pT"), n + 1)
                if n >= 2:
                    pe.wait_ge(sem("n_out"), n - 1)
                pe.wait_ge(sem("sb_a"), 4 * hd + 4)
                vo = (O_S, O_W)[br] + P + o
                for j in range(i + 1):
                    ins = mm(bank[n % 2][:, 0:DH], ptb[:, n % 2, j * P:(j + 1) * P], z[:, j, vo:vo + DH], j == 0, j == i)
                ins.then_inc(sem("n_pv"), 1)

            for hd in range(H):
                sb_qk(hd, 3); sb_qk(hd, 2); sb_sum(hd, 3); sb_qk(hd, 1); sb_sum(hd, 2); sb_pv(hd, 3)
                sb_qk(hd, 0); sb_sum(hd, 1); sb_pv(hd, 2); sb_sum(hd, 0); sb_pv(hd, 1); sb_pv(hd, 0)
                for s in range(10):
                    if s < 8:
                        n_qk(8 * hd + s)
                    if 1 <= s < 9:
                        n_tr(8 * hd + s - 1)
                    if s >= 2:
                        n_pv(8 * hd + s - 2)
            pe.wait_ge(sem("n_out"), 64)

            pe.wait_ge(*signal("att_done", 1))
            for b in range(B):
                ins = mm(bank[0][0:NC, b * H:(b + 1) * H], kc[:, b, 0:NC], qbd[:, b, :])
            ins.then_inc(sem("samples_pe"), 1)
            pe.wait_ge(*signal("c_s", 1))
            tr(bank[1][0:64, 0:NC], s64[0:NC, 0, 0:64]).then_inc(sem("samples_pe"), 1)
            pe.wait_ge(*signal("c_p", 1))
            tr(bank[2][0:NC, 0:64], s64[0:64, 2, 0:NC]).then_inc(sem("samples_pe"), 1)
            pe.wait_ge(*signal("c_pg", 1))
            mm(bank[3][0:16, 0:NSEL], s64[0:NC, 3, 0:16], K("overlap")[0:NC, :]).then_inc(sem("samples_pe"), 1)
            pe.wait_ge(*signal("c_sel", 1))
            tr(bank[4][0:NSEL, 0:16], s64[0:16, 5, 0:NSEL]).then_inc(sem("samples_pe"), 1)
            pe.wait_ge(*signal("c_selx", 1))
            mm(bank[5][:, 0:272], K("half")[0:NSEL, :], selx[0:NSEL].rearrange("p a b -> p (a b)")).then_inc(sem("samples_pe"), 1)
            for br in range(2):
                pe.wait_ge(*signal("m_max", br + 1))
                tr(bank[0][0:64, :][:, 0:P], s64[:, 0, 0:64]).then_inc(sem("samples_pe"), 1)
                pe.wait_ge(*signal("m_diag", br + 1))
                mm(bank[1][:, 0:64], ones[0:64, :], s64[0:64, 1, 0:64]).then_inc(sem("samples_pe"), 1)
                pe.wait_ge(*signal("m_sum", br + 1))
                mm(bank[2][:, 0:64], ones, s64[:, 3, 0:64]).then_inc(sem("samples_pe"), 1)
            pe.wait_ge(*signal("s_suf", 1))
            pe.wait_ge(*signal("m_rec", 2))
            for c in range(2):
                mm(bank[c][:, 0:512], ntri, sps[:, 4 * c:4 * c + 4].rearrange("p b n j -> p (b n j)"), True, False)
                ins = mm(bank[c][:, 0:512], nones, suf[:, 4 * c:4 * c + 4].rearrange("p b n j -> p (b n j)"), False, True)
            ins.then_inc(sem("samples_pe"), 1)
            pe.wait_ge(*signal("zero_set", 1))
            pe.wait_ge(*signal("c_selm", 1))
            for b in range(B):
                ins = mm(bank[5][:, b * H:(b + 1) * H], vc[0:NC, b, :], pcT[0:NC, b * H:(b + 1) * H])
            mm(bank[6][:, 0:64], zero, zero[:, 0:64], True, False, skip_group_check=True)
            mm(bank[7][:, 0:P], zero, zero, True, False, skip_group_check=True)
            pe.wait_ge(*signal("s_a", 1))
            osb = bank[6][:, 0:64].rearrange("p (t b two) -> p t b two", t=4, two=2)
            with pe.Fori(0, B) as b:
                for r in range(2):
                    for u in range(8):
                        pe.wait_ge(sem(f"ring_in{u}"), (2 * b + (r + 1 + 2 * B)) * 16)
                        for t in range(4):
                            ins = mm(osb[:, t, ds(b, 1), :].rearrange("p o j -> p (o j)"), ring[:, u, t * P:(t + 1) * P],
                                     sbs[:, ds(b, 1), r * 8 + u, 2 * t:2 * t + 2].rearrange("p o j -> p (o j)"),
                                     False, False, skip_group_check=True)
                        ins.then_inc(sem(f"ring_free{u}"), 1)
            pe.wait_ge(*signal("m_e", 2))
            with pe.Fori(0, B) as b:
                for q in range(5):
                    pe.wait_ge(sem(f"quad_in{q}"), (b + (1 + B)) * (64 if q < 4 else 16))
                    for j in range(4):
                        if q < 4:
                            out, w_ = bank[7][:, ds(b * H, H)], slc[:, ds(b, 1), 4 * q + j, :]
                        else:
                            out, w_ = bank[7][:, ds(b * H + 64, H)], wsc[:, ds(b, 1), j, :]
                        ins = mm(out, quad[:, q, j, :], w_.rearrange("p o j -> p (o j)"), False, False, skip_group_check=True)
                    ins.then_inc(sem(f"vq_mm{q}"), 1)
            pe.wait_ge(sem("rows_in"), 16 * 6)
            for br in range(2):
                for b in range(B):
                    w_ = slc[0:1, b, NPG, :] if br == 0 else wsc[0:1, b, NW, :]
                    mm(bank[7][:, 64 * br + b * H:64 * br + (b + 1) * H], vnew[0:1, br, b, :], w_, False,
                       br == 1 and b == B - 1, skip_group_check=True)
            pe.wait_ge(*signal("s_sp", 1))
            mm(bank[4][:, 0:B * 24], ones[0:1, :], grow[0:1].rearrange("p b h r -> p (b h r)")).then_inc(sem("samples_pe"), 1)
            pe.wait_ge(*signal("v_sq", 1))
            mm(bank[3][:, 0:64], ones, ofs[:, 9, :]).then_inc(sem("samples_pe"), 1)

            pe.wait_ge(sem("mix_ready"), 1)
            for k in range(KD):
                if k >= 2:
                    pe.wait_ge(sem("mixT_ev"), k - 1)
                for t in range(NT):
                    s = (o_sb, o_n)[k // 4][:, t, (k % 4) * P:(k % 4 + 1) * P]
                    ins = tr(bank[k % 2][:, t * P:(t + 1) * P], s)
                ins.then_inc(sem("mixT_mm"), 1)

            pe.wait_ge(sem("mixT_ev"), KD)
            pe.wait_ge(sem("mix_ready"), 2)
            pe.wait_ge(sem("wout_in"), 64)
            for t in range(T5):
                for c in range(2):
                    n = 2 * t + c
                    if n >= 4:
                        pe.wait_ge(sem("res_ev"), n - 3)
                    for k in range(KD):
                        ins = mm(bank[4 + n % 4][0:rows[t], :], hT[:, k, t * P:t * P + rows[t]],
                                 wout[:, k, c * 512:(c + 1) * 512], k == 0, k == KD - 1)
                    ins.then_inc(sem("out_mm"), 1)
            norm_transposes(h2, 1)
            pe.wait_ge(sem("hT_ev"), 18)
            pe.wait_ge(sem("res_ev"), 10)
            with pe.Fori(0, FT // 2) as i:
                for u in range(2):
                    pe.wait_ge(sem(f"up_in{u}"), i * 16 + 16)
                    pe.wait_ge(sem(f"up_ev{u}"), i + 1)
                    for k in range(KD):
                        mm(bank[4 + u][:, :], upw[u][:, k, :], hT[:, k, 0:SEQ], k == 0, k == KD - 1)
                        ins = mm(bank[6 + u][:, 0:B], upw[u][:, k, :], hT[:, k, SEQ:TOK], k == 0, k == KD - 1)
                    ins.then_inc(sem(f"up_free{u}"), 1)
            for u in range(2):
                pe.wait_ge(sem(f"a_ready{u}"), FT // 2 + 1)
            with pe.Fori(0, KD // 2) as i:
                for u in range(2):
                    pe.wait_ge(sem(f"dn_in{u}"), i * 16 + 16)
                    pe.wait_ge(sem(f"dn_ev{u}"), i + 1)
                    for k in range(FT):
                        mm(bank[u][:, :], dnw[u][:, k, :], aT[:, k, 0:SEQ], k == 0, k == FT - 1)
                        ins = mm(bank[2 + u][:, 0:B], dnw[u][:, k, :], aT[:, k, SEQ:TOK], k == 0, k == FT - 1)
                    ins.then_inc(sem(f"dn_free{u}"), 1)
                    pe.wait_ge(sem(f"dn_ev{u}"), i + 1 + 1)
                    pe.wait_ge(sem(f"y_ev{u}"), i + 1)
                    for t in range(NT):
                        tr(bank[4 + u][:, t * P:(t + 1) * P], yT[u][:, t * P:(t + 1) * P])
                    tr(bank[6 + u][0:B, 0:P], yT[u][:, SEQ:TOK]).then_inc(sem(f"y_mm{u}"), 1)

        @block.scalar
        def _(act):
            S = nc.scalar
            prime(act, "act")
            chain = Chain(act, sem("act_steps"))

            eps = K("eps")
            act.wait_ge(sem("const_in"), 16)
            act.wait_ge(sem("ss"), 1)
            S.activation(st[:, 8:13], st[:, 0:5], ACT.Sqrt, bias=eps, scale=1.0 / D).then_inc(sem("rt"), 1)
            wb, wo = A["state_nsa_win_kv"][0], O["win_s"][0]
            for b in range(B):
                act.dma_start(wo[b, 0:WIN - 1].rearrange("(o s) k h d -> o (s k h d)", o=1),
                    wb[b, 1:WIN].rearrange("(o s) k h d -> o (s k h d)", o=1)).then_inc(sem("kv_out"), 16)
            with act.Fori(0, 4) as i:
                for u in range(2):
                    for t in (1, 3):
                        act.wait_ge(sem("z_mm"), i * (2 * T5) + u * T5 + t + 1)
                        S.activation(z[:, t, ds(i * (2 * CB) + u * CB, CB)], bank[t][:, 0:CB], ACT.Copy).then_inc(sem(f"z_ev{t}"), 1)
            for t in range(T5):
                act.wait_ge(sem(f"z_ev{t}"), 8 + 1)
            act.dma_start(O["sb_p"][0, 0].rearrange("(t p) k h d -> p t (k h d)", p=P), z[:, 0:NT, O_KS:O_KS + 1024]).then_inc(sem("sb_stored"), 16)
            act.dma_start(O["sb_s"][0].rearrange("b o k h d -> (b o) (k h d)"), z[0:B, NT, O_KS:O_KS + 1024]).then_inc(sem("kv_out"), 16)
            act.wait_ge(sem("rope_done"), T5)
            act.dma_start(O["cmp_p"][0, 0].rearrange("(t p) k h d -> p t (k h d)", p=P), z[:, 0:NT, O_C:O_C + 256]).then_inc(sem("cmp_stored"), 16)
            for nm, o in (("slc_p", O_S), ("win_p", O_W)):
                act.dma_start(O[nm][0, 0].rearrange("(t p) k h d -> p t (k h d)", p=P), z[:, 0:NT, o:o + 256]).then_inc(sem("kv_out"), 16)
            for nm, o in (("cmp_s", O_C), ("slc_s", O_S)):
                act.dma_start(O[nm][0].rearrange("b o k h d -> (b o) (k h d)"), z[0:B, NT, o:o + 256]).then_inc(sem("kv_out"), 16)
            act.dma_start(wo[:, WIN - 1].rearrange("b k h d -> b (k h d)"), z[0:B, NT, O_W:O_W + 256]).then_inc(sem("kv_out"), 16)
            act.wait_ge(sem("qscaled"), 1)
            act.dma_start(sbq_dram, qsc[0:B, :]).then_inc(sem("sbq_out"), 16)
            dst = [sbqT[:, j] for j in range(4)] + [sbkT[:, j] for j in range(4)] + [nqT[:, j] for j in range(4)] + [ksT, kwT]
            for j in range(1, 14, 2):
                act.wait_ge(sem("qkT_mm"), j + 1)
                q = j < 4 or 8 <= j < 12
                S.activation(dst[j], bank[j % 4][:, :], ACT.Copy, scale=SCALE if q else 1.0).then_inc(sem("qkT_ev1"), 1)
            S.activation(z[:, :, O_G:O_G + 24], z[:, :, O_G:O_G + 24], ACT.Exp, scale=-1.0).then_inc(sem("gates_e"), 1)
            act.wait_ge(sem("snew"), 2)
            for br in range(2):
                act.dma_start(newrow[0:1, br].rearrange("p b h -> p (b h)"), snew[0:B, br, :]).then_inc(sem("rows_in"), 16)
            for br, o in enumerate((O_S, O_W)):
                act.dma_start(vnew[0:1, br].rearrange("p b c -> p (b c)"), z[0:B, NT, o + P:o + 2 * P]).then_inc(sem("rows_in"), 16)
            act.wait_ge(sem("gates"), 1)
            act.dma_start(grow[0:1].rearrange("p b h r -> p (b h r)"), z[0:B, NT, O_G:O_G + 24]).then_inc(sem("rows_in"), 16)
            act.dma_start(st[0:1, 208:209], A["g_final"].rearrange("(o d) -> o d", o=1)[:, 0:1]).then_inc(sem("rows_in"), 16)

            act.wait_ge(sem("pebias"), 2)

            def compress(c, n):
                nb = n - 1
                for kv in range(2):
                    for s in (0, 2):
                        act.wait_ge(sem("xT_mm"), c * 8 + kv * 4 + s + 1)
                        ins = S.activation(xT[kv][:, 2 * s:2 * s + 2, :, 0:n],
                                           bank[0].rearrange("p (m h c) -> p m h c", m=2, h=2)[:, :, :, 0:n], ACT.Copy)
                        ins.then_inc(sem("xT_ev0"), 1)
                    act.wait_ge(sem(f"hid_mm{kv}"), c + 1)
                    act.wait_ge(sem(f"hid_ready{kv}"), c + 1)
                    S.activation(hid[kv][:, :, 0:nb], bank[2 + kv][:, 0:KVH * nb].rearrange("p (h c) -> p h c", h=KVH),
                                      ACT.Exp, bias=pebias[:, 2 + kv:3 + kv], scale=-1.0).then_inc(sem(f"hid_e{kv}"), 1)

            with act.Fori(0, B) as c:
                compress(c, NCH)
            compress(B, NCP + 1)

            act.wait_ge(sem("kvc_ev0"), B + 1 + 1)
            act.wait_ge(sem("kvc_ev1"), B + 1 + 1)
            with act.Fori(0, B) as b:
                for q in range(5):
                    act.wait_ge(sem(f"kq_mm{q}"), b + 1 + 1)
                    if q == 0:
                        act.wait_ge(sem("qs_mm"), b + 1)
                    S.activation(kqT[:, q].rearrange("p j s -> p (j s)"), bank[q][:, :], ACT.Copy).then_inc(sem("kq_ev"), 1)
                act.wait_ge(sem("qs_mm"), b + 1 + 1)
                S.activation(slc[:, ds(b, 1), 0:NPG, :].rearrange("p o n j -> p (o n j)"), bank[5][:, 0:NPG * H], ACT.Copy)
                S.activation(wsc[:, ds(b, 1), 0:NW, :].rearrange("p o n j -> p (o n j)"), bank[5][:, NPG * H:(NPG + NW) * H], ACT.Copy).then_inc(sem("qs_ev"), 1)

            for i in range(NT):
                act.wait_ge(sem("cp_max"), i + 1)
                S.activation(pbuf[:, 0, 0:H * NCP], pbuf[:, 0, 0:H * NCP], ACT.Exp).then_inc(sem("cp_exp"), 1)
                for c in range(2):
                    act.wait_ge(sem("cp_tr"), 2 * i + c + 1)
                    if c == 0 and i:
                        act.wait_ge(sem("cp_pv"), i)
                    S.activation(ptb[0:NCP, c, :], bank[6 + c][0:NCP, :], ACT.Copy).then_inc(sem("cp_pT"), 1)

            def sb_ln(hd, i):
                m, n = 4 * hd + 3 - i, SEQ - i * P
                act.wait_ge(sem("sb_qk"), m + 1)
                if m >= 2:
                    act.wait_ge(sem("sb_sp"), m - 1)
                e = ebuf[:, m % 2, 0:n]
                chain(S.activation(e, bank[m % 2][:, 0:n], ACT.Abs))
                chain(S.activation(e, e, ACT.Exp, scale=-1.0))
                S.activation(e, e, ACT.Ln, bias=K("one")).then_inc(sem("sb_ln"), 1)

            def sb_exp(hd, i):
                m, n = 4 * hd + 3 - i, SEQ - i * P
                act.wait_ge(sem("sb_c"), m + 1)
                if m >= 2:
                    act.wait_ge(sem("sb_pv"), m - 1)
                S.activation(abuf[:, m % 2, 0:n], bank[m % 2][:, 0:n], ACT.Exp).then_inc(sem("sb_a"), 1)

            def n_exp(n):
                i = n % 4
                act.wait_ge(sem("n_max"), n + 1)
                if n >= 2:
                    act.wait_ge(sem("n_tr"), n - 1)
                    act.wait_ge(sem("n_out"), n - 1)
                S.activation(pbuf[:, n % 2, 0:(i + 1) * P], bank[4 + n % 2][:, 0:(i + 1) * P], ACT.Exp,
                                  bias=st[:, 32 + n % 2:33 + n % 2], accum_out=st[:, 34 + n % 2:35 + n % 2]).then_inc(sem("n_exp"), 1)

            def n_pT(n):
                i = n % 4
                act.wait_ge(sem("n_tr"), n + 1)
                if n >= 2:
                    act.wait_ge(sem("n_pv"), n - 1)
                S.activation(ptb[:, n % 2, 0:(i + 1) * P], bank[6 + n % 2][:, 0:(i + 1) * P], ACT.Copy).then_inc(sem("n_pT"), 1)

            act.wait_ge(sem("cp_pv"), NT)
            for hd in range(H):
                sb_ln(hd, 3); sb_ln(hd, 2); sb_exp(hd, 3); sb_ln(hd, 1); sb_exp(hd, 2); sb_ln(hd, 0)
                sb_exp(hd, 1); sb_exp(hd, 0)
                act.wait_ge(sem("sb_pv"), 4 * hd + 4)
                S.activation(o_sb[:, :, hd * DH:(hd + 1) * DH], bank[2 + hd % 2][:, 0:256].rearrange("p (t d) -> p t d", t=NT), ACT.Copy).then_inc(sem("sb_out"), 1)
                for s in range(9):
                    if s < 8:
                        n_exp(8 * hd + s)
                    if s >= 1:
                        n_pT(8 * hd + s - 1)

            act.wait_ge(*signal("c_nm", 1))
            S.activation(s64[0:64, 1, 0:NC], bank[1][0:64, 0:NC], ACT.Exp, bias=st[0:64, 40:41], accum_out=st[0:64, 41:42]).then_inc(sem("samples_act"), 1)
            for br, (sc, n) in enumerate(((slc, NPG + 1), (wsc, NW + 1))):
                act.wait_ge(*signal("m_sub", br + 1))
                f = sc.rearrange("p b n j -> p (b n j)")
                S.activation(f, f, ACT.Exp).then_inc(sem("samples_act"), 1)
            act.wait_ge(*signal("s_abs", 1))
            f = sps.rearrange("p b n j -> p (b n j)")
            chain(S.activation(f, f, ACT.Exp, scale=-1.0))
            S.activation(f, f, ACT.Ln, bias=K("one")).then_inc(sem("samples_act"), 1)
            act.wait_ge(*signal("s_d", 1))
            f = sbs.rearrange("p b n j -> p (b n j)")
            S.activation(f, f, ACT.Exp).then_inc(sem("samples_act"), 1)
            act.wait_ge(*signal("v_st", 1))
            S.activation(st[:, 64:80], st[:, 48:64], ACT.Sqrt, bias=eps, scale=1.0 / 512).then_inc(sem("samples_act"), 1)
            act.wait_ge(*signal("mix_ss", 1))
            S.activation(st[:, 96:104], st[:, 88:96], ACT.Sqrt, bias=eps, scale=1.0 / 512).then_inc(sem("samples_act"), 1)
            act.wait_ge(sem("ss"), 2)
            S.activation(st[:, 8:13], st[:, 0:5], ACT.Sqrt, bias=eps, scale=1.0 / D).then_inc(sem("rt"), 1)
            act.wait_ge(sem("hT_ev"), 18)
            with act.Fori(0, FT // 2) as i:
                for u in range(2):
                    act.wait_ge(sem(f"up_free{u}"), i + 1 + 1)
                    act.wait_ge(sem(f"a_ready{u}"), i + 1)
                    S.activation(h2[:, u, 0:SEQ], bank[4 + u][:, :], ACT.Relu)
                    S.activation(h2[:, u, SEQ:TOK], bank[6 + u][:, 0:B], ACT.Relu).then_inc(sem(f"up_ev{u}"), 1)
            act.wait_ge(sem("ss"), 3)
            S.activation(st[:, 8:13], st[:, 0:5], ACT.Sqrt, bias=eps, scale=1.0 / D).then_inc(sem("rt"), 1)
            act.wait_ge(sem("kv_out"), 16 * (B + 6))
            act.wait_ge(sem("cmp_stored"), 16)
            act.wait_ge(sem("sbq_out"), 16)

        @block.vector
        def _(dve):
            V = nc.vector
            prime(dve, "dve")
            chain = Chain(dve, sem("dve_steps"))

            def row_scales(dst, turn):
                for t in range(T5):
                    ins = V.tensor_tensor_reduce(dst[0:rows[t], t, :], x[0:rows[t], t, :], x[0:rows[t], t, :], 1.0, 0.0,
                                                 ALU.mult, ALU.add, st[0:rows[t], t:t + 1])
                    if t < NT:
                        chain(ins)
                ins.then_inc(sem("ss"), 1)
                dve.wait_ge(sem("rt"), turn + 1)
                chain(V.reciprocal(st[:, 16:21], st[:, 8:13]))
                for t in range(T5):
                    ins = V.tensor_scalar(dst[0:rows[t], t, :], x[0:rows[t], t, :], st[0:rows[t], 16 + t:17 + t], None, ALU.mult)
                    if t < T5 - 1:
                        chain(ins)
                return ins

            def gained(g0, turn):
                for k in range(KD):
                    dve.wait_ge(sem("hT_mm"), 9 * turn + k + 1)
                    V.tensor_scalar(hT[:, k, 0:SEQ], bank[k % 2][:, :], vcol[:, g0 + k:g0 + k + 1], None, ALU.mult).then_inc(sem("hT_ev"), 1)
                dve.wait_ge(sem("hT_mm"), 9 * turn + 9)
                V.tensor_tensor(hT[:, :, SEQ:TOK], bank[2][:, 0:64].rearrange("p (k b) -> p k b", k=KD),
                                     over(vcol[:, g0:g0 + KD], 2, B), ALU.mult).then_inc(sem("hT_ev"), 1)

            chain(V.memset(st[:, :], 1.0))
            chain(V.memset(zero[:, :], 0.0))
            dve.wait_ge(sem("x_in"), 32)
            row_scales(h, 0).then_inc(sem("h_ready"), 1)
            dve.wait_ge(sem("vcol_mm"), 1)
            V.tensor_copy(vcol[:, :], bank[3][:, 0:56]).then_inc(sem("vcol_ev"), 1)
            dve.wait_ge(sem("vcol_ev"), 1)
            gained(0, 0)
            dve.wait_ge(sem("z_zero"), 1)
            with dve.Fori(0, 4) as i:
                for u in range(2):
                    for t in (0, 2, 4):
                        dve.wait_ge(sem("z_mm"), i * (2 * T5) + u * T5 + t + 1)
                        V.tensor_copy(z[0:rows[t], t, ds(i * (2 * CB) + u * CB, CB)], bank[t][0:rows[t], 0:CB]).then_inc(sem(f"z_ev{t}"), 1)
                    dve.wait_ge(sem(f"z_ev4"), i * 2 + u + 1 + 1)
                    V.memset(st[0:1, 202:203], 0.0).then_inc(sem(f"win_free{u}"), 1)
            for t in range(T5):
                dve.wait_ge(sem(f"z_ev{t}"), 8 + 1)
            chain(V.memset(qbd[:, :, :], 0.0))
            for t in range(T5):
                cos, sin = (K(n)[:, t * DH:(t + 1) * DH] for n in ("cos", "sin"))
                qn = z[:, t, O_QN:O_QN + 512].rearrange("p (h d) -> p h d", h=H)
                kk = z[:, t, O_C:O_C + 768].rearrange("p (r k h d) -> p r k h d", r=3, k=2, h=2)[:, :, 0]
                a8, b8 = (v.rearrange("p (h d) -> p h d", h=H) for v in (ropeA, ropeB))
                a6, b6 = (v[:, 0:384].rearrange("p (r h d) -> p r h d", r=3, h=2) for v in (ropeA, ropeB))
                chain(V.tensor_tensor(a8, qn, over(cos, 1, H), ALU.mult))
                chain(V.tensor_tensor(b8[:, :, 0:32], qn[:, :, 32:64], over(sin[:, 0:32], 1, H), ALU.mult))
                chain(V.tensor_tensor(b8[:, :, 32:64], qn[:, :, 0:32], over(sin[:, 32:64], 1, H), ALU.mult))
                qp = z[:, t, O_QN:O_QN + 512].rearrange("p (g k d) -> p k g d", g=G, k=KVH)
                chain(V.tensor_tensor(qp, *(v.rearrange("p (k g) d -> p k g d", k=KVH) for v in (a8, b8)), ALU.add))
                cos6, sin6 = over(over(cos, 1, 2), 1, 3), over(over(sin, 1, 2), 1, 3)
                chain(V.tensor_tensor(a6, kk, cos6, ALU.mult))
                chain(V.tensor_tensor(b6[:, :, :, 0:32], kk[:, :, :, 32:64], sin6[:, :, :, 0:32], ALU.mult))
                chain(V.tensor_tensor(b6[:, :, :, 32:64], kk[:, :, :, 0:32], sin6[:, :, :, 32:64], ALU.mult))
                V.tensor_tensor(kk, a6, b6, ALU.add).then_inc(sem("rope_done"), 1)
                dve.wait_ge(sem("rope_done"), t + 1)
            dve.wait_ge(sem("rope_done"), T5)
            zs = z[0:B, NT]
            chain(V.tensor_scalar(qsc[0:B, :], zs[:, O_QS:O_QS + 512], SCALE, None, ALU.mult))
            V.memset(st[0:1, 204:205], 0.0).then_inc(sem("qscaled"), 1)
            for j in range(0, 14, 2):
                dve.wait_ge(sem("qkT_mm"), j + 1)
                q = j < 4 or 8 <= j < 12
                dst = ([sbqT[:, n] for n in range(4)] + [sbkT[:, n] for n in range(4)] + [nqT[:, n] for n in range(4)] + [ksT, kwT])[j]
                if q:
                    ins = V.tensor_scalar(dst, bank[j % 4][:, :], SCALE, None, ALU.mult)
                else:
                    ins = V.tensor_copy(dst, bank[j % 4][:, :])
                ins.then_inc(sem("qkT_ev0"), 1)
            dve.wait_ge(sem("qkT_mm"), 15)
            for kh in range(2):
                lo = kh * DH
                ins = V.tensor_scalar(qbd[lo:lo + DH, :, kh * G:(kh + 1) * G],
                                      bank[4][lo:lo + DH, 0:32].rearrange("p (g b) -> p b g", g=G), SCALE, None, ALU.mult)
                if kh == 0:
                    chain(ins)
            ins.then_inc(sem("qkT_ev0"), 1)
            for br, o in enumerate((O_S, O_W)):
                qn = zs[:, O_QN:O_QN + 512].rearrange("p (g k d) -> p k g d", k=2, g=G)
                kn = over(zs[:, o:o + P].rearrange("p (k d) -> p k d", k=2), 2, G)
                chain(V.tensor_tensor(ropeA[0:B].rearrange("p (k g d) -> p k g d", k=2, g=G), qn, kn, ALU.mult))
                chain(V.tensor_reduce(ropeB[0:B, 0:H], ropeA[0:B].rearrange("p (h d) -> p h d", h=H), AX.X, ALU.add))
                V.tensor_scalar(snew[0:B, br, :], ropeB[0:B, 0:H], SCALE, None, ALU.mult).then_inc(sem("snew"), 1)
                dve.wait_ge(sem("snew"), br + 1)
            dve.wait_ge(sem("gates_e"), 1)
            g = z[:, :, O_G:O_G + 24]
            chain(V.tensor_scalar(g, g, 1.0, None, ALU.add))
            V.reciprocal(g, g).then_inc(sem("gates"), 1)
            dve.wait_ge(sem("pe_mm"), 1)
            V.tensor_copy(pebias[:, 0:2], bank[6][:, 0:2]).then_inc(sem("pebias"), 1)
            V.tensor_scalar(pebias[:, 2:4], bank[6][:, 0:2], -1.0, None, ALU.mult).then_inc(sem("pebias"), 1)
            dve.wait_ge(sem("pebias"), 2)
            dve.wait_ge(sem("gates"), 1)

            def compress(c, dst_k, dst_v, n):
                nb = n - 1
                for kv in range(2):
                    for s in (1, 3):
                        dve.wait_ge(sem("xT_mm"), c * 8 + kv * 4 + s + 1)
                        ins = V.tensor_copy(xT[kv][:, 2 * s:2 * s + 2, :, 0:n],
                                            bank[1].rearrange("p (m h c) -> p m h c", m=2, h=2)[:, :, :, 0:n])
                        ins.then_inc(sem("xT_ev1"), 1)
                for kv in range(2):
                    dve.wait_ge(sem(f"hid_e{kv}"), c + 1)
                    e = hid[kv][:, :, 0:nb]
                    chain(V.tensor_scalar(e, e, 1.0, None, ALU.add))
                    chain(V.reciprocal(e, e))
                    if kv == 0:
                        dve.wait_ge(sem("w2_mm0"), c + 1)
                    else:
                        dve.wait_ge(sem("w2_mm1"), c + 1)
                    hp = bank[2 + kv][:, 0:KVH * nb].rearrange("p (h c) -> p h c", h=KVH)
                    V.scalar_tensor_tensor(out=hid[2 + kv][:, :, 0:nb], in0=hp, scalar=pebias[:, kv:kv + 1], in1=e,
                                                op0=ALU.add, op1=ALU.mult).then_inc(sem(f"hid_ready{kv}"), 1)
                    dve.wait_ge(sem(f"hid_ready{kv}"), c + 1 + 1)
                    V.memset(st[0:1, 206:207], 0.0).then_inc(sem(f"hid_ev{kv}"), 1)
                dve.wait_ge(sem("w2_mm0"), c + 1 + 1)
                V.tensor_copy(dst_k, bank[4][:, 0:nb]).then_inc(sem("kvc_ev0"), 1)
                dve.wait_ge(sem("w2_mm1"), c + 1 + 1)
                V.tensor_copy(dst_v, bank[5][0:nb, 0:P]).then_inc(sem("kvc_ev1"), 1)

            with Turns(chain, 4, 8) as i:
                for u in range(2):
                    c = i * 2 + u
                    compress(c, kc[:, ds(c, 1), 0:NC].rearrange("p o c -> p (o c)"), vc[0:NC, ds(c, 1), :].rearrange("p o c -> p (o c)"), NCH)
            compress(B, kc[:, B, 0:NCP], vc[0:NCP, B, :], NCP + 1)

            dve.wait_ge(sem("kvc_ev0"), B + 1 + 1)
            dve.wait_ge(sem("kvc_ev1"), B + 1 + 1)
            dve.wait_ge(sem("qs_ev"), B + 1)
            pc = pbuf[:, 0, 0:H * NCP].rearrange("p (h c) -> p h c", h=H)
            for i in range(NT):
                dve.wait_ge(sem("cp_qk"), i + 1)
                if i:
                    dve.wait_ge(sem("cp_tr"), 2 * i)
                add, mul = (over(K(nm)[:, i * NCP:(i + 1) * NCP], 1, H) for nm in ("cadd", "cmul"))
                for kh in range(KVH):
                    hs = slice(G * kh, G * kh + G)
                    chain(V.tensor_tensor(pc[:, hs], bank[4 + kh][:, 0:G * NCP].rearrange("p (h c) -> p h c", h=G), add[:, hs], ALU.add))
                chain(V.tensor_reduce(st[:, 104:112], pc, AX.X, ALU.max))
                V.tensor_tensor(pc, pc, over(st[:, 104:112], 2, NCP), ALU.subtract).then_inc(sem("cp_max"), 1)
                dve.wait_ge(sem("cp_exp"), i + 1)
                chain(V.tensor_tensor(pc, pc, mul, ALU.mult))
                chain(V.tensor_reduce(st[:, 112:120], pc, AX.X, ALU.add))
                chain(V.tensor_scalar(st[:, 112:120], st[:, 112:120], TINY, None, ALU.max))
                chain(V.reciprocal(st[:, 120:128], st[:, 112:120]))
                gate = z[:, i, O_G:O_G + 24].rearrange("p (h r) -> p h r", r=3)[:, :, 0]
                chain(V.tensor_tensor(st[:, 120:128], st[:, 120:128], gate, ALU.mult))
                V.tensor_tensor(pc, pc, over(st[:, 120:128], 2, NCP), ALU.mult).then_inc(sem("cp_soft"), 1)
                dve.wait_ge(sem("cp_pv"), i + 1)
                V.tensor_copy(o_n[:, i, :], bank[i % 2][:, :]).then_inc(sem("cp_out"), 1)
            dve.wait_ge(sem("cp_out"), NT)
            dve.wait_ge(sem("cp_tr"), 2 * NT)

            def sb_keys(b):
                dve.wait_ge(sem(f"qb_in{b % 2}"), 16 * (b // 2 + 1))
                with Turns(chain, 2, 8) as r:
                    for u in range(8):
                        dve.wait_ge(sem(f"ring_in{u}"), 16 * (2 * b + 1) + r * 16)
                        chain(V.tensor_tensor(prod[:, u % 2, :], ring[:, u, :], qb[:, b % 2, :], ALU.mult))
                        V.tensor_reduce(sbs[:, b, ds(r * 8 + u, 1), :].rearrange("p o j -> p (o j)"),
                                        prod[:, u % 2, :].rearrange("p (h d) -> p h d", h=H), AX.X, ALU.add).then_inc(sem("k_red"), 1)
                        dve.wait_ge(sem("k_red"), NPG * b + 1 + u + r * 8)
                        V.memset(st[0:1, 209:210], 0.0).then_inc(sem(f"ring_free{u}"), 1)

            def sb_soft(hd, i):
                m, n = 4 * hd + 3 - i, SEQ - i * P
                dve.wait_ge(sem("sb_ln"), m + 1)
                if m >= 2:
                    dve.wait_ge(sem("sb_c"), m - 1)
                    dve.wait_ge(sem("sb_run"), m - 1)
                s = spb[:, m % 2]
                chain(V.scalar_tensor_tensor(out=s[:, 0:n], in0=bank[m % 2][:, 0:n], scalar=0.0, in1=ebuf[:, m % 2, 0:n],
                                             op0=ALU.max, op1=ALU.add))
                V.tensor_tensor(s[:, 0:P], s[:, 0:P], K("before"), ALU.mult).then_inc(sem("sb_sp"), 1)

            def sb_amask(hd, i):
                m = 4 * hd + 3 - i
                dve.wait_ge(sem("sb_a"), m + 1)
                V.tensor_tensor(abuf[:, m % 2, 0:P], abuf[:, m % 2, 0:P], K("before"), ALU.mult).then_inc(sem("sb_am"), 1)

            def n_max(n):
                i = n % 4
                dve.wait_ge(sem("n_qk"), n + 1)
                if n >= 2:
                    dve.wait_ge(sem("n_exp"), n - 1)
                pb = bank[4 + n % 2]
                chain(V.tensor_tensor(pb[:, i * P:(i + 1) * P], pb[:, i * P:(i + 1) * P], K("causal"), ALU.add))
                V.tensor_reduce(st[:, 32 + n % 2:33 + n % 2], pb[:, 0:(i + 1) * P], AX.X, ALU.max, negate=True).then_inc(sem("n_max"), 1)

            def n_out(n):
                hd, br, i = n // 8, (n // 4) % 2, n % 4
                dve.wait_ge(sem("n_pv"), n + 1)
                c = 36 + n % 2
                chain(V.reciprocal(st[:, c:c + 1], st[:, c - 2:c - 1]))
                gate = z[:, i, O_G + 3 * hd + 1 + br:O_G + 3 * hd + 2 + br]
                chain(V.tensor_tensor(st[:, c:c + 1], st[:, c:c + 1], gate, ALU.mult))
                o = o_n[:, i, place(hd) * DH:(place(hd) + 1) * DH]
                V.scalar_tensor_tensor(out=o, in0=bank[n % 2][:, 0:DH], scalar=st[:, c:c + 1], in1=o, op0=ALU.mult, op1=ALU.add).then_inc(sem("n_out"), 1)
                dve.wait_ge(sem("n_out"), n + 1)

            for hd in range(H):
                sb_keys(hd)
                sb_soft(hd, 3); sb_soft(hd, 2); sb_amask(hd, 3); sb_soft(hd, 1); sb_amask(hd, 2)
                sb_soft(hd, 0); sb_amask(hd, 1); sb_amask(hd, 0)
                for s in range(9):
                    if s < 8:
                        n_max(8 * hd + s)
                    if s >= 1:
                        n_out(8 * hd + s - 1)

            dve.wait_ge(sem("sb_out"), H)
            dve.wait_ge(sem("sb_run"), 4 * H)
            dve.wait_ge(sem("sb_pv"), 4 * H)
            dve.wait_ge(sem("n_pv"), 64)
            V.memset(st[0:1, 210:211], 0.0).then_inc(sem("samples_dve"), 1)
            V.memset(st[0:1, 211:212], 0.0).then_inc(sem("samples_dve"), 1)
            dve.wait_ge(*signal("c_sc", 1))
            V.tensor_copy(s64[0:NC, 0, 0:64], bank[0][0:NC, 0:64]).then_inc(sem("samples_dve"), 1)
            dve.wait_ge(*signal("c_scT", 1))
            V.tensor_reduce(st[0:64, 40:41], bank[1][0:64, 0:NC], AX.X, ALU.max, negate=True).then_inc(sem("samples_dve"), 1)
            dve.wait_ge(*signal("c_e", 1))
            chain(V.tensor_scalar(st[0:64, 41:42], st[0:64, 41:42], TINY, None, ALU.max))
            chain(V.reciprocal(st[0:64, 42:43], st[0:64, 41:42]))
            V.tensor_scalar(s64[0:64, 2, 0:NC], s64[0:64, 1, 0:NC], st[0:64, 42:43], None, ALU.mult).then_inc(sem("samples_dve"), 1)
            dve.wait_ge(*signal("c_pT", 1))
            chain(V.tensor_copy(pcT[0:NC, :], bank[2][0:NC, 0:64]))
            V.tensor_reduce(s64[0:NC, 3, 0:16], pcT[0:NC, :].rearrange("p (k g) -> p k g", g=G), AX.X, ALU.add).then_inc(sem("samples_dve"), 1)
            dve.wait_ge(*signal("c_imp", 1))
            imp = s64[0:16, 4, 0:NSEL]
            chain(V.tensor_copy(imp, bank[3][0:16, 0:NSEL]))
            chain(V.memset(imp[:, 0:1], FORCE))
            chain(V.memset(imp[:, NSEL - 2:NSEL], FORCE))
            im_i, im_j = over(imp, 1, NSEL), over(imp, 2, NSEL)
            chain(V.tensor_tensor(rankA[0:16], im_i, im_j, ALU.is_gt))
            chain(V.tensor_tensor(rankB[0:16], im_i, im_j, ALU.is_equal))
            chain(V.tensor_tensor(rankB[0:16], rankB[0:16], K("lower")[0:16].rearrange("p (j i) -> p j i", j=NSEL), ALU.mult))
            chain(V.tensor_tensor(rankA[0:16], rankA[0:16], rankB[0:16], ALU.add))
            chain(V.tensor_reduce(s64[0:16, 6, 0:NSEL], rankA[0:16], AX.X, ALU.add))
            V.tensor_scalar(s64[0:16, 5, 0:NSEL], s64[0:16, 6, 0:NSEL], float(TOPN), None, ALU.is_lt).then_inc(sem("samples_dve"), 1)
            dve.wait_ge(*signal("c_selT", 1))
            V.tensor_tensor(selx[0:NSEL], over(bank[4][0:NSEL, 0:16], 1, NPG + 1),
                                 K("pagemap")[0:NSEL].rearrange("p (n k) -> p n k", k=16), ALU.mult).then_inc(sem("samples_dve"), 1)
            dve.wait_ge(*signal("c_mask", 1))
            V.tensor_scalar(selm.rearrange("p n k -> p (n k)"), bank[5][:, 0:272], -1.0, -NEG, ALU.add, ALU.mult).then_inc(sem("samples_dve"), 1)
            dve.wait_ge(*signal("c_selm", 1))
            dve.wait_ge(sem("rows_in"), 96)
            chain(V.memset(slc[:, :, NPG, :], NEG))
            chain(V.memset(wsc[:, :, NW, :], NEG))
            chain(V.tensor_copy(slc[0:1, :, NPG, :], newrow[0:1, 0]))
            chain(V.tensor_copy(wsc[0:1, :, NW, :], newrow[0:1, 1]))
            chain(V.memset(wsc[0:1, :, 0, :], NEG))
            for b in range(B):
                v = slc[:, b].rearrange("p n (k g) -> p n k g", k=2)
                chain(V.tensor_tensor(v, v, over(selm[:, :, 2 * b:2 * b + 2], 3, G), ALU.add))
            for br, (sc, n) in enumerate(((slc, NPG + 1), (wsc, NW + 1))):
                V.tensor_reduce(s64[:, 0, 0:64].rearrange("p (b j) -> p b j", b=B), sc.rearrange("p b n j -> p b j n"), AX.X, ALU.max).then_inc(sem("samples_dve"), 1)
                dve.wait_ge(*signal("m_T", br + 1))
                chain(V.tensor_reduce(st[0:64, 44:45], bank[0][0:64, 0:P], AX.X, ALU.max))
                V.tensor_scalar(s64[0:64, 1, 0:64], ident[0:64, 0:64], st[0:64, 44:45], None, ALU.mult).then_inc(sem("samples_dve"), 1)
                dve.wait_ge(*signal("m_b", br + 1))
                chain(V.tensor_copy(s64[:, 2, 0:64], bank[1][:, 0:64]))
                V.tensor_tensor(sc, sc, over(s64[:, 2, 0:64].rearrange("p (b j) -> p b j", b=B), 2, n), ALU.subtract).then_inc(sem("samples_dve"), 1)
                dve.wait_ge(*signal("m_e", br + 1))
                V.tensor_reduce(s64[:, 3, 0:64].rearrange("p (b j) -> p b j", b=B), sc.rearrange("p b n j -> p b j n"), AX.X, ALU.add).then_inc(sem("samples_dve"), 1)
                dve.wait_ge(*signal("m_den", br + 1))
                V.reciprocal(s64[:, 7 + br, 0:64], bank[2][:, 0:64]).then_inc(sem("samples_dve"), 1)
                dve.wait_ge(*signal("m_rec", br + 1))
            flat = lambda a: a.rearrange("p b n j -> p (b n j)")
            V.scalar_tensor_tensor(out=flat(sps), in0=flat(sbs), scalar=-1.0, in1=flat(sbs), op0=ALU.mult, op1=ALU.max).then_inc(sem("samples_dve"), 1)
            dve.wait_ge(*signal("s_ln", 1))
            V.scalar_tensor_tensor(out=flat(sps), in0=flat(sbs), scalar=0.0, in1=flat(sps), op0=ALU.max, op1=ALU.add).then_inc(sem("samples_dve"), 1)
            dve.wait_ge(*signal("s_sp", 1))
            chain(V.memset(suf[:, :, NPG - 1, :], 0.0))
            for n in range(NPG - 2, -1, -1):
                ins = V.tensor_tensor(suf[:, :, n, :], suf[:, :, n + 1, :], sps[:, :, n + 1, :], ALU.add)
                if n:
                    chain(ins)
            ins.then_inc(sem("samples_dve"), 1)
            V.memset(st[0:1, 212:213], 0.0).then_inc(sem("samples_dve"), 1)
            dve.wait_ge(*signal("s_c", 1))
            for c in range(2):
                f = sbs[:, 4 * c:4 * c + 4].rearrange("p b n j -> p (b n j)")
                ins = V.tensor_tensor(f, f, bank[c][:, :], ALU.add)
                if c == 0:
                    chain(ins)
            ins.then_inc(sem("samples_dve"), 1)
            dve.wait_ge(*signal("v_mm", 1))
            gb = ofs[:, 0:3, :].rearrange("p a b -> p (a b)")
            chain(V.tensor_copy(gb, bank[4][:, 0:192]))
            g3 = gb.rearrange("p (c r) -> p c r", r=3)
            acc, tmp = ofs[:, 3, :], ofs[:, 4, :]
            chain(V.tensor_tensor(acc, bank[5][:, 0:64], g3[:, :, 0], ALU.mult))
            for br in range(2):
                chain(V.tensor_tensor(tmp, bank[7][:, 64 * br:64 * br + 64], s64[:, 7 + br, 0:64], ALU.mult))
                chain(V.tensor_tensor(tmp, tmp, g3[:, :, 1 + br], ALU.mult))
                chain(V.tensor_tensor(acc, acc, tmp, ALU.add))
            mx = ofs[:, 8, :].rearrange("p (k b) -> p k b", k=KD)
            a3 = acc.rearrange("p (b j) -> p b j", b=B)
            o4 = bank[6][:, 0:64].rearrange("p (t b two) -> p t b two", t=4, two=2)
            for kh in range(2):
                lo = kh * DH
                chain(V.tensor_copy(mx[lo:lo + DH, 0:4, :], o4[lo:lo + DH, :, :, kh]))
                chain(V.tensor_copy(mx[lo:lo + DH, 4:8, :], a3[lo:lo + DH, :, kh * G:(kh + 1) * G].rearrange("p b g -> p g b")))
            V.tensor_tensor(ofs[:, 9, :], ofs[:, 8, :], ofs[:, 8, :], ALU.mult).then_inc(sem("samples_dve"), 1)
            dve.wait_ge(*signal("v_ss", 1))
            V.tensor_reduce(st[:, 48:64].rearrange("p (a b) -> p a b", a=2), bank[3][:, 0:64].rearrange("p (a t b) -> p a b t", a=2, t=4), AX.X, ALU.add).then_inc(sem("samples_dve"), 1)
            dve.wait_ge(*signal("v_rt", 1))
            chain(V.reciprocal(st[:, 128:144], st[:, 64:80]))
            for a in range(2):
                v = mx[:, 4 * a:4 * a + 4, :]
                chain(V.tensor_tensor(v, v, over(st[:, 128 + 8 * a:136 + 8 * a], 1, 4), ALU.mult))
            chain(V.tensor_tensor(hT[:, :, SEQ:TOK], mx, over(vcol[:, 16:24], 2, B), ALU.mult))
            for a, o in enumerate((o_sb, o_n)):
                for t in range(NT):
                    chain(V.tensor_tensor_reduce(sps[:, 0:4].rearrange("p b n j -> p (b n j)"), o[:, t, :], o[:, t, :], 1.0, 0.0,
                                                 ALU.mult, ALU.add, st[:, 88 + 4 * a + t:89 + 4 * a + t]))
            V.memset(st[0:1, 213:214], 0.0).then_inc(sem("samples_dve"), 1)
            dve.wait_ge(*signal("mix_rt", 1))
            chain(V.reciprocal(st[:, 144:152], st[:, 96:104]))
            for a, o in enumerate((o_sb, o_n)):
                for t in range(NT):
                    ins = V.tensor_scalar(o[:, t, :], o[:, t, :], st[:, 144 + 4 * a + t:145 + 4 * a + t], None, ALU.mult)
                    if 4 * a + t < 7:
                        chain(ins)
            ins.then_inc(sem("mix_ready"), 1)
            for k in range(KD):
                dve.wait_ge(sem("mixT_mm"), k + 1)
                V.tensor_scalar(hT[:, k, 0:SEQ], bank[k % 2][:, :], vcol[:, 16 + k:17 + k], None, ALU.mult).then_inc(sem("mixT_ev"), 1)
            dve.wait_ge(sem("mixT_ev"), KD)
            V.memset(st[0:1, 214:215], 0.0).then_inc(sem("mix_ready"), 1)
            dve.wait_ge(sem("x2_in"), 32)
            for n in range(2 * T5):
                t, c = n // 2, n % 2
                dve.wait_ge(sem("out_mm"), n + 1)
                xv = x[0:rows[t], t, c * 512:(c + 1) * 512]
                V.tensor_tensor(xv, xv, bank[4 + n % 4][0:rows[t], :], ALU.add).then_inc(sem("res_ev"), 1)
            dve.wait_ge(sem("res_ev"), 2 * T5)
            row_scales(h2, 1).then_inc(sem("h_ready"), 1)
            gained(8, 1)
            dve.wait_ge(sem("hT_ev"), 18)
            with dve.Fori(0, FT // 2) as i:
                for u in range(2):
                    dve.wait_ge(sem(f"up_ev{u}"), i + 1 + 1)
                    a = aT[:, ds(i * 2 + u, 1), :].rearrange("p o c -> p (o c)")
                    V.tensor_tensor(a, h2[:, u, 0:TOK], h2[:, u, 0:TOK], ALU.mult).then_inc(sem(f"a_ready{u}"), 1)
            for u in range(2):
                dve.wait_ge(sem(f"a_ready{u}"), FT // 2 + 1)
            with dve.Fori(0, KD // 2) as i:
                for u in range(2):
                    dve.wait_ge(sem(f"dn_free{u}"), i + 1 + 1)
                    dve.wait_ge(sem(f"y_mm{u}"), i + 1)
                    V.tensor_copy(yT[u][:, 0:SEQ], bank[u][:, :])
                    V.tensor_copy(yT[u][:, SEQ:TOK], bank[2 + u][:, 0:B]).then_inc(sem(f"dn_ev{u}"), 1)
                    dve.wait_ge(sem(f"y_mm{u}"), i + 1 + 1)
                    xv = x[:, 0:NT, ds(i * (2 * P) + u * P, P)]
                    V.tensor_tensor(xv, xv, bank[4 + u].rearrange("p (t c) -> p t c", t=NT), ALU.add)
                    xv = x[0:B, NT, ds(i * (2 * P) + u * P, P)]
                    V.tensor_tensor(xv, xv, bank[6 + u][0:B, 0:P], ALU.add).then_inc(sem(f"y_ev{u}"), 1)
            for u in range(2):
                dve.wait_ge(sem(f"y_ev{u}"), KD // 2 + 1)
            chain(row_scales(h2, 2))
            dve.wait_ge(sem("gfin_in"), 16)
            for t in range(T5):
                ins = V.tensor_tensor(h2[0:rows[t], t, :], h2[0:rows[t], t, :], gfin[0:rows[t], :], ALU.mult)
                if t < T5 - 1:
                    chain(ins)
            ins.then_inc(sem("y_ready"), 1)

        @block.gpsimd
        def _(pool):
            G_ = nc.gpsimd
            prime(pool, "pool")

            G_.memset(z[:, NT, :], 0.0).then_inc(sem("z_zero"), 1)
            pool.wait_ge(sem("qkT_mm"), 15)
            pool.wait_ge(sem("sb_stored"), 16)

            def permute(c, u, n):
                for kv in range(2):
                    if c:
                        pool.wait_ge(sem(f"hid_mm{kv}"), c)
                    for hh in range(KVH):
                        ins = G_.tensor_copy(per(kv, hh)[0:n], nat[u][0:n, :, kv, hh, :])
                    ins.then_inc(sem("perm0" if kv == 0 else f"perm1_{u}"), 1)

            for c in range(B):
                pool.wait_ge(sem(f"nat_in{c % 2}"), (c // 2 + 1) * (16 * NPG))
                permute(c, c % 2, NCH)
            pool.wait_ge(sem("nat_in0"), 4 * 16 * NPG + 16)
            permute(B, 0, NCP + 1)
            pool.wait_ge(sem("cp_out"), NT)
            for hd in range(H):
                if hd:
                    pool.wait_ge(sem("sb_c"), 4 * hd)
                    pool.wait_ge(sem("sb_run"), 4 * hd)
                G_.memset(srun[:, :], 0.0).then_inc(sem("run_zero"), 1)
                pool.wait_ge(sem("run_zero"), hd + 1)
                for i in (3, 2, 1, 0):
                    m = 4 * hd + 3 - i
                    pool.wait_ge(sem("sb_sp"), m + 1)
                    pool.wait_ge(sem("sb_c"), m + 1)
                    if i < 3:
                        pool.wait_ge(sem("sb_run"), m)
                    G_.tensor_tensor(srun[:, i * P:SEQ], srun[:, i * P:SEQ], spb[:, m % 2, 0:SEQ - i * P], ALU.add).then_inc(sem("sb_run"), 1)


_INS = ["x_prompt", "x_sample", "cache_sb_kv", "cache_nsa_cmp_kv", "cache_nsa_slc_kv", "state_nsa_win_kv", "page_table",
        "w_in", "w_cmp_k1", "w_cmp_k2", "w_cmp_v1", "w_cmp_v2", "pe_cmp_k", "pe_cmp_v", "g_sb_out", "g_nsa_out", "w_out",
        "g_attn_norm", "g_mlp_norm", "w_up", "w_down", "g_final"]
_OUTS = [("y_p", (1, SEQ, D)), ("y_s", (B, 1, D)), ("sb_p", (1, 1, SEQ, 2, H, DH)), ("sb_s", (1, B, 1, 2, H, DH)),
         ("cmp_p", (1, 1, SEQ, 2, KVH, DH)), ("cmp_s", (1, B, 1, 2, KVH, DH)),
         ("slc_p", (1, 1, SEQ, 2, KVH, DH)), ("slc_s", (1, B, 1, 2, KVH, DH)),
         ("win_p", (1, 1, SEQ, 2, KVH, DH)), ("win_s", (1, B, WIN, 2, KVH, DH))]


def build(nc, shapes):
    A = {n: nc.dram_tensor(f"in_{n}_dram", s, d, kind="ExternalInput").ap() for n, (s, d) in shapes.items()}
    O = {n: nc.dram_tensor(f"out_{n}_dram", s, F32, kind="ExternalOutput").ap() for n, s in _OUTS}
    decoder_step(nc, A, O)


def kernel(**inputs):
    import concourse.bacc as bacc
    from concourse.bass_utils import run_bass_kernel_spmd as run

    arrays = {n: np.ascontiguousarray(inputs[n]) for n in _INS}
    arrays["consts"] = shape_constants()
    nc = bacc.Bacc("TRN2", target_bir_lowering=False, num_devices=1)
    build(nc, {n: (a.shape, mybir.dt.from_np(a.dtype)) for n, a in arrays.items()})
    r = run(nc, [{f"in_{n}_dram": a for n, a in arrays.items()}], core_ids=[0])
    return tuple(r.results[0][f"out_{n}_dram"] for n, _ in _OUTS)
```

```python
from contextlib import ExitStack

import numpy as np
import concourse.bass as bass
from concourse import mybir
from concourse.alu_op_type import AluOpType as ALU

ACT = mybir.ActivationFunctionType
AX = mybir.AxisListType
F32 = mybir.dt.float32
I32 = mybir.dt.int32
ds = bass.ds

P = 128
D = 1024
KD = D // P
SEQ, NT = 512, 4
B = 8
TOK = SEQ + B
HALF = TOK // 2
T5 = NT + 1
H, DH, KVH, G = 8, 64, 2, 4
PAST, PAGE = 2048, 128
NPG = PAST // PAGE
NPHYS = 160
COLS = 2840
CB = COLS // 8
O_QS, O_KS, O_VS, O_QN, O_C, O_S, O_W, O_G = 0, 512, 1024, 1536, 2048, 2304, 2560, 2816
CH = 16
NCH = PAST // CH
NC = NCH - 1
NCP = SEQ // CH - 1
NSEL = 33
TOPN = 16
WIN = 512
NW = WIN // PAGE
DFF = 4096
FT = DFF // P
NEG, TINY, FORCE, EPS = -1e30, 1e-30, 1e9, 1e-6
SCALE = DH ** -0.5


class Fields:

    def __init__(self, start, end):
        self.at, self.end = start, end

    def take(self, n):
        lo = self.at
        self.at += n
        assert self.at <= self.end, (self.at, self.end)
        return lo


CONST_FIELDS = [("ident", P), ("ntri", P), ("nones", P), ("ones", P), ("causal", P), ("before", P),
                ("half", P), ("pagemap", (NPG + 1) * 16), ("overlap", NSEL), ("lower", NSEL * NSEL),
                ("cadd", NT * NCP), ("cmul", NT * NCP), ("cos", T5 * DH), ("sin", T5 * DH), ("eps", 1), ("one", 1)]
CONST_AT = {}
_n = 0
for _name, _w in CONST_FIELDS:
    CONST_AT[_name] = (_n, _w)
    _n += _w
NCONST = _n


def shape_constants():
    c = np.zeros((P, NCONST), np.float32)

    def put(name, a):
        lo, _ = CONST_AT[name]
        a = a.reshape(a.shape[0], -1)
        c[:a.shape[0], lo:lo + a.shape[1]] = a

    r = np.arange(P)
    put("ident", np.eye(P))
    put("ntri", -(r[:, None] >= r[None, :]).astype(np.float32))
    put("nones", -np.ones((P, P)))
    put("ones", np.ones((P, P)))
    put("causal", np.where(r[None, :] <= r[:, None], 0.0, NEG))
    put("before", (r[:, None] < r[None, :]).astype(np.float32))
    blk = np.arange(NSEL)
    put("half", (blk[:, None] % 2 == (r[None, :] >= P // 2)).astype(np.float32))
    put("pagemap", np.repeat((blk[:, None] // 2 == np.arange(NPG + 1)[None, :])[:, :, None], 16, 2).astype(np.float32))
    cs = np.arange(NC) * CH
    put("overlap", ((cs[:, None] < blk[None, :] * 64 + 64) & (cs[:, None] + 32 > blk[None, :] * 64)).astype(np.float32))
    put("lower", np.broadcast_to((blk[None, :] < blk[:, None])[None], (16, NSEL, NSEL)).astype(np.float32))
    q = np.arange(NT)[None, :, None] * P + r[:, None, None]
    ok = (np.arange(NCP) * CH + 31)[None, None, :] <= q
    put("cadd", np.where(ok, 0.0, NEG))
    put("cmul", ok.astype(np.float32))
    inv = np.float32(10000.0) ** (-np.arange(32, dtype=np.float32) / np.float32(32))
    pos = np.zeros((P, T5), np.float32)
    pos[:, :NT] = np.arange(NT)[None, :] * P + r[:, None]
    pos[:, NT] = PAST
    ang = pos[:, :, None] * inv[None, None, :].astype(np.float32)
    co, si = np.cos(ang), np.sin(ang)
    put("cos", np.concatenate([co, co], -1))
    put("sin", np.concatenate([-si, si], -1))
    put("eps", np.full((P, 1), EPS))
    put("one", np.full((P, 1), 1.0))
    return c


_MAX = ["m_max", "m_diag", "m_sub", "m_sum", "m_rec"]
SIGNALS = {
    "samples_pe": ["c_sc", "c_scT", "c_pT", "c_imp", "c_selT", "c_mask", "m_T", "m_b", "m_den", "m_T", "m_b", "m_den",
                   "s_c", "v_mm", "v_ss"],
    "samples_dve": ["c_s", "s_abs", "c_nm", "c_p", "s_sp", "c_pg", "c_sel", "s_suf", "c_selx", "c_selm"] + _MAX * 2
    + ["s_d", "z_free", "v_sq", "v_st", "mix_ss"],
    "samples_act": ["s_ln", "c_e", "m_e", "m_e", "s_a", "v_rt", "mix_rt"],
}


PRIMED = {
    "pe": ["kq_mm0", "kq_mm1"] + [f"vq_mm{q}" for q in range(5)] + [f"ring_free{u}" for u in range(8)]
    + ["w2_mm0", "w2_mm1", "qs_mm", "up_free0", "up_free1", "dn_free0", "dn_free1", "y_mm0", "y_mm1"],
    "act": ["z_ev1", "z_ev3", "xT_ev0", "xT_ev1", "qs_ev", "kq_ev", "up_ev0", "up_ev1"],
    "dve": ["win_free0", "win_free1", "z_ev0", "z_ev2", "z_ev4", "hid_ready0", "hid_ready1", "qb_free0", "qb_free1", "kvc_ev0", "kvc_ev1",
            "a_ready0", "a_ready1", "dn_ev0", "dn_ev1", "y_ev0", "y_ev1"],
    "pool": ["perm1_0", "perm1_1"],
}


class Chain:

    def __init__(self, eng, sem):
        self.eng, self.sem, self.n, self.off = eng, sem, 0, 0

    def __call__(self, ins):
        self.n += 1
        ins.then_inc(self.sem, 1)
        self.eng.wait_ge(self.sem, self.off + self.n)


class Turns:

    def __init__(self, chain, count, per):
        self.chain, self.count, self.per = chain, count, per

    def __enter__(self):
        c = self.chain
        self.first = c.n
        self.loop = c.eng.Fori(0, self.count)
        i = self.loop.__enter__()
        c.off = i * self.per
        return i

    def __exit__(self, *e):
        c = self.chain
        if e[0] is None:
            assert c.n - self.first == self.per, (c.n - self.first, self.per)
        c.off = 0
        c.n = self.first + self.count * self.per
        return self.loop.__exit__(*e)


def decoder_step(nc, A, O):
    with ExitStack() as ctx:
        sems = {}

        def signal(name, v):
            group = [g for g, order in SIGNALS.items() if name in order][0]
            return sem(group), [n for n, x in enumerate(SIGNALS[group], 1) if x == name][v - 1]

        def prime(eng, who):
            for name in PRIMED[who]:
                eng.sem_inc(sem(name), 1)

        def sem(name):
            if name not in sems:
                sems[name] = ctx.enter_context(nc.semaphore(name))
            return sems[name]

        TOTAL = 52900
        arena = ctx.enter_context(nc.sbuf_tensor("arena", [P, TOTAL], F32))
        pt = ctx.enter_context(nc.sbuf_tensor("page_ids", [1, B * NPG], I32))
        bank = [ctx.enter_context(nc.psum_tensor(f"bank{i}", [P, 512], F32)) for i in range(8)]
        sbq_dram = nc.dram_tensor("sb_queries", (B, 512), F32, kind="Internal").ap()

        def view(lo, *dims):
            n = int(np.prod(dims))
            a = arena[:, lo:lo + n]
            names = "abcd"[:len(dims)]
            if len(dims) > 1:
                a = a.rearrange(f"p ({' '.join(names)}) -> p {' '.join(names)}", **dict(zip(names, dims)))
            return a

        allr = Fields(0, TOTAL)
        const = view(allr.take(NCONST), NCONST)

        def K(name):
            lo, w = CONST_AT[name]
            return const[:, lo:lo + w]

        ident, ntri, nones, ones = K("ident"), K("ntri"), K("nones"), K("ones")
        vrow = view(allr.take(P), P)
        vcol = view(allr.take(56), 56)
        st = view(allr.take(256), 256)
        zero = view(allr.take(P), P)
        z = view(allr.take(T5 * COLS), T5, COLS)
        sbqT = view(allr.take(4 * SEQ), 4, SEQ)
        sbkT = view(allr.take(4 * SEQ), 4, SEQ)
        nqT = view(allr.take(4 * SEQ), 4, SEQ)
        ksT = view(allr.take(SEQ), SEQ)
        kwT = view(allr.take(SEQ), SEQ)
        hT_at = allr.take(KD * TOK)
        hT = view(hT_at, KD, TOK)
        x_at = allr.take(T5 * D)
        x = view(x_at, T5, D)
        r_at = allr.at

        r = Fields(r_at, TOTAL)
        h_at = r.take(T5 * D)
        h = view(h_at, T5, D)
        win = [view(r.take(KD * CB), KD, CB) for _ in range(2)]
        r = Fields(r_at, TOTAL)
        ropeA, ropeB = view(r.take(512), 512), view(r.take(512), 512)
        r = Fields(r_at + 1024, TOTAL)
        qbd = view(r.take(B * H), B, H)
        snew = view(r.take(2 * H), 2, H)
        qsc = view(r.take(512), 512)
        newrow = view(r.take(2 * B * H), 2, B, H)
        vnew = view(r.take(2 * B * P), 2, B, P)
        grow = view(r.take(B * 24), B, H, 3)
        kc = view(r.take((B + 1) * P), B + 1, P)
        vc = view(r.take((B + 1) * P), B + 1, P)
        slc = view(r.take(B * (NPG + 1) * H), B, NPG + 1, H)
        wsc = view(r.take(B * (NW + 1) * H), B, NW + 1, H)
        att_at = r.at
        w1 = [view(x_at + i * 2048, 16, P) for i in range(2)]
        w2 = [view(x_at + 4096 + i * DH, DH) for i in range(2)]
        pebias = view(x_at + 4224, 4)
        xT = [view(hT_at + i * 2048, KD, KVH, P) for i in range(2)]
        nat = [view(r.take(4096), CH, 2, KVH, DH) for _ in range(2)]
        hid = [view(r.take(256), KVH, P) for _ in range(4)]
        qb = view(r.take(2 * 512), 2, 512)
        kqT = view(x_at + 4228, 4, P)
        kring = [z[:, t, O_QN:O_QN + 512] for t in range(NT)] + [z[:, NT, u * 512:(u + 1) * 512] for u in range(4)]
        kquad = [z[:, 0:NT, o:o + P] for o in (O_S, O_W)]

        def raw_scores(i, u):
            return z[:, i, O_C + u * P:O_C + (u + 1) * P].rearrange("p o (n j) -> p (o n) j", j=H)


        def per(kv, hh):
            return z[:, 2 * kv + hh, 0:1024].rearrange("p (t d) -> p t d", t=CH)

        a1 = Fields(x_at, r_at)
        r = Fields(att_at, TOTAL)
        ring = view(a1.take(8 * 512), 8, 512)
        vsum = view(a1.take(2 * 512), 2, 512)
        quad = view(r.take(5 * 512), 5, 4, P)
        sbs = view(r.take(B * NPG * H), B, NPG, H)
        osb_at = r.take(NT * 512)
        o_sb = view(osb_at, NT, 512)
        o_n = view(r.take(NT * 512), NT, 512)
        w0 = w = Fields(r.at, TOTAL)
        pbuf = view(w.take(2 * 512), 2, 512)
        ptb = view(w.take(2 * 512), 2, 512)
        w = Fields(hT_at, hT_at + KD * TOK)
        spb = view(w.take(2 * 512), 2, 512)
        ebuf = view(w.take(2 * 512), 2, 512)
        abuf = view(w.take(2 * 512), 2, 512)
        srun = view(w.take(512), 512)
        ofs = view(w0.take(12 * 64), 12, 64)
        w = Fields(osb_at, osb_at + NT * 512)
        sps = view(w.take(1024), B, NPG, H)
        suf = view(w.take(1024), B, NPG, H)
        w = Fields(hT_at, hT_at + KD * TOK)
        s64 = view(w.take(9 * P), 9, P)
        rankA = view(w.take(NSEL * NSEL), NSEL, NSEL)
        rankB = view(w.take(NSEL * NSEL), NSEL, NSEL)
        selx = view(w.take(272), NPG + 1, 16)
        selm = view(w.take(272), NPG + 1, 16)
        pcT = view(w.take(64), 64)
        aT_at = NCONST + P + 56 + 256 + P
        aT = view(aT_at, FT, TOK)
        wout = view(aT_at, KD, D)
        assert aT_at + FT * TOK <= hT_at
        r = Fields(r_at, TOTAL)
        h2 = view(r.take(T5 * D), T5, D)
        upw = [view(r.take(KD * P), KD, P) for _ in range(2)]
        dnw = [view(r.take(FT * P), FT, P) for _ in range(2)]
        yT = [view(r.take(TOK), TOK) for _ in range(2)]
        gfin = view(r.take(D), D)
        rows = [P] * NT + [B]

        def over(ap, axis, n):
            a = ap.unsqueeze(axis)
            shape = list(a.shape)
            shape[axis] = n
            return a.broadcast_to(shape)

        def place(hd):
            return (hd % G) * KVH + hd // G

        block = ctx.enter_context(nc.Block())
        xp, xs = A["x_prompt"][0], A["x_sample"].rearrange("b o d -> (b o) d")
        c_sb, c_cmp, c_slc = A["cache_sb_kv"][0], A["cache_nsa_cmp_kv"][0], A["cache_nsa_slc_kv"][0]
        w_in, w_up, w_down, w_out = A["w_in"][0], A["w_up"][0], A["w_down"][0], A["w_out"][0]

        @block.sync
        def _(sp):
            sp.dma_start(const, A["consts"]).then_inc(sem("const_in"), 16)
            sp.dma_start(x[:, 0:NT, :], xp.rearrange("(t p) d -> p t d", p=P)).then_inc(sem("x_in"), 16)
            sp.dma_start(x[0:B, NT, :], xs).then_inc(sem("x_in"), 16)
            for r0, n, src in ((0, 8, A["g_attn_norm"][0]), (8, 8, A["g_mlp_norm"][0]), (16, 4, A["g_sb_out"][0])):
                sp.dma_start(vrow[r0:r0 + n, :], src.rearrange("(r c) -> r c", c=P)).then_inc(sem("vrow_in"), 16)
            for two in range(2):
                sp.dma_start(vrow[20:24, two * DH:(two + 1) * DH],
                    A["g_nsa_out"][0].rearrange("(two t d) -> two t d", two=2, t=4)[two]).then_inc(sem("vrow_in"), 16)
            for r0, src in ((24, A["pe_cmp_k"][0]), (40, A["pe_cmp_v"][0])):
                sp.dma_start(vrow[r0:r0 + 16, :], src.rearrange("(m two) d -> m (two d)", two=2)).then_inc(sem("vrow_in"), 16)
            sp.dma_start(pt[:, :], A["page_table"].rearrange("(o b) n -> o (b n)", o=1)).then_inc(sem("pages_in"), 16)
            w_in_v = w_in.rearrange("(k p) c -> p k c", p=P)
            with sp.Fori(0, 4) as i:
                for u in range(2):
                    sp.wait_ge(sem(f"win_free{u}"), i + 1)
                    sp.dma_start(win[u][:, :, :], w_in_v[:, :, ds(i * (2 * CB) + u * CB, CB)]).then_inc(sem(f"win_in{u}"), 16)
            sp.wait_ge(sem("h_ready"), 2)
            for kv, n in enumerate(("w_cmp_k1", "w_cmp_v1")):
                sp.dma_start(w1[kv][:, :, :], A[n][0].rearrange("(m p) c -> p m c", p=P)).then_inc(sem("cmpw_in"), 16)
            for kv, n in enumerate(("w_cmp_k2", "w_cmp_v2")):
                sp.dma_start(w2[kv], A[n][0]).then_inc(sem("cmpw_in"), 16)
            sp.wait_ge(sem("pages_in"), 16)
            for t in range(T5):
                sp.wait_ge(sem(f"z_ev{t}"), 8 + 1)
            sp.wait_ge(sem("rope_done"), T5)
            sp.wait_ge(sem("qkT_mm"), 15)
            sp.wait_ge(sem("kv_out"), 16 * (B + 6))
            sp.wait_ge(sem("sbq_out"), 16)
            sp.wait_ge(sem("rows_in"), 96)
            win_v = A["state_nsa_win_kv"][0].rearrange("b (t p) k h d -> b p t k (h d)", p=P)

            def page_ids(lo):
                return nc.values_load_multi_w_load_instructions(
                    pt[0:1, ds(lo, 8)], engines=[mybir.EngineType.SP], min_val=0, max_val=NPHYS - 1,
                    skip_runtime_bounds_check_because="entries of the page table are pages of the caches")[1]

            def load_chunks(lo, u, half):
                for p, pg in enumerate(page_ids(lo + 8 * half), 8 * half):
                    sp.dma_start(nat[u][8 * p:8 * p + 8].rearrange("p t k h d -> p (t k h d)"),
                                 c_cmp[ds(pg, 1)].rearrange("o (c t) k h d -> (o c) (t k h d)", t=CH)).then_inc(sem(f"nat_in{u}"), 16)

            def load_keys(i, u, ahead):
                c = i * 2 + u
                sp.wait_ge(sem(f"qb_free{u}"), i + 1)
                sp.dma_start(qb[:, u, :], sbq_dram[ds(c, 1), :].broadcast_to([P, 512])).then_inc(sem(f"qb_in{u}"), 16)
                for half in range(2):
                    if ahead:
                        if half == 0:
                            sp.wait_ge(sem(f"perm1_{1 - u}"), i + u + 1)
                        load_chunks(c * NPG + NPG, 1 - u, half)
                    pages = page_ids(c * NPG + 8 * half)
                    for p in range(8):
                        if p % 4 == 0:
                            n = 5 * u + 2 * half + p // 4
                            sp.wait_ge(sem(f"kq_mm{n % 2}"), i * 5 + n // 2 + 1)
                            for j in range(4):
                                sp.dma_start(kquad[n % 2][:, j], c_slc[ds(pages[p + j], 1), :, 0].rearrange("o s h d -> (o s) (h d)")
                                             ).then_inc(sem(f"kq_in{n % 2}"), 16)
                        sp.wait_ge(sem(f"ring_free{p}"), i * 4 + 2 * u + half + 1)
                        sp.dma_start(kring[p], c_sb[ds(pages[p], 1), :, 0].rearrange("o s h d -> (o s) (h d)")).then_inc(sem(f"ring_in{p}"), 16)
                n = 5 * u + 4
                sp.wait_ge(sem(f"kq_mm{n % 2}"), i * 5 + n // 2 + 1)
                sp.dma_start(kquad[n % 2], win_v[ds(c, 1), :, :, 0, :].rearrange("o p t c -> (o p) t c")).then_inc(sem(f"kq_in{n % 2}"), 64)

            for half in range(2):
                load_chunks(0, 0, half)
            with sp.Fori(0, 3) as i:
                for u in range(2):
                    load_keys(i, u, True)
            load_keys(3, 0, True)
            sp.wait_ge(sem("cmp_stored"), 16)
            sp.wait_ge(sem("perm1_0"), 4 + 1)
            sp.dma_start(nat[0][0:NCP + 1].rearrange("p t k h d -> p (t k h d)"),
                O["cmp_p"][0, 0].rearrange("(c t) k h d -> c (t k h d)", t=CH)).then_inc(sem("nat_in0"), 16)
            load_keys(3, 1, False)
            sp.wait_ge(sem("kvc_ev0"), 9 + 1)
            sp.wait_ge(sem("kvc_ev1"), 9 + 1)
            sp.wait_ge(sem("qs_ev"), B + 1)
            with sp.Fori(0, B) as b:
                for half in range(2):
                    pages = page_ids(b * NPG + 8 * half)
                    for u in range(8):
                        sp.wait_ge(sem(f"ring_free{u}"), b * 2 + (2 * B + half + 1))
                        sp.dma_start(ring[:, u, :], c_sb[ds(pages[u], 1), :, 1].rearrange("o s h d -> (o s) (h d)")).then_inc(sem(f"ring_in{u}"), 16)
                        if u % 4 == 3:
                            q = 2 * half + u // 4
                            sp.wait_ge(sem(f"vq_mm{q}"), b + 1)
                            for j in range(4):
                                sp.dma_start(quad[:, q, j, :], c_slc[ds(pages[u - 3 + j], 1), :, 1].rearrange("o s h d -> (o s) (h d)")
                                             ).then_inc(sem(f"quad_in{q}"), 16)
                sp.wait_ge(sem("vq_mm4"), b + 1)
                sp.dma_start(quad[:, 4], win_v[ds(b, 1), :, :, 1, :].rearrange("o p t c -> (o p) t c")).then_inc(sem("quad_in4"), 64)
            sp.wait_ge(*signal("z_free", 1))
            sp.wait_ge(sem("kv_out"), 16 * (B + 6))
            sp.wait_ge(sem("rows_in"), 96)
            for r0 in range(0, 4, 2):
                sp.dma_start(wout[:, r0:r0 + 2, :], w_out.rearrange("(k p) c -> p k c", p=P)[:, r0:r0 + 2, :]).then_inc(sem("wout_in"), 16)
            for two in range(2):
                sp.dma_start(wout[two * DH:(two + 1) * DH, 4:8, :],
                    w_out[512 + 256 * two:768 + 256 * two, :].rearrange("(t d) c -> d t c", d=DH)).then_inc(sem("wout_in"), 16)
            sp.wait_ge(sem("vsum_mm"), B)
            sp.dma_start(x[:, 0:NT, :], xp.rearrange("(t p) d -> p t d", p=P)).then_inc(sem("x2_in"), 16)
            sp.dma_start(x[0:B, NT, :], xs).then_inc(sem("x2_in"), 16)
            sp.wait_ge(sem("mix_ready"), 2)
            sp.wait_ge(sem("mixT_mm"), 4)
            sp.dma_start(gfin, A["g_final"].rearrange("(o d) -> o d", o=1).broadcast_to([P, D])).then_inc(sem("gfin_in"), 16)
            w_up_v = w_up.rearrange("(k p) c -> p k c", p=P)
            with sp.Fori(0, FT // 2) as i:
                for u in range(2):
                    sp.wait_ge(sem(f"up_free{u}"), i + 1)
                    sp.dma_start(upw[u][:, :, :], w_up_v[:, :, ds(i * (2 * P) + u * P, P)]).then_inc(sem(f"up_in{u}"), 16)
            w_dn_v = w_down.rearrange("(k p) c -> p k c", p=P)
            with sp.Fori(0, KD // 2) as i:
                for u in range(2):
                    sp.wait_ge(sem(f"dn_free{u}"), i + 1)
                    sp.dma_start(dnw[u][:, :, :], w_dn_v[:, :, ds(i * (2 * P) + u * P, P)]).then_inc(sem(f"dn_in{u}"), 16)
            sp.wait_ge(sem("y_ready"), 1)
            sp.dma_start(O["y_p"][0].rearrange("(t p) d -> p t d", p=P), h2[:, 0:NT, :]).then_inc(sem("y_out"), 16)
            sp.dma_start(O["y_s"].rearrange("b o d -> (b o) d"), h2[0:B, NT, :]).then_inc(sem("y_out"), 16)
            sp.wait_ge(sem("y_out"), 32)

        @block.tensor
        def _(pe):
            T = nc.tensor
            prime(pe, "pe")

            def mm(out, l, r, start=True, stop=True, **k):
                return T.matmul(out, lhsT=l, rhs=r, start=start, stop=stop, **k)

            def tr(out, in_):
                n = in_.shape[0]
                return T.transpose(out, in_, ident[0:n, 0:n])

            def norm_transposes(src, turn):
                pe.wait_ge(sem("h_ready"), 2 * turn + 1)
                for k in range(KD):
                    if k >= 2:
                        pe.wait_ge(sem("hT_ev"), turn * 9 + k - 1)
                    for t in range(NT):
                        i = tr(bank[k % 2][:, t * P:(t + 1) * P], src[:, t, k * P:(k + 1) * P])
                    i.then_inc(sem("hT_mm"), 1)
                pe.wait_ge(sem("h_ready"), 2 * turn + 2)
                for k in range(KD):
                    i = tr(bank[2][:, k * B:(k + 1) * B], src[0:B, NT, k * P:(k + 1) * P])
                i.then_inc(sem("hT_mm"), 1)

            pe.wait_ge(sem("const_in"), 16)
            pe.wait_ge(sem("vrow_in"), 16 * 7)
            tr(bank[3][:, 0:56], vrow[0:56, :]).then_inc(sem("vcol_mm"), 1)
            norm_transposes(h, 0)
            pe.wait_ge(sem("vcol_ev"), 1)
            pe.wait_ge(sem("hT_ev"), 9)
            with pe.Fori(0, 4) as i:
                for u in range(2):
                    pe.wait_ge(sem(f"win_in{u}"), i * 16 + 16)
                    for t in range(T5):
                        pe.wait_ge(sem(f"z_ev{t}"), i * 2 + u + 1)
                        for k in range(KD):
                            ins = mm(bank[t][0:rows[t], 0:CB], hT[:, k, t * P:t * P + rows[t]], win[u][:, k, :],
                                     k == 0, k == KD - 1)
                        ins.then_inc(sem("z_mm"), 1)
            pe.wait_ge(sem("rope_done"), T5)
            for t in range(T5):
                pe.wait_ge(sem(f"z_ev{t}"), 8 + 1)
            src = [(lambda t, j=j: z[:, t, O_QS + j * P:O_QS + (j + 1) * P]) for j in range(4)]
            src += [(lambda t, j=j: z[:, t, O_KS + j * P:O_KS + (j + 1) * P]) for j in range(4)]
            src += [(lambda t, j=j: z[:, t, O_QN + j * P:O_QN + (j + 1) * P]) for j in range(4)]
            src += [(lambda t, o=o: z[:, t, o:o + P]) for o in (O_S, O_W)]
            for j, s in enumerate(src):
                if j >= 4:
                    pe.wait_ge(sem(f"qkT_ev{j % 2}"), (j - 4) // 2 + 1)
                for t in range(NT):
                    ins = tr(bank[j % 4][:, t * P:(t + 1) * P], s(t))
                ins.then_inc(sem("qkT_mm"), 1)
            for j in range(4):
                ins = tr(bank[4][:, j * B:(j + 1) * B], z[0:B, NT, O_QN + j * P:O_QN + (j + 1) * P])
            ins.then_inc(sem("qkT_mm"), 1)
            pe.wait_ge(sem("cmpw_in"), 64)
            for kv in range(2):
                for m in range(16):
                    ins = mm(bank[6][:, kv:kv + 1], w1[kv][:, m, :], vcol[:, 24 + 16 * kv + m:25 + 16 * kv + m],
                             m == 0, m == 15)
            ins.then_inc(sem("pe_mm"), 1)
            for j in range(2):
                pe.wait_ge(sem(f"qkT_ev{j}"), 7)
            pe.wait_ge(sem("qkT_ev0"), 8)
            pe.wait_ge(sem("pebias"), 2)

            def keys_T(i, u, q):
                n = 5 * u + q
                pe.wait_ge(sem(f"kq_in{n % 2}"), (i * 5 + n // 2 + 1) * 64)
                pe.wait_ge(sem("kq_ev"), i * 10 + n + 1)
                for j in range(4):
                    ins = tr(bank[6][:, j * P:(j + 1) * P], kquad[n % 2][:, j])
                ins.then_inc(sem(f"kq_mm{n % 2}"), 1)

            def key_scores(i, u, q):
                pe.wait_ge(sem("kq_ev"), i * 10 + 5 * u + q + 1 + 1)
                if q == 0:
                    pe.wait_ge(sem("qs_ev"), i * 2 + u + 1)
                for j in range(4):
                    c = (4 * q + j) * H
                    ins = mm(bank[7][:, c:c + H], kqT[:, j, :], qbd[:, ds(i * 2 + u, 1), :].rearrange("p o j -> p (o j)"))
                ins.then_inc(sem("qs_mm"), 1)

            def compress(c, u, i, n, between):
                nb = n - 1
                for kv in range(2):
                    if kv == 0:
                        pe.wait_ge(sem("perm0"), c + 1)
                    else:
                        pe.wait_ge(sem(f"perm1_{u}"), i + 1 + 1)
                    pe.wait_ge(sem(f"hid_ready{kv}"), c + 1)
                    for s in range(5):
                        if s < 4:
                            pe.wait_ge(sem(f"xT_ev{s % 2}"), c * 4 + kv * 2 + s // 2 + 1)
                            for j in range(2):
                                for hh in range(KVH):
                                    m = 2 * s + j
                                    ins = tr(bank[s % 2][:, (2 * j + hh) * P:(2 * j + hh) * P + n],
                                             per(kv, hh)[0:n, 2 * m:2 * m + 2, :].rearrange("p t d -> p (t d)"))
                            ins.then_inc(sem("xT_mm"), 1)
                        if s >= 1:
                            pe.wait_ge(sem(f"xT_ev{(s - 1) % 2}"), c * 4 + kv * 2 + (s - 1) // 2 + 1 + 1)
                            for m in (2 * s - 2, 2 * s - 1):
                                out = bank[2 + kv][:, 0:KVH * nb].rearrange("p (h c) -> p h c", h=KVH)
                                mm(out, w1[kv][:, m, :], xT[kv][:, m, :, 0:nb], m == 0, False)
                                ins = mm(out, w1[kv][:, 8 + m, :], xT[kv][:, m, :, 1:n], False, m == 7)
                            if s == 4:
                                ins.then_inc(sem(f"hid_mm{kv}"), 1)
                        if s in (1, 3):
                            between()
                between()
                between()
                pe.wait_ge(sem("hid_ready0"), c + 1 + 1)
                pe.wait_ge(sem("kvc_ev0"), c + 1)
                for hh in range(KVH):
                    ins = mm(bank[4][DH * hh:DH * (hh + 1), 0:nb], w2[0], hid[2][:, hh, 0:nb])
                ins.then_inc(sem("w2_mm0"), 1)
                pe.wait_ge(sem("hid_ready1"), c + 1 + 1)
                pe.wait_ge(sem("kvc_ev1"), c + 1)
                for hh in range(KVH):
                    ins = mm(bank[5][0:nb, DH * hh:DH * (hh + 1)], hid[3][:, hh, 0:nb], w2[1])
                ins.then_inc(sem("w2_mm1"), 1)

            with pe.Fori(0, 4) as i:
                for u in range(2):
                    todo = [lambda: keys_T(i, u, 0)]
                    for q in range(4):
                        todo.append(lambda q=q: (key_scores(i, u, q), keys_T(i, u, q + 1)))
                    todo.append(lambda: key_scores(i, u, 4))
                    compress(i * 2 + u, u, i, NCH, lambda: todo.pop(0)())
            compress(B, 0, 4, NCP + 1, lambda: None)

            for kv in range(2):
                pe.wait_ge(sem(f"kvc_ev{kv}"), B + 1 + 1)
            pe.wait_ge(sem("qs_ev"), B + 1)

            def cp_qk(i):
                if i >= 1:
                    pe.wait_ge(sem("cp_soft"), i)
                for n in range(H):
                    o = DH * (n // G)
                    ins = mm(bank[4 + n // G][:, (n % G) * NCP:(n % G + 1) * NCP], nqT[o:o + DH, n % G, i * P:(i + 1) * P],
                             kc[o:o + DH, B, 0:NCP])
                ins.then_inc(sem("cp_qk"), 1)

            def cp_tr(i):
                pe.wait_ge(sem("cp_soft"), i + 1)
                if i >= 1:
                    pe.wait_ge(sem("cp_pT"), 2 * i)
                for n in range(H):
                    ins = tr(bank[6 + n // 4][0:NCP, (n % 4) * P:(n % 4 + 1) * P], pbuf[:, 0, n * NCP:(n + 1) * NCP])
                    if n % 4 == 3:
                        ins.then_inc(sem("cp_tr"), 1)

            def cp_pv(i):
                pe.wait_ge(sem("cp_pT"), 2 * i + 2)
                if i >= 2:
                    pe.wait_ge(sem("cp_out"), i - 1)
                for n in range(H):
                    o = DH * (n // G)
                    ins = mm(bank[i % 2][:, place(n) * DH:(place(n) + 1) * DH], ptb[0:NCP].rearrange("p a b -> p (a b)")[:, n * P:(n + 1) * P],
                             vc[0:NCP, B, o:o + DH])
                ins.then_inc(sem("cp_pv"), 1)

            def row_max(br):
                pe.wait_ge(*signal("m_max", br + 1))
                tr(bank[2][0:64, 0:P], s64[:, 0, 0:64]).then_inc(sem("samples_pe"), 1)

            def row_max_over(br):
                pe.wait_ge(*signal("m_diag", br + 1))
                mm(bank[3][:, 0:64], ones[0:64, :], s64[0:64, 1, 0:64]).then_inc(sem("samples_pe"), 1)

            def row_sum_over(br):
                pe.wait_ge(*signal("m_sum", br + 1))
                mm(bank[2][:, 0:64], ones, s64[:, 3, 0:64]).then_inc(sem("samples_pe"), 1)

            for b in range(B):
                ins = mm(bank[2][0:NC, b * H:(b + 1) * H], kc[:, b, 0:NC], qbd[:, b, :])
            ins.then_inc(sem("samples_pe"), 1)
            cp_qk(0)
            pe.wait_ge(*signal("c_s", 1))
            tr(bank[3][0:64, 0:NC], s64[0:NC, 0, 0:64]).then_inc(sem("samples_pe"), 1)
            cp_tr(0)
            pe.wait_ge(*signal("c_p", 1))
            tr(bank[2][0:NC, 0:64], s64[0:64, 2, 0:NC]).then_inc(sem("samples_pe"), 1)
            cp_pv(0)
            cp_qk(1)
            pe.wait_ge(*signal("c_pg", 1))
            mm(bank[3][0:16, 0:NSEL], s64[0:NC, 3, 0:16], K("overlap")[0:NC, :]).then_inc(sem("samples_pe"), 1)
            cp_tr(1)
            cp_pv(1)
            cp_qk(2)
            pe.wait_ge(*signal("c_sel", 1))
            tr(bank[2][0:NSEL, 0:16], s64[0:16, 5, 0:NSEL]).then_inc(sem("samples_pe"), 1)
            cp_tr(2)
            cp_pv(2)
            pe.wait_ge(*signal("c_selx", 1))
            mm(bank[3][:, 0:272], K("half")[0:NSEL, :], selx[0:NSEL].rearrange("p a b -> p (a b)")).then_inc(sem("samples_pe"), 1)
            cp_qk(3)
            row_max(0)
            cp_tr(3)
            row_max_over(0)
            cp_pv(3)
            row_sum_over(0)
            row_max(1)
            row_max_over(1)
            row_sum_over(1)
            pe.wait_ge(sem("cp_pT"), 2 * NT)
            mm(bank[7][:, 0:256], zero, over(zero, 1, 2), True, False, skip_group_check=True)
            for b in range(B):
                mm(bank[7][:, 192 + b * H:192 + (b + 1) * H], vc[0:NC, b, :], pcT[0:NC, b * H:(b + 1) * H], False, False, skip_group_check=True)
            pe.wait_ge(*signal("s_suf", 1))
            pe.wait_ge(*signal("m_rec", 2))
            for c in range(2):
                mm(bank[2 + c][:, 0:512], ntri, sps[:, 4 * c:4 * c + 4].rearrange("p b n j -> p (b n j)"), True, False)
                ins = mm(bank[2 + c][:, 0:512], nones, suf[:, 4 * c:4 * c + 4].rearrange("p b n j -> p (b n j)"), False, True)
            ins.then_inc(sem("samples_pe"), 1)
            pe.wait_ge(sem("cp_out"), NT)
            pe.wait_ge(*signal("s_d", 1))

            def sb_qk(hd, i):
                m = 4 * hd + 3 - i
                if m >= 2:
                    pe.wait_ge(sem("sb_a"), m - 1)
                o = DH * (hd % 2)
                mm(bank[m % 2][:, 0:SEQ - i * P], sbkT[o:o + DH, hd // 2, i * P:(i + 1) * P],
                        sbqT[o:o + DH, hd // 2, i * P:SEQ], True, False, skip_group_check=True).then_inc(sem("sb_qk"), 1)

            def sb_sum(hd, i):
                m = 4 * hd + 3 - i
                pe.wait_ge(sem("sb_sp"), m + 1)
                n = SEQ - i * P
                ins = mm(bank[m % 2][:, 0:n], ntri, spb[:, m % 2, 0:n], False, i == 3, skip_group_check=True)
                if i < 3:
                    pe.wait_ge(sem("sb_run"), m)
                    ins = mm(bank[m % 2][:, P:n], nones, srun[:, (i + 1) * P:SEQ], False, True, skip_group_check=True)
                ins.then_inc(sem("sb_c"), 1)

            def sb_pv(hd, i):
                m = 4 * hd + 3 - i
                pe.wait_ge(sem("sb_am"), m + 1)
                if i == 3 and hd:
                    pe.wait_ge(sem("sb_out"), hd)
                for j in range(i, NT):
                    ins = mm(bank[2][:, j * DH:(j + 1) * DH], abuf[:, m % 2, (j - i) * P:(j - i + 1) * P],
                             z[:, i, O_VS + hd * DH:O_VS + (hd + 1) * DH], i == 3, i == 0, skip_group_check=True)
                ins.then_inc(sem("sb_pv"), 1)

            def n_unit(n):
                hd, br, i = n // 8, (n // 4) % 2, n % 4
                return hd, br, i, DH * (hd // G)

            def n_qk(n):
                hd, br, i, o = n_unit(n)
                if n >= 2:
                    pe.wait_ge(sem("n_exp"), n - 1)
                mm(bank[3 + n % 2][:, 0:(i + 1) * P], nqT[o:o + DH, hd % G, i * P:(i + 1) * P],
                        (ksT, kwT)[br][o:o + DH, 0:(i + 1) * P]).then_inc(sem("n_qk"), 1)

            def n_tr(n):
                hd, br, i, o = n_unit(n)
                pe.wait_ge(sem("n_exp"), n + 1)
                if n >= 1:
                    pe.wait_ge(sem("n_pT"), n)
                for j in range(i + 1):
                    ins = tr(bank[5][:, j * P:(j + 1) * P], pbuf[:, n % 2, j * P:(j + 1) * P])
                ins.then_inc(sem("n_tr"), 1)

            def n_pv(n):
                hd, br, i, o = n_unit(n)
                pe.wait_ge(sem("n_pT"), n + 1)
                if n >= 1:
                    pe.wait_ge(sem("n_out"), n)
                vo = (O_S, O_W)[br] + P + o
                for j in range(i + 1):
                    ins = mm(bank[6][:, 0:DH], ptb[:, n % 2, j * P:(j + 1) * P], z[:, j, vo:vo + DH], j == 0, j == i)
                ins.then_inc(sem("n_pv"), 1)

            def page_values(b):
                pe.wait_ge(sem("ring_free7"), 2 * B + 2 * b + 2 + 1)
                for t in range(4):
                    ins = mm(bank[7][:, t * B + b:t * B + b + 1], vsum[:, b % 2, t * P:(t + 1) * P], ones[:, 0:1],
                             False, False, skip_group_check=True)
                ins.then_inc(sem("vsum_mm"), 1)

            def quad_values(b, q):
                pe.wait_ge(sem(f"quad_in{q}"), (b + 1) * 64)
                for j in range(4):
                    w_, c = (slc[:, b, 4 * q + j, :], 64) if q < 4 else (wsc[:, b, j, :], 128)
                    ins = mm(bank[7][:, c + b * H:c + (b + 1) * H], quad[:, q, j, :], w_, False, False, skip_group_check=True)
                ins.then_inc(sem(f"vq_mm{q}"), 1)

            for n in range(8 * H + 2):
                hd, k = n // 8, n % 8
                if n < 8 * H:
                    n_qk(n)
                    if k == 0:
                        sb_qk(hd, 3)
                        sb_qk(hd, 2)
                    if k in (2, 3):
                        sb_qk(hd, 3 - k)
                    if 1 <= k < 5:
                        sb_sum(hd, 4 - k)
                if 1 <= n < 8 * H + 1:
                    n_tr(n - 1)
                if n < 8 * H and 2 <= k < 6:
                    sb_pv(hd, 5 - k)
                if n >= 2:
                    n_pv(n - 2)
                if n < 8 * H:
                    if n == 0:
                        pe.wait_ge(*signal("m_e", 2))
                    if k == 1 and hd:
                        page_values(hd - 1)
                    if k % 2:
                        quad_values(hd, k // 2)
                    if k == 7:
                        quad_values(hd, 4)
            page_values(B - 1)
            pe.wait_ge(sem("n_out"), 64)

            pe.wait_ge(sem("rows_in"), 16 * 6)
            for br in range(2):
                for b in range(B):
                    w_ = slc[0:1, b, NPG, :] if br == 0 else wsc[0:1, b, NW, :]
                    mm(bank[7][:, 64 + 64 * br + b * H:64 + 64 * br + (b + 1) * H], vnew[0:1, br, b, :], w_, False,
                       br == 1 and b == B - 1, skip_group_check=True)
            pe.wait_ge(*signal("s_sp", 1))
            mm(bank[4][:, 0:B * 24], ones[0:1, :], grow[0:1].rearrange("p b h r -> p (b h r)")).then_inc(sem("samples_pe"), 1)
            pe.wait_ge(*signal("v_sq", 1))
            mm(bank[3][:, 0:64], ones, ofs[:, 9, :]).then_inc(sem("samples_pe"), 1)

            pe.wait_ge(sem("mix_ready"), 1)
            for k in range(KD):
                if k >= 2:
                    pe.wait_ge(sem("mixT_ev"), k - 1)
                for t in range(NT):
                    s = (o_sb, o_n)[k // 4][:, t, (k % 4) * P:(k % 4 + 1) * P]
                    ins = tr(bank[k % 2][:, t * P:(t + 1) * P], s)
                ins.then_inc(sem("mixT_mm"), 1)

            pe.wait_ge(sem("mixT_ev"), KD)
            pe.wait_ge(sem("mix_ready"), 2)
            pe.wait_ge(sem("wout_in"), 64)
            for t in range(T5):
                for c in range(2):
                    n = 2 * t + c
                    if n >= 4:
                        pe.wait_ge(sem("res_ev"), n - 3)
                    for k in range(KD):
                        ins = mm(bank[4 + n % 4][0:rows[t], :], hT[:, k, t * P:t * P + rows[t]],
                                 wout[:, k, c * 512:(c + 1) * 512], k == 0, k == KD - 1)
                    ins.then_inc(sem("out_mm"), 1)
            norm_transposes(h2, 1)
            pe.wait_ge(sem("hT_ev"), 18)
            pe.wait_ge(sem("res_ev"), 10)
            with pe.Fori(0, FT // 2) as i:
                for u in range(2):
                    pe.wait_ge(sem(f"up_in{u}"), i * 16 + 16)
                    pe.wait_ge(sem(f"up_ev{u}"), i + 1)
                    for k in range(KD):
                        mm(bank[4 + u][:, 0:HALF], upw[u][:, k, :], hT[:, k, 0:HALF], k == 0, k == KD - 1)
                        ins = mm(bank[6 + u][:, 0:HALF], upw[u][:, k, :], hT[:, k, HALF:TOK], k == 0, k == KD - 1)
                    ins.then_inc(sem(f"up_free{u}"), 1)
            for u in range(2):
                pe.wait_ge(sem(f"a_ready{u}"), FT // 2 + 1)

            def down_products(u, i):
                pe.wait_ge(sem(f"dn_in{u}"), i * 16 + 16)
                pe.wait_ge(sem(f"dn_ev{u}"), i + 1)
                for k in range(FT):
                    mm(bank[u][:, 0:HALF], dnw[u][:, k, :], aT[:, k, 0:HALF], k == 0, k == FT - 1)
                    ins = mm(bank[2 + u][:, 0:HALF], dnw[u][:, k, :], aT[:, k, HALF:TOK], k == 0, k == FT - 1)
                ins.then_inc(sem(f"dn_free{u}"), 1)

            def down_transposes(u, i):
                pe.wait_ge(sem(f"dn_ev{u}"), i + 1 + 1)
                pe.wait_ge(sem(f"y_ev{u}"), i + 1)
                for t in range(NT):
                    tr(bank[4 + u][:, t * P:(t + 1) * P], yT[u][:, t * P:(t + 1) * P])
                tr(bank[6 + u][0:B, 0:P], yT[u][:, SEQ:TOK]).then_inc(sem(f"y_mm{u}"), 1)

            down_products(0, 0)
            with pe.Fori(0, KD // 2 - 1) as i:
                down_products(1, i)
                down_transposes(0, i)
                down_products(0, i + 1)
                down_transposes(1, i)
            down_products(1, KD // 2 - 1)
            down_transposes(0, KD // 2 - 1)
            down_transposes(1, KD // 2 - 1)

        @block.scalar
        def _(act):
            S = nc.scalar
            prime(act, "act")
            chain = Chain(act, sem("act_steps"))

            eps = K("eps")
            act.wait_ge(sem("const_in"), 16)
            act.wait_ge(sem("ss"), 1)
            S.activation(st[:, 8:13], st[:, 0:5], ACT.Sqrt, bias=eps, scale=1.0 / D).then_inc(sem("rt"), 1)
            wb, wo = A["state_nsa_win_kv"][0], O["win_s"][0]
            for b in range(B):
                act.dma_start(wo[b, 0:WIN - 1].rearrange("(o s) k h d -> o (s k h d)", o=1),
                    wb[b, 1:WIN].rearrange("(o s) k h d -> o (s k h d)", o=1)).then_inc(sem("kv_out"), 16)
            with act.Fori(0, 4) as i:
                for u in range(2):
                    for t in (1, 3):
                        act.wait_ge(sem("z_mm"), i * (2 * T5) + u * T5 + t + 1)
                        S.activation(z[:, t, ds(i * (2 * CB) + u * CB, CB)], bank[t][:, 0:CB], ACT.Copy).then_inc(sem(f"z_ev{t}"), 1)
            for t in range(T5):
                act.wait_ge(sem(f"z_ev{t}"), 8 + 1)
            act.dma_start(O["sb_p"][0, 0].rearrange("(t p) k h d -> p t (k h d)", p=P), z[:, 0:NT, O_KS:O_KS + 1024]).then_inc(sem("sb_stored"), 16)
            act.dma_start(O["sb_s"][0].rearrange("b o k h d -> (b o) (k h d)"), z[0:B, NT, O_KS:O_KS + 1024]).then_inc(sem("kv_out"), 16)
            act.wait_ge(sem("rope_done"), T5)
            act.dma_start(O["cmp_p"][0, 0].rearrange("(t p) k h d -> p t (k h d)", p=P), z[:, 0:NT, O_C:O_C + 256]).then_inc(sem("cmp_stored"), 16)
            for nm, o in (("slc_p", O_S), ("win_p", O_W)):
                act.dma_start(O[nm][0, 0].rearrange("(t p) k h d -> p t (k h d)", p=P), z[:, 0:NT, o:o + 256]).then_inc(sem("kv_out"), 16)
            for nm, o in (("cmp_s", O_C), ("slc_s", O_S)):
                act.dma_start(O[nm][0].rearrange("b o k h d -> (b o) (k h d)"), z[0:B, NT, o:o + 256]).then_inc(sem("kv_out"), 16)
            act.dma_start(wo[:, WIN - 1].rearrange("b k h d -> b (k h d)"), z[0:B, NT, O_W:O_W + 256]).then_inc(sem("kv_out"), 16)
            act.wait_ge(sem("qscaled"), 1)
            act.dma_start(sbq_dram, qsc[0:B, :]).then_inc(sem("sbq_out"), 16)
            dst = [sbqT[:, j] for j in range(4)] + [sbkT[:, j] for j in range(4)] + [nqT[:, j] for j in range(4)] + [ksT, kwT]
            for j in range(1, 14, 2):
                act.wait_ge(sem("qkT_mm"), j + 1)
                q = j < 4 or 8 <= j < 12
                S.activation(dst[j], bank[j % 4][:, :], ACT.Copy, scale=SCALE if q else 1.0).then_inc(sem("qkT_ev1"), 1)
            S.activation(z[:, :, O_G:O_G + 24], z[:, :, O_G:O_G + 24], ACT.Exp, scale=-1.0).then_inc(sem("gates_e"), 1)
            act.wait_ge(sem("snew"), 2)
            for br in range(2):
                act.dma_start(newrow[0:1, br].rearrange("p b h -> p (b h)"), snew[0:B, br, :]).then_inc(sem("rows_in"), 16)
            for br, o in enumerate((O_S, O_W)):
                act.dma_start(vnew[0:1, br].rearrange("p b c -> p (b c)"), z[0:B, NT, o + P:o + 2 * P]).then_inc(sem("rows_in"), 16)
            act.wait_ge(sem("gates"), 1)
            act.dma_start(grow[0:1].rearrange("p b h r -> p (b h r)"), z[0:B, NT, O_G:O_G + 24]).then_inc(sem("rows_in"), 16)
            act.dma_start(st[0:1, 208:209], A["g_final"].rearrange("(o d) -> o d", o=1)[:, 0:1]).then_inc(sem("rows_in"), 16)

            act.wait_ge(sem("pebias"), 2)

            def keys_out(i, u, q):
                n = 5 * u + q
                act.wait_ge(sem(f"kq_mm{n % 2}"), i * 5 + n // 2 + 1 + 1)
                act.wait_ge(sem("qs_mm"), i * 10 + n + 1)
                S.activation(kqT.rearrange("p j s -> p (j s)"), bank[6][:, :], ACT.Copy).then_inc(sem("kq_ev"), 1)

            def compress(c, n, between):
                nb = n - 1
                for kv in range(2):
                    for s in range(4):
                        act.wait_ge(sem("xT_mm"), c * 8 + kv * 4 + s + 1)
                        S.activation(xT[kv][:, 2 * s:2 * s + 2, :, 0:n],
                                     bank[s % 2].rearrange("p (m h c) -> p m h c", m=2, h=2)[:, :, :, 0:n],
                                     ACT.Copy).then_inc(sem(f"xT_ev{s % 2}"), 1)
                        if s in (1, 3):
                            between()
                    act.wait_ge(sem(f"hid_mm{kv}"), c + 1)
                    act.wait_ge(sem(f"hid_ready{kv}"), c + 1)
                    S.activation(hid[kv][:, :, 0:nb], bank[2 + kv][:, 0:KVH * nb].rearrange("p (h c) -> p h c", h=KVH),
                                 ACT.Exp, bias=pebias[:, 2 + kv:3 + kv], scale=-1.0).then_inc(sem(f"hid_e{kv}"), 1)

            with act.Fori(0, 4) as i:
                for u in range(2):
                    c = i * 2 + u
                    todo = [lambda q=q: keys_out(i, u, q) for q in range(4)]
                    compress(c, NCH, lambda: todo.pop(0)())
                    keys_out(i, u, 4)
                    act.wait_ge(sem("qs_mm"), i * 10 + 5 * u + 5 + 1)
                    S.activation(slc[:, ds(c, 1), 0:NPG, :].rearrange("p o n j -> p (o n j)"), bank[7][:, 0:NPG * H], ACT.Copy)
                    S.activation(wsc[:, ds(c, 1), 0:NW, :].rearrange("p o n j -> p (o n j)"), bank[7][:, NPG * H:(NPG + NW) * H],
                                 ACT.Copy).then_inc(sem("qs_ev"), 1)
            compress(B, NCP + 1, lambda: None)
            act.wait_ge(sem("kvc_ev0"), B + 1 + 1)
            act.wait_ge(sem("kvc_ev1"), B + 1 + 1)

            def cp_exp(i):
                act.wait_ge(sem("cp_max"), i + 1)
                S.activation(pbuf[:, 0, 0:H * NCP], pbuf[:, 0, 0:H * NCP], ACT.Exp).then_inc(sem("cp_exp"), 1)

            def cp_pT(i):
                for c in range(2):
                    act.wait_ge(sem("cp_tr"), 2 * i + c + 1)
                    if c == 0 and i:
                        act.wait_ge(sem("cp_pv"), i)
                    S.activation(ptb[0:NCP, c, :], bank[6 + c][0:NCP, :], ACT.Copy).then_inc(sem("cp_pT"), 1)

            def samples_exp(br):
                act.wait_ge(*signal("m_sub", br + 1))
                f = (slc, wsc)[br].rearrange("p b n j -> p (b n j)")
                S.activation(f, f, ACT.Exp).then_inc(sem("samples_act"), 1)

            cp_exp(0)
            act.wait_ge(*signal("s_abs", 1))
            f = sps.rearrange("p b n j -> p (b n j)")
            chain(S.activation(f, f, ACT.Exp, scale=-1.0))
            S.activation(f, f, ACT.Ln, bias=K("one")).then_inc(sem("samples_act"), 1)
            act.wait_ge(*signal("c_nm", 1))
            S.activation(s64[0:64, 1, 0:NC], bank[3][0:64, 0:NC], ACT.Exp, bias=st[0:64, 40:41], accum_out=st[0:64, 41:42]).then_inc(sem("samples_act"), 1)
            cp_pT(0)
            cp_exp(1)
            cp_pT(1)
            cp_exp(2)
            cp_pT(2)
            cp_exp(3)
            cp_pT(3)
            samples_exp(0)
            samples_exp(1)
            act.wait_ge(*signal("s_d", 1))
            f = sbs.rearrange("p b n j -> p (b n j)")
            S.activation(f, f, ACT.Exp).then_inc(sem("samples_act"), 1)

            def sb_ln(hd, i):
                m, n = 4 * hd + 3 - i, SEQ - i * P
                act.wait_ge(sem("sb_qk"), m + 1)
                if m >= 2:
                    act.wait_ge(sem("sb_sp"), m - 1)
                e = ebuf[:, m % 2, 0:n]
                chain(S.activation(e, bank[m % 2][:, 0:n], ACT.Abs))
                chain(S.activation(e, e, ACT.Exp, scale=-1.0))
                S.activation(e, e, ACT.Ln, bias=K("one")).then_inc(sem("sb_ln"), 1)

            def sb_exp(hd, i):
                m, n = 4 * hd + 3 - i, SEQ - i * P
                act.wait_ge(sem("sb_c"), m + 1)
                if m >= 2:
                    act.wait_ge(sem("sb_pv"), m - 1)
                S.activation(abuf[:, m % 2, 0:n], bank[m % 2][:, 0:n], ACT.Exp).then_inc(sem("sb_a"), 1)

            def n_exp(n):
                i = n % 4
                act.wait_ge(sem("n_max"), n + 1)
                if n >= 2:
                    act.wait_ge(sem("n_tr"), n - 1)
                if n >= 4:
                    act.wait_ge(sem("n_out"), n - 3)
                S.activation(pbuf[:, n % 2, 0:(i + 1) * P], bank[3 + n % 2][:, 0:(i + 1) * P], ACT.Exp,
                             bias=st[:, 160 + n % 4:161 + n % 4], accum_out=st[:, 164 + n % 4:165 + n % 4]).then_inc(sem("n_exp"), 1)

            def n_pT(n):
                i = n % 4
                act.wait_ge(sem("n_tr"), n + 1)
                if n >= 2:
                    act.wait_ge(sem("n_pv"), n - 1)
                S.activation(ptb[:, n % 2, 0:(i + 1) * P], bank[5][:, 0:(i + 1) * P], ACT.Copy).then_inc(sem("n_pT"), 1)

            act.wait_ge(sem("cp_pv"), NT)
            S.preload_act_table_set("natural_log_exp_and_others")
            for n in range(8 * H + 1):
                hd, k = n // 8, n % 8
                if n < 8 * H:
                    if k == 0:
                        sb_ln(hd, 3)
                    n_exp(n)
                    if k == 0:
                        sb_ln(hd, 2)
                    if k in (2, 3):
                        sb_ln(hd, 3 - k)
                    if 1 <= k < 5:
                        sb_exp(hd, 4 - k)
                if n >= 1:
                    n_pT(n - 1)
                if k == 6:
                    act.wait_ge(sem("sb_pv"), 4 * hd + 4)
                    S.activation(o_sb[:, :, hd * DH:(hd + 1) * DH], bank[2][:, 0:256].rearrange("p (t d) -> p t d", t=NT), ACT.Copy).then_inc(sem("sb_out"), 1)

            act.wait_ge(*signal("v_st", 1))
            S.activation(st[:, 64:80], st[:, 48:64], ACT.Sqrt, bias=eps, scale=1.0 / 512).then_inc(sem("samples_act"), 1)
            act.wait_ge(*signal("mix_ss", 1))
            S.activation(st[:, 96:104], st[:, 88:96], ACT.Sqrt, bias=eps, scale=1.0 / 512).then_inc(sem("samples_act"), 1)
            act.wait_ge(sem("ss"), 2)
            S.activation(st[:, 8:12], st[:, 0:4], ACT.Sqrt, bias=eps, scale=1.0 / D).then_inc(sem("rt"), 1)
            act.wait_ge(sem("ss"), 3)
            S.activation(st[0:B, 12:13], st[0:B, 4:5], ACT.Sqrt, bias=eps[0:B], scale=1.0 / D).then_inc(sem("rt"), 1)
            act.wait_ge(sem("hT_ev"), 18)
            with act.Fori(0, FT // 2) as i:
                for u in range(2):
                    act.wait_ge(sem(f"up_free{u}"), i + 1 + 1)
                    act.wait_ge(sem(f"a_ready{u}"), i + 1)
                    S.activation(h2[:, u, 0:HALF], bank[4 + u][:, 0:HALF], ACT.Relu)
                    S.activation(h2[:, u, HALF:TOK], bank[6 + u][:, 0:HALF], ACT.Relu).then_inc(sem(f"up_ev{u}"), 1)
            act.wait_ge(sem("ss"), 4)
            S.activation(st[:, 8:13], st[:, 0:5], ACT.Sqrt, bias=eps, scale=1.0 / D).then_inc(sem("rt"), 1)
            act.wait_ge(sem("kv_out"), 16 * (B + 6))
            act.wait_ge(sem("cmp_stored"), 16)
            act.wait_ge(sem("sbq_out"), 16)

        @block.vector
        def _(dve):
            V = nc.vector
            prime(dve, "dve")
            chain = Chain(dve, sem("dve_steps"))

            def squares(dst, t, after):
                ins = V.tensor_tensor_reduce(dst[0:rows[t], t, :], x[0:rows[t], t, :], x[0:rows[t], t, :], 1.0, 0.0,
                                             ALU.mult, ALU.add, st[0:rows[t], t:t + 1])
                after(ins)

            def row_scales(dst, tiles, turn):
                lo, hi = tiles[0], tiles[-1] + 1
                dve.wait_ge(sem("rt"), turn)
                chain(V.reciprocal(st[:, 16 + lo:16 + hi], st[:, 8 + lo:8 + hi]))
                for t in tiles:
                    ins = V.tensor_scalar(dst[0:rows[t], t, :], x[0:rows[t], t, :], st[0:rows[t], 16 + t:17 + t], None, ALU.mult)
                    if t < hi - 1:
                        chain(ins)
                return ins

            def gained(g0, turn):
                for k in range(KD):
                    dve.wait_ge(sem("hT_mm"), 9 * turn + k + 1)
                    V.tensor_scalar(hT[:, k, 0:SEQ], bank[k % 2][:, :], vcol[:, g0 + k:g0 + k + 1], None, ALU.mult).then_inc(sem("hT_ev"), 1)

            def gained_samples(g0, turn):
                dve.wait_ge(sem("hT_mm"), 9 * turn + 9)
                V.tensor_tensor(hT[:, :, SEQ:TOK], bank[2][:, 0:64].rearrange("p (k b) -> p k b", k=KD),
                                over(vcol[:, g0:g0 + KD], 2, B), ALU.mult).then_inc(sem("hT_ev"), 1)

            chain(V.memset(st[:, :], 1.0))
            chain(V.memset(zero[:, :], 0.0))
            dve.wait_ge(sem("x_in"), 32)
            for t in range(NT):
                squares(h, t, chain)
            squares(h, NT, lambda ins: ins.then_inc(sem("ss"), 1))
            row_scales(h, range(NT), 1).then_inc(sem("h_ready"), 1)
            row_scales(h, [NT], 1).then_inc(sem("h_ready"), 1)
            dve.wait_ge(sem("vcol_mm"), 1)
            V.tensor_copy(vcol[:, :], bank[3][:, 0:56]).then_inc(sem("vcol_ev"), 1)
            dve.wait_ge(sem("vcol_ev"), 1)
            gained(0, 0)
            gained_samples(0, 0)
            dve.wait_ge(sem("z_zero"), 1)
            with dve.Fori(0, 4) as i:
                for u in range(2):
                    for t in (0, 2, 4):
                        dve.wait_ge(sem("z_mm"), i * (2 * T5) + u * T5 + t + 1)
                        V.tensor_copy(z[0:rows[t], t, ds(i * (2 * CB) + u * CB, CB)], bank[t][0:rows[t], 0:CB]).then_inc(sem(f"z_ev{t}"), 1)
                    dve.wait_ge(sem(f"z_ev4"), i * 2 + u + 1 + 1)
                    V.memset(st[0:1, 202:203], 0.0).then_inc(sem(f"win_free{u}"), 1)
            for t in range(T5):
                dve.wait_ge(sem(f"z_ev{t}"), 8 + 1)
            chain(V.memset(qbd[:, :, :], 0.0))
            for t in range(T5):
                cos, sin = (K(n)[:, t * DH:(t + 1) * DH] for n in ("cos", "sin"))
                qn = z[:, t, O_QN:O_QN + 512].rearrange("p (h d) -> p h d", h=H)
                kk = z[:, t, O_C:O_C + 768].rearrange("p (r k h d) -> p r k h d", r=3, k=2, h=2)[:, :, 0]
                a8, b8 = (v.rearrange("p (h d) -> p h d", h=H) for v in (ropeA, ropeB))
                a6, b6 = (v[:, 0:384].rearrange("p (r h d) -> p r h d", r=3, h=2) for v in (ropeA, ropeB))
                chain(V.tensor_tensor(a8, qn, over(cos, 1, H), ALU.mult))
                chain(V.tensor_tensor(b8[:, :, 0:32], qn[:, :, 32:64], over(sin[:, 0:32], 1, H), ALU.mult))
                chain(V.tensor_tensor(b8[:, :, 32:64], qn[:, :, 0:32], over(sin[:, 32:64], 1, H), ALU.mult))
                qp = z[:, t, O_QN:O_QN + 512].rearrange("p (g k d) -> p k g d", g=G, k=KVH)
                chain(V.tensor_tensor(qp, *(v.rearrange("p (k g) d -> p k g d", k=KVH) for v in (a8, b8)), ALU.add))
                cos6, sin6 = over(over(cos, 1, 2), 1, 3), over(over(sin, 1, 2), 1, 3)
                chain(V.tensor_tensor(a6, kk, cos6, ALU.mult))
                chain(V.tensor_tensor(b6[:, :, :, 0:32], kk[:, :, :, 32:64], sin6[:, :, :, 0:32], ALU.mult))
                chain(V.tensor_tensor(b6[:, :, :, 32:64], kk[:, :, :, 0:32], sin6[:, :, :, 32:64], ALU.mult))
                V.tensor_tensor(kk, a6, b6, ALU.add).then_inc(sem("rope_done"), 1)
                dve.wait_ge(sem("rope_done"), t + 1)
            dve.wait_ge(sem("rope_done"), T5)
            zs = z[0:B, NT]
            chain(V.tensor_scalar(qsc[0:B, :], zs[:, O_QS:O_QS + 512], SCALE, None, ALU.mult))
            V.memset(st[0:1, 204:205], 0.0).then_inc(sem("qscaled"), 1)
            for j in range(0, 14, 2):
                dve.wait_ge(sem("qkT_mm"), j + 1)
                q = j < 4 or 8 <= j < 12
                dst = ([sbqT[:, n] for n in range(4)] + [sbkT[:, n] for n in range(4)] + [nqT[:, n] for n in range(4)] + [ksT, kwT])[j]
                if q:
                    ins = V.tensor_scalar(dst, bank[j % 4][:, :], SCALE, None, ALU.mult)
                else:
                    ins = V.tensor_copy(dst, bank[j % 4][:, :])
                ins.then_inc(sem("qkT_ev0"), 1)
            dve.wait_ge(sem("qkT_mm"), 15)
            for kh in range(2):
                lo = kh * DH
                ins = V.tensor_scalar(qbd[lo:lo + DH, :, kh * G:(kh + 1) * G],
                                      bank[4][lo:lo + DH, 0:32].rearrange("p (g b) -> p b g", g=G), SCALE, None, ALU.mult)
                if kh == 0:
                    chain(ins)
            ins.then_inc(sem("qkT_ev0"), 1)
            for br, o in enumerate((O_S, O_W)):
                qn = zs[:, O_QN:O_QN + 512].rearrange("p (g k d) -> p k g d", k=2, g=G)
                kn = over(zs[:, o:o + P].rearrange("p (k d) -> p k d", k=2), 2, G)
                chain(V.tensor_tensor(ropeA[0:B].rearrange("p (k g d) -> p k g d", k=2, g=G), qn, kn, ALU.mult))
                chain(V.tensor_reduce(ropeB[0:B, 0:H], ropeA[0:B].rearrange("p (h d) -> p h d", h=H), AX.X, ALU.add))
                V.tensor_scalar(snew[0:B, br, :], ropeB[0:B, 0:H], SCALE, None, ALU.mult).then_inc(sem("snew"), 1)
                dve.wait_ge(sem("snew"), br + 1)
            dve.wait_ge(sem("gates_e"), 1)
            g = z[:, :, O_G:O_G + 24]
            chain(V.tensor_scalar(g, g, 1.0, None, ALU.add))
            V.reciprocal(g, g).then_inc(sem("gates"), 1)
            dve.wait_ge(sem("pe_mm"), 1)
            V.tensor_copy(pebias[:, 0:2], bank[6][:, 0:2]).then_inc(sem("pebias"), 1)
            V.tensor_scalar(pebias[:, 2:4], bank[6][:, 0:2], -1.0, None, ALU.mult).then_inc(sem("pebias"), 1)
            dve.wait_ge(sem("pebias"), 2)
            dve.wait_ge(sem("gates"), 1)

            def silu(c, kv, n):
                nb = n - 1
                dve.wait_ge(sem(f"hid_e{kv}"), c + 1)
                e = hid[kv][:, :, 0:nb]
                chain(V.tensor_scalar(e, e, 1.0, None, ALU.add))
                chain(V.reciprocal(e, e))
                dve.wait_ge(sem(f"w2_mm{kv}"), c + 1)
                hp = bank[2 + kv][:, 0:KVH * nb].rearrange("p (h c) -> p h c", h=KVH)
                V.scalar_tensor_tensor(out=hid[2 + kv][:, :, 0:nb], in0=hp, scalar=pebias[:, kv:kv + 1], in1=e,
                                       op0=ALU.add, op1=ALU.mult).then_inc(sem(f"hid_ready{kv}"), 1)

            def compressed_out(c, dst_k, dst_v, n):
                dve.wait_ge(sem("w2_mm0"), c + 1 + 1)
                V.tensor_copy(dst_k, bank[4][:, 0:n - 1]).then_inc(sem("kvc_ev0"), 1)
                dve.wait_ge(sem("w2_mm1"), c + 1 + 1)
                V.tensor_copy(dst_v, bank[5][0:n - 1, 0:P]).then_inc(sem("kvc_ev1"), 1)

            def sb_keys(i, u, first, last):
                if first == 0:
                    dve.wait_ge(sem(f"qb_in{u}"), i * 16 + 16)
                for p in range(first, last):
                    k = kring[p % 8]
                    dve.wait_ge(sem(f"ring_in{p % 8}"), (i * 4 + (2 * u + p // 8 + 1)) * 16)
                    if p < NPG - 1:
                        chain(V.tensor_tensor(k, k, qb[:, u, :], ALU.mult))
                    else:
                        V.tensor_tensor(k, k, qb[:, u, :], ALU.mult).then_inc(sem(f"qb_free{u}"), 1)
                        dve.wait_ge(sem(f"qb_free{u}"), i + 1 + 1)
                    V.tensor_reduce(raw_scores(ds(i, 1), u)[:, p, :], k.rearrange("p (h d) -> p h d", h=H),
                                    AX.X, ALU.add).then_inc(sem(f"ring_free{p % 8}"), 1)

            dve.wait_ge(sem("cmp_stored"), 16)
            with Turns(chain, 4, 2 * (NPG - 1 + 4)) as i:
                for u in range(2):
                    c = i * 2 + u
                    sb_keys(i, u, 0, 8)
                    silu(c, 0, NCH)
                    sb_keys(i, u, 8, 14)
                    silu(c, 1, NCH)
                    sb_keys(i, u, 14, 16)
                    compressed_out(c, kc[:, ds(c, 1), 0:NC].rearrange("p o c -> p (o c)"), vc[0:NC, ds(c, 1), :].rearrange("p o c -> p (o c)"), NCH)
            silu(B, 0, NCP + 1)
            silu(B, 1, NCP + 1)
            compressed_out(B, kc[:, B, 0:NCP], vc[0:NCP, B, :], NCP + 1)
            for k in range(8):
                dve.wait_ge(sem(f"ring_free{k}"), 2 * B + 1)

            dve.wait_ge(sem("kvc_ev0"), B + 1 + 1)
            dve.wait_ge(sem("kvc_ev1"), B + 1 + 1)
            dve.wait_ge(sem("qs_ev"), B + 1)
            pc = pbuf[:, 0, 0:H * NCP].rearrange("p (h c) -> p h c", h=H)

            def cp_max(i):
                dve.wait_ge(sem("cp_qk"), i + 1)
                if i:
                    dve.wait_ge(sem("cp_tr"), 2 * i)
                add = over(K("cadd")[:, i * NCP:(i + 1) * NCP], 1, H)
                for kh in range(KVH):
                    hs = slice(G * kh, G * kh + G)
                    chain(V.tensor_tensor(pc[:, hs], bank[4 + kh][:, 0:G * NCP].rearrange("p (h c) -> p h c", h=G), add[:, hs], ALU.add))
                chain(V.tensor_reduce(st[:, 104:112], pc, AX.X, ALU.max))
                V.tensor_tensor(pc, pc, over(st[:, 104:112], 2, NCP), ALU.subtract).then_inc(sem("cp_max"), 1)

            def cp_soft(i):
                dve.wait_ge(sem("cp_exp"), i + 1)
                mul = over(K("cmul")[:, i * NCP:(i + 1) * NCP], 1, H)
                chain(V.tensor_tensor(pc, pc, mul, ALU.mult))
                chain(V.tensor_reduce(st[:, 112:120], pc, AX.X, ALU.add))
                chain(V.tensor_scalar(st[:, 112:120], st[:, 112:120], TINY, None, ALU.max))
                chain(V.reciprocal(st[:, 120:128], st[:, 112:120]))
                gate = z[:, i, O_G:O_G + 24].rearrange("p (h r) -> p h r", r=3)[:, :, 0]
                chain(V.tensor_tensor(st[:, 120:128], st[:, 120:128], gate, ALU.mult))
                V.tensor_tensor(pc, pc, over(st[:, 120:128], 2, NCP), ALU.mult).then_inc(sem("cp_soft"), 1)

            def cp_out(i):
                dve.wait_ge(sem("cp_pv"), i + 1)
                V.tensor_copy(o_n[:, i, :], bank[i % 2][:, :]).then_inc(sem("cp_out"), 1)

            def row_max(br):
                sc = (slc, wsc)[br]
                V.tensor_reduce(s64[:, 0, 0:64].rearrange("p (b j) -> p b j", b=B), sc.rearrange("p b n j -> p b j n"), AX.X, ALU.max).then_inc(sem("samples_dve"), 1)

            def row_max_diagonal(br):
                dve.wait_ge(*signal("m_T", br + 1))
                chain(V.tensor_reduce(st[0:64, 44:45], bank[2][0:64, 0:P], AX.X, ALU.max))
                V.tensor_scalar(s64[0:64, 1, 0:64], ident[0:64, 0:64], st[0:64, 44:45], None, ALU.mult).then_inc(sem("samples_dve"), 1)

            def row_max_subtract(br):
                sc, n = ((slc, NPG + 1), (wsc, NW + 1))[br]
                dve.wait_ge(*signal("m_b", br + 1))
                chain(V.tensor_copy(s64[:, 2, 0:64], bank[3][:, 0:64]))
                V.tensor_tensor(sc, sc, over(s64[:, 2, 0:64].rearrange("p (b j) -> p b j", b=B), 2, n), ALU.subtract).then_inc(sem("samples_dve"), 1)

            def row_sum(br):
                sc = (slc, wsc)[br]
                dve.wait_ge(*signal("m_e", br + 1))
                V.tensor_reduce(s64[:, 3, 0:64].rearrange("p (b j) -> p b j", b=B), sc.rearrange("p b n j -> p b j n"), AX.X, ALU.add).then_inc(sem("samples_dve"), 1)

            def row_reciprocal(br):
                dve.wait_ge(*signal("m_den", br + 1))
                V.reciprocal(ofs[:, 5 + br, :], bank[2][:, 0:64]).then_inc(sem("samples_dve"), 1)

            dve.wait_ge(*signal("c_sc", 1))
            V.tensor_copy(s64[0:NC, 0, 0:64], bank[2][0:NC, 0:64]).then_inc(sem("samples_dve"), 1)
            cp_max(0)
            flat = lambda a: a.rearrange("p b n j -> p (b n j)")
            raw = z[:, 0:NT, O_C:O_C + 256]
            chain(V.tensor_copy(flat(sbs).rearrange("p (t c) -> p t c", t=NT), raw))
            V.scalar_tensor_tensor(out=flat(sps), in0=flat(sbs), scalar=-1.0, in1=flat(sbs), op0=ALU.mult, op1=ALU.max).then_inc(sem("samples_dve"), 1)
            dve.wait_ge(*signal("c_scT", 1))
            V.tensor_reduce(st[0:64, 40:41], bank[3][0:64, 0:NC], AX.X, ALU.max, negate=True).then_inc(sem("samples_dve"), 1)
            cp_soft(0)
            dve.wait_ge(*signal("c_e", 1))
            chain(V.tensor_scalar(st[0:64, 41:42], st[0:64, 41:42], TINY, None, ALU.max))
            chain(V.reciprocal(st[0:64, 42:43], st[0:64, 41:42]))
            V.tensor_scalar(s64[0:64, 2, 0:NC], s64[0:64, 1, 0:NC], st[0:64, 42:43], None, ALU.mult).then_inc(sem("samples_dve"), 1)
            dve.wait_ge(*signal("s_ln", 1))
            V.scalar_tensor_tensor(out=flat(sps), in0=flat(sbs), scalar=0.0, in1=flat(sps), op0=ALU.max, op1=ALU.add).then_inc(sem("samples_dve"), 1)
            dve.wait_ge(*signal("c_pT", 1))
            chain(V.tensor_copy(pcT[0:NC, :], bank[2][0:NC, 0:64]))
            V.tensor_reduce(s64[0:NC, 3, 0:16], pcT[0:NC, :].rearrange("p (k g) -> p k g", g=G), AX.X, ALU.add).then_inc(sem("samples_dve"), 1)
            cp_out(0)
            cp_max(1)
            dve.wait_ge(*signal("c_imp", 1))
            imp = s64[0:16, 4, 0:NSEL]
            chain(V.tensor_copy(imp, bank[3][0:16, 0:NSEL]))
            chain(V.memset(imp[:, 0:1], FORCE))
            chain(V.memset(imp[:, NSEL - 2:NSEL], FORCE))
            im_i, im_j = over(imp, 1, NSEL), over(imp, 2, NSEL)
            chain(V.tensor_tensor(rankA[0:16], im_i, im_j, ALU.is_gt))
            chain(V.tensor_tensor(rankB[0:16], im_i, im_j, ALU.is_equal))
            chain(V.tensor_tensor(rankB[0:16], rankB[0:16], K("lower")[0:16].rearrange("p (j i) -> p j i", j=NSEL), ALU.mult))
            chain(V.tensor_tensor(rankA[0:16], rankA[0:16], rankB[0:16], ALU.add))
            chain(V.tensor_reduce(s64[0:16, 6, 0:NSEL], rankA[0:16], AX.X, ALU.add))
            V.tensor_scalar(s64[0:16, 5, 0:NSEL], s64[0:16, 6, 0:NSEL], float(TOPN), None, ALU.is_lt).then_inc(sem("samples_dve"), 1)
            cp_soft(1)
            dve.wait_ge(*signal("s_sp", 1))
            chain(V.memset(suf[:, :, NPG - 1, :], 0.0))
            for n in range(NPG - 2, -1, -1):
                ins = V.tensor_tensor(suf[:, :, n, :], suf[:, :, n + 1, :], sps[:, :, n + 1, :], ALU.add)
                if n:
                    chain(ins)
            ins.then_inc(sem("samples_dve"), 1)
            cp_out(1)
            cp_max(2)
            dve.wait_ge(*signal("c_selT", 1))
            V.tensor_tensor(selx[0:NSEL], over(bank[2][0:NSEL, 0:16], 1, NPG + 1),
                                 K("pagemap")[0:NSEL].rearrange("p (n k) -> p n k", k=16), ALU.mult).then_inc(sem("samples_dve"), 1)
            dve.wait_ge(sem("rows_in"), 96)
            chain(V.memset(slc[:, :, NPG, :], NEG))
            chain(V.memset(wsc[:, :, NW, :], NEG))
            chain(V.tensor_copy(slc[0:1, :, NPG, :], newrow[0:1, 0]))
            chain(V.tensor_copy(wsc[0:1, :, NW, :], newrow[0:1, 1]))
            chain(V.memset(wsc[0:1, :, 0, :], NEG))
            cp_soft(2)
            cp_out(2)
            dve.wait_ge(*signal("c_mask", 1))
            V.tensor_scalar(selm.rearrange("p n k -> p (n k)"), bank[3][:, 0:272], -1.0, -NEG, ALU.add, ALU.mult).then_inc(sem("samples_dve"), 1)
            dve.wait_ge(*signal("c_selm", 1))
            for b in range(B):
                v = slc[:, b].rearrange("p n (k g) -> p n k g", k=2)
                chain(V.tensor_tensor(v, v, over(selm[:, :, 2 * b:2 * b + 2], 3, G), ALU.add))
            cp_max(3)
            row_max(0)
            row_max_diagonal(0)
            cp_soft(3)
            row_max_subtract(0)
            cp_out(3)
            row_sum(0)
            row_reciprocal(0)
            row_max(1)
            row_max_diagonal(1)
            row_max_subtract(1)
            row_sum(1)
            row_reciprocal(1)
            dve.wait_ge(*signal("s_c", 1))
            for c in range(2):
                f = sbs[:, 4 * c:4 * c + 4].rearrange("p b n j -> p (b n j)")
                ins = V.tensor_tensor(f, f, bank[2 + c][:, :], ALU.add)
                if c == 0:
                    chain(ins)
            ins.then_inc(sem("samples_dve"), 1)
            dve.wait_ge(sem("cp_tr"), 2 * NT)

            def sb_soft(hd, i):
                m, n = 4 * hd + 3 - i, SEQ - i * P
                dve.wait_ge(sem("sb_ln"), m + 1)
                if m >= 2:
                    dve.wait_ge(sem("sb_c"), m - 1)
                    dve.wait_ge(sem("sb_run"), m - 1)
                s = spb[:, m % 2]
                chain(V.scalar_tensor_tensor(out=s[:, 0:n], in0=bank[m % 2][:, 0:n], scalar=0.0, in1=ebuf[:, m % 2, 0:n],
                                             op0=ALU.max, op1=ALU.add))
                V.tensor_tensor(s[:, 0:P], s[:, 0:P], K("before"), ALU.mult).then_inc(sem("sb_sp"), 1)

            def sb_amask(hd, i):
                m = 4 * hd + 3 - i
                dve.wait_ge(sem("sb_a"), m + 1)
                V.tensor_tensor(abuf[:, m % 2, 0:P], abuf[:, m % 2, 0:P], K("before"), ALU.mult).then_inc(sem("sb_am"), 1)

            def n_max(n):
                i = n % 4
                dve.wait_ge(sem("n_qk"), n + 1)
                if n >= 2:
                    dve.wait_ge(sem("n_exp"), n - 1)
                pb = bank[3 + n % 2]
                chain(V.tensor_tensor(pb[:, i * P:(i + 1) * P], pb[:, i * P:(i + 1) * P], K("causal"), ALU.add))
                V.tensor_reduce(st[:, 160 + n % 4:161 + n % 4], pb[:, 0:(i + 1) * P], AX.X, ALU.max, negate=True).then_inc(sem("n_max"), 1)

            def n_out(n):
                hd, br, i = n // 8, (n // 4) % 2, n % 4
                dve.wait_ge(sem("n_pv"), n + 1)
                c = 168 + n % 4
                chain(V.reciprocal(st[:, c:c + 1], st[:, c - 4:c - 3]))
                gate = z[:, i, O_G + 3 * hd + 1 + br:O_G + 3 * hd + 2 + br]
                chain(V.tensor_tensor(st[:, c:c + 1], st[:, c:c + 1], gate, ALU.mult))
                o = o_n[:, i, place(hd) * DH:(place(hd) + 1) * DH]
                V.scalar_tensor_tensor(out=o, in0=bank[6][:, 0:DH], scalar=st[:, c:c + 1], in1=o, op0=ALU.mult, op1=ALU.add).then_inc(sem("n_out"), 1)
                dve.wait_ge(sem("n_out"), n + 1)

            def page_values(b, n):
                u, r = n % 8, n // 8
                dve.wait_ge(sem(f"ring_in{u}"), (2 * B + 2 * b + r + 1) * 16)
                if n == 0 and b >= 2:
                    dve.wait_ge(sem("vsum_mm"), b - 1)
                if n == 0 and b == 0:
                    dve.wait_ge(*signal("s_a", 1))
                page = ring[:, u, :]
                V.tensor_tensor((page if n else vsum[:, b % 2, :]).rearrange("p (h d) -> p h d", h=H),
                                page.rearrange("p (h d) -> p h d", h=H), over(sbs[:, b, n, :], 2, DH), ALU.mult
                                ).then_inc(sem("weighted" if n else "ring_free0"), 1)

            for n in range(8 * H + 2):
                hd, k = n // 8, n % 8
                if n < 8 * H:
                    if k == 0:
                        sb_soft(hd, 3)
                    n_max(n)
                    if k == 0:
                        sb_soft(hd, 2)
                    if k in (2, 3):
                        sb_soft(hd, 3 - k)
                    if 1 <= k < 5:
                        sb_amask(hd, 4 - k)
                    page_values(hd, 2 * k)
                    page_values(hd, 2 * k + 1)
                if n >= 2:
                    n_out(n - 2)

            dve.wait_ge(sem("sb_out"), H)
            dve.wait_ge(sem("sb_run"), 4 * H)
            dve.wait_ge(sem("sb_pv"), 4 * H)
            V.memset(st[0:1, 211:212], 0.0).then_inc(sem("samples_dve"), 1)
            dve.wait_ge(*signal("v_mm", 1))
            gb = ofs[:, 0:3, :].rearrange("p a b -> p (a b)")
            chain(V.tensor_copy(gb, bank[4][:, 0:192]))
            g3 = gb.rearrange("p (c r) -> p c r", r=3)
            acc, tmp = ofs[:, 3, :], ofs[:, 4, :]
            chain(V.tensor_tensor(acc, bank[7][:, 192:256], g3[:, :, 0], ALU.mult))
            for br in range(2):
                chain(V.tensor_tensor(tmp, bank[7][:, 64 + 64 * br:128 + 64 * br], ofs[:, 5 + br, :], ALU.mult))
                chain(V.tensor_tensor(tmp, tmp, g3[:, :, 1 + br], ALU.mult))
                chain(V.tensor_tensor(acc, acc, tmp, ALU.add))
            mx = ofs[:, 8, :].rearrange("p (k b) -> p k b", k=KD)
            a3 = acc.rearrange("p (b j) -> p b j", b=B)
            chain(V.tensor_copy(mx[:, 0:4, :], bank[7][:, 0:4 * B].rearrange("p (t b) -> p t b", t=4)))
            for kh in range(2):
                lo = kh * DH
                chain(V.tensor_copy(mx[lo:lo + DH, 4:8, :], a3[lo:lo + DH, :, kh * G:(kh + 1) * G].rearrange("p b g -> p g b")))
            V.tensor_tensor(ofs[:, 9, :], ofs[:, 8, :], ofs[:, 8, :], ALU.mult).then_inc(sem("samples_dve"), 1)
            dve.wait_ge(*signal("v_ss", 1))
            V.tensor_reduce(st[:, 48:64].rearrange("p (a b) -> p a b", a=2), bank[3][:, 0:64].rearrange("p (a t b) -> p a b t", a=2, t=4), AX.X, ALU.add).then_inc(sem("samples_dve"), 1)
            dve.wait_ge(*signal("v_rt", 1))
            chain(V.reciprocal(st[:, 128:144], st[:, 64:80]))
            for a in range(2):
                v = mx[:, 4 * a:4 * a + 4, :]
                chain(V.tensor_tensor(v, v, over(st[:, 128 + 8 * a:136 + 8 * a], 1, 4), ALU.mult))
            chain(V.tensor_tensor(hT[:, :, SEQ:TOK], mx, over(vcol[:, 16:24], 2, B), ALU.mult))
            for a, o in enumerate((o_sb, o_n)):
                for t in range(NT):
                    chain(V.tensor_tensor_reduce(pbuf[:, 0, :], o[:, t, :], o[:, t, :], 1.0, 0.0,
                                                 ALU.mult, ALU.add, st[:, 88 + 4 * a + t:89 + 4 * a + t]))
            V.memset(st[0:1, 213:214], 0.0).then_inc(sem("samples_dve"), 1)
            dve.wait_ge(*signal("mix_rt", 1))
            chain(V.reciprocal(st[:, 144:152], st[:, 96:104]))
            for a, o in enumerate((o_sb, o_n)):
                for t in range(NT):
                    ins = V.tensor_scalar(o[:, t, :], o[:, t, :], st[:, 144 + 4 * a + t:145 + 4 * a + t], None, ALU.mult)
                    if 4 * a + t < 7:
                        chain(ins)
            ins.then_inc(sem("mix_ready"), 1)
            for k in range(KD):
                dve.wait_ge(sem("mixT_mm"), k + 1)
                V.tensor_scalar(hT[:, k, 0:SEQ], bank[k % 2][:, :], vcol[:, 16 + k:17 + k], None, ALU.mult).then_inc(sem("mixT_ev"), 1)
            dve.wait_ge(sem("mixT_ev"), KD)
            V.memset(st[0:1, 214:215], 0.0).then_inc(sem("mix_ready"), 1)
            dve.wait_ge(sem("x2_in"), 32)
            for n in range(2 * T5):
                t, c = n // 2, n % 2
                dve.wait_ge(sem("out_mm"), n + 1)
                xv = x[0:rows[t], t, c * 512:(c + 1) * 512]
                V.tensor_tensor(xv, xv, bank[4 + n % 4][0:rows[t], :], ALU.add).then_inc(sem("res_ev"), 1)
                if c == 1:
                    dve.wait_ge(sem("res_ev"), n + 1)
                    squares(h2, t, chain if t < NT - 1 else lambda ins: ins.then_inc(sem("ss"), 1))
                    if t == NT - 1:
                        row_scales(h2, range(NT), 2).then_inc(sem("h_ready"), 1)
            gained(8, 1)
            row_scales(h2, [NT], 3).then_inc(sem("h_ready"), 1)
            gained_samples(8, 1)
            dve.wait_ge(sem("hT_ev"), 18)
            with dve.Fori(0, FT // 2) as i:
                for u in range(2):
                    dve.wait_ge(sem(f"up_ev{u}"), i + 1 + 1)
                    a = aT[:, ds(i * 2 + u, 1), :].rearrange("p o c -> p (o c)")
                    V.tensor_tensor(a, h2[:, u, 0:TOK], h2[:, u, 0:TOK], ALU.mult).then_inc(sem(f"a_ready{u}"), 1)
            for u in range(2):
                dve.wait_ge(sem(f"a_ready{u}"), FT // 2 + 1)

            def down_out(u, i):
                dve.wait_ge(sem(f"dn_free{u}"), i + 1 + 1)
                dve.wait_ge(sem(f"y_mm{u}"), i + 1)
                V.tensor_copy(yT[u][:, 0:HALF], bank[u][:, 0:HALF])
                V.tensor_copy(yT[u][:, HALF:TOK], bank[2 + u][:, 0:HALF]).then_inc(sem(f"dn_ev{u}"), 1)

            def down_residual(u, i):
                dve.wait_ge(sem(f"y_mm{u}"), i + 1 + 1)
                xv = x[:, 0:NT, ds(i * (2 * P) + u * P, P)]
                V.tensor_tensor(xv, xv, bank[4 + u].rearrange("p (t c) -> p t c", t=NT), ALU.add)
                xv = x[0:B, NT, ds(i * (2 * P) + u * P, P)]
                V.tensor_tensor(xv, xv, bank[6 + u][0:B, 0:P], ALU.add).then_inc(sem(f"y_ev{u}"), 1)

            down_out(0, 0)
            with dve.Fori(0, KD // 2 - 1) as i:
                down_out(1, i)
                down_residual(0, i)
                down_out(0, i + 1)
                down_residual(1, i)
            down_out(1, KD // 2 - 1)
            down_residual(0, KD // 2 - 1)
            down_residual(1, KD // 2 - 1)
            for u in range(2):
                dve.wait_ge(sem(f"y_ev{u}"), KD // 2 + 1)
            for t in range(NT):
                squares(h2, t, chain)
            squares(h2, NT, lambda ins: ins.then_inc(sem("ss"), 1))
            chain(row_scales(h2, range(T5), 4))
            dve.wait_ge(sem("gfin_in"), 16)
            for t in range(T5):
                ins = V.tensor_tensor(h2[0:rows[t], t, :], h2[0:rows[t], t, :], gfin[0:rows[t], :], ALU.mult)
                if t < T5 - 1:
                    chain(ins)
            ins.then_inc(sem("y_ready"), 1)

        @block.gpsimd
        def _(pool):
            G_ = nc.gpsimd
            prime(pool, "pool")

            G_.memset(z[:, NT, :], 0.0).then_inc(sem("z_zero"), 1)
            pool.wait_ge(sem("qkT_mm"), 15)
            pool.wait_ge(sem("sb_stored"), 16)

            def permute(c, u, n):
                for kv in range(2):
                    if c:
                        pool.wait_ge(sem(f"hid_mm{kv}"), c)
                    for hh in range(KVH):
                        ins = G_.tensor_copy(per(kv, hh)[0:n], nat[u][0:n, :, kv, hh, :])
                    ins.then_inc(sem("perm0" if kv == 0 else f"perm1_{u}"), 1)

            for c in range(B):
                pool.wait_ge(sem(f"nat_in{c % 2}"), (c // 2 + 1) * (16 * NPG))
                permute(c, c % 2, NCH)
            pool.wait_ge(sem("nat_in0"), 4 * 16 * NPG + 16)
            permute(B, 0, NCP + 1)
            pool.wait_ge(*signal("s_d", 1))
            def run_zero(hd):
                if hd:
                    pool.wait_ge(sem("sb_c"), 4 * hd)
                    pool.wait_ge(sem("sb_run"), 4 * hd)
                G_.memset(srun[:, :], 0.0).then_inc(sem("run_zero"), 1)
                pool.wait_ge(sem("run_zero"), hd + 1)

            def run_add(hd, i):
                m = 4 * hd + 3 - i
                pool.wait_ge(sem("sb_sp"), m + 1)
                pool.wait_ge(sem("sb_c"), m + 1)
                if i < 3:
                    pool.wait_ge(sem("sb_run"), m)
                G_.tensor_tensor(srun[:, i * P:SEQ], srun[:, i * P:SEQ], spb[:, m % 2, 0:SEQ - i * P], ALU.add).then_inc(sem("sb_run"), 1)

            def page_add(b, n):
                u = n % 8
                pool.wait_ge(sem("weighted"), (NPG - 1) * b + n)
                if n == 1:
                    pool.wait_ge(sem("ring_free0"), 2 * B + 2 * b + 1 + 1)
                else:
                    v = (n - 1) // 8
                    pool.wait_ge(sem(f"ring_free{(n - 1) % 8}"), 2 * B + 2 * b + v + 1 + 1)
                G_.tensor_tensor(vsum[:, b % 2, :], vsum[:, b % 2, :], ring[:, u, :], ALU.add).then_inc(sem(f"ring_free{u}"), 1)

            for n in range(8 * H):
                hd, k = n // 8, n % 8
                if k == 0:
                    run_zero(hd)
                if k in (0, 1, 3, 4):
                    run_add(hd, {0: 3, 1: 2, 3: 1, 4: 0}[k])
                for p in (2 * k, 2 * k + 1):
                    if p:
                        page_add(hd, p)


_INS = ["x_prompt", "x_sample", "cache_sb_kv", "cache_nsa_cmp_kv", "cache_nsa_slc_kv", "state_nsa_win_kv", "page_table",
        "w_in", "w_cmp_k1", "w_cmp_k2", "w_cmp_v1", "w_cmp_v2", "pe_cmp_k", "pe_cmp_v", "g_sb_out", "g_nsa_out", "w_out",
        "g_attn_norm", "g_mlp_norm", "w_up", "w_down", "g_final"]
_OUTS = [("y_p", (1, SEQ, D)), ("y_s", (B, 1, D)), ("sb_p", (1, 1, SEQ, 2, H, DH)), ("sb_s", (1, B, 1, 2, H, DH)),
         ("cmp_p", (1, 1, SEQ, 2, KVH, DH)), ("cmp_s", (1, B, 1, 2, KVH, DH)),
         ("slc_p", (1, 1, SEQ, 2, KVH, DH)), ("slc_s", (1, B, 1, 2, KVH, DH)),
         ("win_p", (1, 1, SEQ, 2, KVH, DH)), ("win_s", (1, B, WIN, 2, KVH, DH))]


def build(nc, shapes):
    A = {n: nc.dram_tensor(f"in_{n}_dram", s, d, kind="ExternalInput").ap() for n, (s, d) in shapes.items()}
    O = {n: nc.dram_tensor(f"out_{n}_dram", s, F32, kind="ExternalOutput").ap() for n, s in _OUTS}
    decoder_step(nc, A, O)


def kernel(**inputs):
    import concourse.bacc as bacc
    from concourse.bass_utils import run_bass_kernel_spmd as run

    arrays = {n: np.ascontiguousarray(inputs[n]) for n in _INS}
    arrays["consts"] = shape_constants()
    nc = bacc.Bacc("TRN2", target_bir_lowering=False, num_devices=1)
    build(nc, {n: (a.shape, mybir.dt.from_np(a.dtype)) for n, a in arrays.items()})
    r = run(nc, [{f"in_{n}_dram": a for n, a in arrays.items()}], core_ids=[0])
    return tuple(r.results[0][f"out_{n}_dram"] for n, _ in _OUTS)
```

```python
from contextlib import ExitStack

import numpy as np
import concourse.bass as bass
from concourse import mybir
from concourse.alu_op_type import AluOpType as ALU

ACT = mybir.ActivationFunctionType
AX = mybir.AxisListType
F32 = mybir.dt.float32
I32 = mybir.dt.int32
F32R = mybir.dt.float32r
ds = bass.ds

P = 128
D = 1024
KD = D // P
SEQ, NT = 512, 4
B = 8
TOK = SEQ + B
HALF = TOK // 2
T5 = NT + 1
H, DH, KVH, G = 8, 64, 2, 4
PAST, PAGE = 2048, 128
NPG = PAST // PAGE
NPHYS = 160
COLS = 2840
NCB = 10
CB = COLS // NCB
FIRST = 6
O_QS, O_KS, O_VS, O_QN, O_C, O_S, O_W, O_G = 0, 512, 1024, 1536, 2048, 2304, 2560, 2816
CH = 16
NCH = PAST // CH
NC = NCH - 1
NCP = SEQ // CH - 1
NSEL = 33
TOPN = 16
WIN = 512
NW = WIN // PAGE
DFF = 4096
FT = DFF // P
W0 = NCB // 2
FH = FT // 2
NEG, TINY, FORCE, EPS = -1e30, 1e-30, 1e9, 1e-6
SCALE = DH ** -0.5


COLUMNS = [(0, FIRST // 2, (NCB - FIRST) * CB), (FIRST // 2, (NCB - FIRST) // 2, 0)]


class Fields:

    def __init__(self, start, end):
        self.at, self.end = start, end

    def take(self, n):
        lo = self.at
        self.at += n
        assert self.at <= self.end, (self.at, self.end)
        return lo


CONST_FIELDS = [("ident", P), ("ntri", P), ("nones", P), ("ones", P), ("causal", P), ("before", P),
                ("half", P), ("pagemap", (NPG + 1) * 16), ("overlap", NSEL), ("lower", NSEL * NSEL),
                ("cadd", NT * NCP), ("cmul", NT * NCP), ("cos", T5 * DH), ("sin", T5 * DH), ("eps", 1), ("one", 1)]
CONST_AT = {}
_n = 0
for _name, _w in CONST_FIELDS:
    CONST_AT[_name] = (_n, _w)
    _n += _w
NCONST = -(-_n // 8) * 8


def shape_constants():
    c = np.zeros((P, NCONST), np.float32)

    def put(name, a):
        lo, _ = CONST_AT[name]
        a = a.reshape(a.shape[0], -1)
        c[:a.shape[0], lo:lo + a.shape[1]] = a

    r = np.arange(P)
    put("ident", np.eye(P))
    put("ntri", -(r[:, None] >= r[None, :]).astype(np.float32))
    put("nones", -np.ones((P, P)))
    put("ones", np.ones((P, P)))
    put("causal", np.where(r[None, :] <= r[:, None], 0.0, NEG))
    put("before", (r[:, None] < r[None, :]).astype(np.float32))
    blk = np.arange(NSEL)
    put("half", (blk[:, None] % 2 == (r[None, :] >= P // 2)).astype(np.float32))
    put("pagemap", np.repeat((blk[:, None] // 2 == np.arange(NPG + 1)[None, :])[:, :, None], 16, 2).astype(np.float32))
    cs = np.arange(NC) * CH
    put("overlap", ((cs[:, None] < blk[None, :] * 64 + 64) & (cs[:, None] + 32 > blk[None, :] * 64)).astype(np.float32))
    put("lower", np.broadcast_to((blk[None, :] < blk[:, None])[None], (16, NSEL, NSEL)).astype(np.float32))
    q = np.arange(NT)[None, :, None] * P + r[:, None, None]
    ok = (np.arange(NCP) * CH + 31)[None, None, :] <= q
    put("cadd", np.where(ok, 0.0, NEG))
    put("cmul", ok.astype(np.float32))
    inv = np.float32(10000.0) ** (-np.arange(32, dtype=np.float32) / np.float32(32))
    pos = np.zeros((P, T5), np.float32)
    pos[:, :NT] = np.arange(NT)[None, :] * P + r[:, None]
    pos[:, NT] = PAST
    ang = pos[:, :, None] * inv[None, None, :].astype(np.float32)
    co, si = np.cos(ang), np.sin(ang)
    put("cos", np.concatenate([co, co], -1))
    put("sin", np.concatenate([-si, si], -1))
    put("eps", np.full((P, 1), EPS))
    put("one", np.full((P, 1), 1.0))
    return c


SIGNALS = {
    "samples_pe": ["c_sc", "m_T", "c_scT", "m_b", "c_pT", "m_den", "c_imp", "c_selT", "c_mask", "m_T", "m_b", "m_den",
                   "s_c", "v_mm", "v_ss"],
    "samples_dve": ["m_max", "c_s", "m_diag", "s_abs", "c_nm", "m_sub", "c_p", "s_sp", "m_sum", "c_pg", "m_rec", "c_sel",
                    "s_suf", "c_selx", "c_selm", "m_max", "m_diag", "m_sub", "m_sum", "m_rec", "s_d", "z_free",
                    "v_sq", "v_st", "mix_ss"],
    "samples_act": ["s_ln", "c_e", "m_e", "m_e", "s_a", "v_rt", "mix_rt"],
}


PRIMED = {
    "pe": ["w_used0", "w_used1", "kq_mm0", "kq_mm1"] + [f"vq_mm{q}" for q in range(5)] + [f"ring_free{u}" for u in range(8)]
    + ["w2_mm0", "w2_mm1", "qs_mm", "y_mm0", "y_mm1"],
    "act": ["z_ev1", "z_ev3", "xT_ev0", "xT_ev1", "qs_ev", "kq_ev", "up_ev0", "up_ev1"],
    "dve": ["win_free0", "win_free1", "z_ev0", "z_ev2", "z_ev4", "hid_ready0", "hid_ready1", "qb_free0", "qb_free1", "kvc_ev0", "kvc_ev1",
            "w_lo0", "w_lo1", "a_ready0", "a_ready1", "dn_ev0", "dn_ev1", "y_ev0", "y_ev1"],
    "pool": ["perm1_0", "perm1_1"],
}


class Chain:

    def __init__(self, eng, sem):
        self.eng, self.sem, self.n, self.off = eng, sem, 0, 0

    def __call__(self, ins):
        self.n += 1
        ins.then_inc(self.sem, 1)
        self.eng.wait_ge(self.sem, self.off + self.n)


class Turns:

    def __init__(self, chain, count, per):
        self.chain, self.count, self.per = chain, count, per

    def __enter__(self):
        c = self.chain
        self.first = c.n
        self.loop = c.eng.Fori(0, self.count)
        i = self.loop.__enter__()
        c.off = i * self.per
        return i

    def __exit__(self, *e):
        c = self.chain
        if e[0] is None:
            assert c.n - self.first == self.per, (c.n - self.first, self.per)
        c.off = 0
        c.n = self.first + self.count * self.per
        return self.loop.__exit__(*e)


def decoder_step(nc, A, O):
    with ExitStack() as ctx:
        sems = {}

        def signal(name, v):
            group = [g for g, order in SIGNALS.items() if name in order][0]
            return sem(group), [n for n, x in enumerate(SIGNALS[group], 1) if x == name][v - 1]

        def prime(eng, who):
            for name in PRIMED[who]:
                eng.sem_inc(sem(name), 1)

        def sem(name):
            if name not in sems:
                sems[name] = ctx.enter_context(nc.semaphore(name))
            return sems[name]

        TOTAL = 52904
        aT_at = NCONST + P + 56 + 256 + P
        hT_at = aT_at + T5 * COLS + 14 * SEQ
        base = -(-nc.sbuf_base // 64) * 64 + 64
        low_arena = nc.alloc_sbuf_tensor_at("low_arena", [P, hT_at], F32, offset=base)
        high_arena = nc.alloc_sbuf_tensor_at("high_arena", [P, TOTAL - hT_at], F32, offset=base + 4 * hT_at)
        pt = nc.alloc_sbuf_tensor_at("page_ids", [1, B * NPG], I32, offset=base + 4 * TOTAL)
        bank = [ctx.enter_context(nc.psum_tensor(f"bank{i}", [P, 512], F32)) for i in range(8)]
        sbq_dram = nc.dram_tensor("sb_queries", (B, 512), F32, kind="Internal").ap()

        def shaped(a, dims):
            names = "abcd"[:len(dims)]
            if len(dims) > 1:
                a = a.rearrange(f"p ({' '.join(names)}) -> p {' '.join(names)}", **dict(zip(names, dims)))
            return a

        def view(lo, *dims):
            n = int(np.prod(dims))
            assert lo + n <= hT_at or lo >= hT_at
            return shaped(low_arena[:, lo:lo + n] if lo < hT_at else high_arena[:, lo - hT_at:lo - hT_at + n], dims)

        def rounded(name, lo, *dims):
            n = int(np.prod(dims))
            return shaped(nc.alloc_sbuf_tensor_at(name, [P, n], F32R, offset=base + 4 * lo)[:, :], dims)

        def parts(name, lo, *dims):
            v = rounded(name, lo, *dims)
            return v.bitcast(F32), v

        allr = Fields(0, TOTAL)
        const = view(allr.take(NCONST), NCONST)

        def K(name):
            lo, w = CONST_AT[name]
            return const[:, lo:lo + w]

        ident, ntri, nones, ones = K("ident"), K("ntri"), K("nones"), K("ones")
        vrow = view(allr.take(P), P)
        vcol = view(allr.take(56), 56)
        st = view(allr.take(256), 256)
        zero = view(allr.take(P), P)
        z = view(allr.take(T5 * COLS), T5, COLS)
        hT_lo1_r = rounded("h_low_in", allr.at, KD, TOK)
        sbqT = view(allr.take(4 * SEQ), 4, SEQ)
        sbkT = view(allr.take(4 * SEQ), 4, SEQ)
        nqT = view(allr.take(4 * SEQ), 4, SEQ)
        ksT = view(allr.take(SEQ), SEQ)
        kwT = view(allr.take(SEQ), SEQ)
        assert allr.take(KD * TOK) == hT_at
        hT, hT_r = parts("h_high", hT_at, KD, TOK)
        x_at = allr.take(T5 * D)
        x = view(x_at, T5, D)
        r_at = allr.at

        r = Fields(r_at, TOTAL)
        h_at = r.take(T5 * D)
        h = view(h_at, T5, D)
        win_at = [r.take(KD * CB) for _ in range(2)]
        win = [view(at, KD, CB) for at in win_at]
        win_r = [rounded(f"w_in_low{u}", at, KD, CB) for u, at in enumerate(win_at)]
        win_hi, win_hi_r = zip(*(parts(f"w_in_high{u}", r.take(KD * CB), KD, CB) for u in range(2)))
        r = Fields(r_at, TOTAL)
        ropeA, ropeB = view(r.take(512), 512), view(r.take(512), 512)
        r = Fields(r_at + 1024, TOTAL)
        qbd = view(r.take(B * H), B, H)
        snew = view(r.take(2 * H), 2, H)
        qsc = view(r.take(512), 512)
        newrow = view(r.take(2 * B * H), 2, B, H)
        vnew = view(r.take(2 * B * P), 2, B, P)
        grow = view(r.take(B * 24), B, H, 3)
        kc_at = r.at
        kc = view(r.take((B + 1) * P), B + 1, P)
        vc = view(r.take((B + 1) * P), B + 1, P)
        slc = view(r.take(B * (NPG + 1) * H), B, NPG + 1, H)
        wsc = view(r.take(B * (NW + 1) * H), B, NW + 1, H)
        att_at = r.at
        w1 = [view(x_at + i * 2048, 16, P) for i in range(2)]
        w2 = [view(x_at + 4096 + i * DH, DH) for i in range(2)]
        pebias = view(x_at + 4224, 4)
        xT = [view(hT_at + i * 2048, KD, KVH, P) for i in range(2)]
        nat = [view(r.take(4096), CH, 2, KVH, DH) for _ in range(2)]
        hid = [view(r.take(256), KVH, P) for _ in range(4)]
        qb = view(r.take(2 * 512), 2, 512)
        kqT = view(x_at + 4228, 4, P)
        kring = [z[:, t, O_QN:O_QN + 512] for t in range(NT)] + [z[:, NT, u * 512:(u + 1) * 512] for u in range(4)]
        kquad = [z[:, 0:NT, o:o + P] for o in (O_S, O_W)]

        def raw_scores(i, u):
            return z[:, i, O_C + u * P:O_C + (u + 1) * P].rearrange("p o (n j) -> p (o n) j", j=H)


        def per(kv, hh):
            return z[:, 2 * kv + hh, 0:1024].rearrange("p (t d) -> p t d", t=CH)

        a1 = Fields(x_at, r_at)
        r = Fields(att_at, TOTAL)
        ring = view(a1.take(8 * 512), 8, 512)
        vsum = view(a1.take(2 * 512), 2, 512)
        quad = view(r.take(5 * 512), 5, 4, P)
        sbs = view(r.take(B * NPG * H), B, NPG, H)
        osb_at = r.take(NT * 512)
        o_sb = view(osb_at, NT, 512)
        o_n = view(r.take(NT * 512), NT, 512)
        w0 = w = Fields(r.at, TOTAL)
        pbuf = view(w.take(2 * 512), 2, 512)
        ptb = view(w.take(2 * 512), 2, 512)
        w = Fields(hT_at, hT_at + KD * TOK)
        spb = view(w.take(2 * 512), 2, 512)
        ebuf = view(w.take(2 * 512), 2, 512)
        abuf = view(w.take(2 * 512), 2, 512)
        srun = view(w.take(512), 512)
        ofs = view(w0.take(12 * 64), 12, 64)
        w = Fields(osb_at, osb_at + NT * 512)
        sps = view(w.take(1024), B, NPG, H)
        suf = view(w.take(1024), B, NPG, H)
        w = Fields(hT_at, hT_at + KD * TOK)
        s64 = view(w.take(9 * P), 9, P)
        rankA = view(w.take(NSEL * NSEL), NSEL, NSEL)
        rankB = view(w.take(NSEL * NSEL), NSEL, NSEL)
        selx = view(w.take(272), NPG + 1, 16)
        selm = view(w.take(272), NPG + 1, 16)
        pcT = view(w.take(64), 64)
        w = Fields(aT_at, hT_at)
        aT, aT_r = parts("a_high", w.take(FH * TOK), FH, TOK)
        aT_lo_r = rounded("a_low", w.take(FH * TOK), FH, TOK)
        wout = view(aT_at, KD, D)
        wout_r = rounded("w_out_low", aT_at, KD, D)
        wout_hi, wout_hi_r = parts("w_out_high", aT_at + KD * D, KD, D)
        gfin = view(w.take(D), D)
        relu = view(w.take(2 * TOK), 2, TOK)
        act2 = view(w.take(TOK), TOK)
        yT = [view(w.take(TOK), TOK) for _ in range(2)]
        w_raw = [view(r_at + u * KD * P, KD, P) for u in range(2)]
        r = Fields(kc_at, TOTAL)
        hT_lo_r = rounded("h_low", r.take(KD * TOK), KD, TOK)
        h2 = view(r.take(T5 * D), T5, D)
        w_hi, w_hi_r = zip(*(parts(f"w_high{u}", r.take(KD * P), KD, P) for u in range(2)))
        w_lo_r = [rounded(f"w_low{u}", r.take(KD * P), KD, P) for u in range(2)]
        rows = [P] * NT + [B]


        def over(ap, axis, n):
            a = ap.unsqueeze(axis)
            shape = list(a.shape)
            shape[axis] = n
            return a.broadcast_to(shape)

        def place(hd):
            return (hd % G) * KVH + hd // G

        block = ctx.enter_context(nc.Block())
        xp, xs = A["x_prompt"][0], A["x_sample"].rearrange("b o d -> (b o) d")
        c_sb, c_cmp, c_slc = A["cache_sb_kv"][0], A["cache_nsa_cmp_kv"][0], A["cache_nsa_slc_kv"][0]
        w_in, w_up, w_down, w_out = A["w_in"][0], A["w_up"][0], A["w_down"][0], A["w_out"][0]

        @block.sync
        def _(sp):
            sp.dma_start(x[:, 0:NT, :], xp.rearrange("(t p) d -> p t d", p=P)).then_inc(sem("x_in"), 16)
            sp.dma_start(x[0:B, NT, :], xs).then_inc(sem("x_in"), 16)
            sp.dma_start(const, A["consts"]).then_inc(sem("const_in"), 16)
            for r0, n, src in ((0, 8, A["g_attn_norm"][0]), (8, 8, A["g_mlp_norm"][0]), (16, 4, A["g_sb_out"][0])):
                sp.dma_start(vrow[r0:r0 + n, :], src.rearrange("(r c) -> r c", c=P)).then_inc(sem("vrow_in"), 16)
            for two in range(2):
                sp.dma_start(vrow[20:24, two * DH:(two + 1) * DH],
                    A["g_nsa_out"][0].rearrange("(two t d) -> two t d", two=2, t=4)[two]).then_inc(sem("vrow_in"), 16)
            for r0, src in ((24, A["pe_cmp_k"][0]), (40, A["pe_cmp_v"][0])):
                sp.dma_start(vrow[r0:r0 + 16, :], src.rearrange("(m two) d -> m (two d)", two=2)).then_inc(sem("vrow_in"), 16)
            sp.dma_start(pt[:, :], A["page_table"].rearrange("(o b) n -> o (b n)", o=1)).then_inc(sem("pages_in"), 16)
            w_in_v = w_in.rearrange("(k p) c -> p k c", p=P)
            for turn, turns, col in COLUMNS:
                with sp.Fori(0, turns) as i:
                    for u in range(2):
                        sp.wait_ge(sem(f"win_free{u}"), i + turn + 1)
                        sp.dma_start(win[u][:, :, :], w_in_v[:, :, ds(i * (2 * CB) + (u * CB + col), CB)]).then_inc(sem(f"win_in{u}"), 16)
            sp.wait_ge(sem("h_ready"), 2)
            for kv, n in enumerate(("w_cmp_k1", "w_cmp_v1")):
                sp.dma_start(w1[kv][:, :, :], A[n][0].rearrange("(m p) c -> p m c", p=P)).then_inc(sem("cmpw_in"), 16)
            for kv, n in enumerate(("w_cmp_k2", "w_cmp_v2")):
                sp.dma_start(w2[kv], A[n][0]).then_inc(sem("cmpw_in"), 16)
            sp.wait_ge(sem("pages_in"), 16)
            for t in range(T5):
                sp.wait_ge(sem(f"z_ev{t}"), NCB + 1)
            def page_ids(lo):
                return nc.values_load_multi_w_load_instructions(
                    pt[0:1, ds(lo, 8)], engines=[mybir.EngineType.SP], min_val=0, max_val=NPHYS - 1,
                    skip_runtime_bounds_check_because="entries of the page table are pages of the caches")[1]

            def load_chunks(lo, u, half):
                for p, pg in enumerate(page_ids(lo + 8 * half), 8 * half):
                    sp.dma_start(nat[u][8 * p:8 * p + 8].rearrange("p t k h d -> p (t k h d)"),
                                 c_cmp[ds(pg, 1)].rearrange("o (c t) k h d -> (o c) (t k h d)", t=CH)).then_inc(sem(f"nat_in{u}"), 16)

            for half in range(2):
                load_chunks(0, 0, half)
            sp.wait_ge(sem("rope_done"), T5)
            sp.wait_ge(sem("qkT_mm"), 15)
            sp.wait_ge(sem("kv_out"), 16 * (B + 6))
            sp.wait_ge(sem("sbq_out"), 16)
            sp.wait_ge(sem("rows_in"), 96)
            win_v = A["state_nsa_win_kv"][0].rearrange("b (t p) k h d -> b p t k (h d)", p=P)

            def load_keys(i, u, ahead):
                c = i * 2 + u
                sp.wait_ge(sem(f"qb_free{u}"), i + 1)
                sp.dma_start(qb[:, u, :], sbq_dram[ds(c, 1), :].broadcast_to([P, 512])).then_inc(sem(f"qb_in{u}"), 16)
                for half in range(2):
                    if ahead:
                        if half == 0:
                            sp.wait_ge(sem(f"perm1_{1 - u}"), i + u + 1)
                        load_chunks(c * NPG + NPG, 1 - u, half)
                    pages = page_ids(c * NPG + 8 * half)
                    for p in range(8):
                        if p % 4 == 0:
                            n = 5 * u + 2 * half + p // 4
                            sp.wait_ge(sem(f"kq_mm{n % 2}"), i * 5 + n // 2 + 1)
                            for j in range(4):
                                sp.dma_start(kquad[n % 2][:, j], c_slc[ds(pages[p + j], 1), :, 0].rearrange("o s h d -> (o s) (h d)")
                                             ).then_inc(sem(f"kq_in{n % 2}"), 16)
                        sp.wait_ge(sem(f"ring_free{p}"), i * 4 + 2 * u + half + 1)
                        sp.dma_start(kring[p], c_sb[ds(pages[p], 1), :, 0].rearrange("o s h d -> (o s) (h d)")).then_inc(sem(f"ring_in{p}"), 16)
                n = 5 * u + 4
                sp.wait_ge(sem(f"kq_mm{n % 2}"), i * 5 + n // 2 + 1)
                sp.dma_start(kquad[n % 2], win_v[ds(c, 1), :, :, 0, :].rearrange("o p t c -> (o p) t c")).then_inc(sem(f"kq_in{n % 2}"), 64)

            with sp.Fori(0, 3) as i:
                for u in range(2):
                    load_keys(i, u, True)
            load_keys(3, 0, True)
            sp.wait_ge(sem("cmp_stored"), 16)
            sp.wait_ge(sem("perm1_0"), 4 + 1)
            sp.dma_start(nat[0][0:NCP + 1].rearrange("p t k h d -> p (t k h d)"),
                O["cmp_p"][0, 0].rearrange("(c t) k h d -> c (t k h d)", t=CH)).then_inc(sem("nat_in0"), 16)
            load_keys(3, 1, False)
            sp.wait_ge(sem("kvc_ev0"), 9 + 1)
            sp.wait_ge(sem("kvc_ev1"), 9 + 1)
            sp.wait_ge(sem("qs_ev"), B + 1)
            with sp.Fori(0, B) as b:
                for half in range(2):
                    pages = page_ids(b * NPG + 8 * half)
                    for u in range(8):
                        sp.wait_ge(sem(f"ring_free{u}"), b * 2 + (2 * B + half + 1))
                        sp.dma_start(ring[:, u, :], c_sb[ds(pages[u], 1), :, 1].rearrange("o s h d -> (o s) (h d)")).then_inc(sem(f"ring_in{u}"), 16)
                        if u % 4 == 3:
                            q = 2 * half + u // 4
                            sp.wait_ge(sem(f"vq_mm{q}"), b + 1)
                            for j in range(4):
                                sp.dma_start(quad[:, q, j, :], c_slc[ds(pages[u - 3 + j], 1), :, 1].rearrange("o s h d -> (o s) (h d)")
                                             ).then_inc(sem(f"quad_in{q}"), 16)
                sp.wait_ge(sem("vq_mm4"), b + 1)
                sp.dma_start(quad[:, 4], win_v[ds(b, 1), :, :, 1, :].rearrange("o p t c -> (o p) t c")).then_inc(sem("quad_in4"), 64)
            sp.wait_ge(*signal("z_free", 1))
            sp.wait_ge(sem("kv_out"), 16 * (B + 6))
            sp.wait_ge(sem("rows_in"), 96)
            for r0 in range(0, 4, 2):
                sp.dma_start(wout[:, r0:r0 + 2, :], w_out.rearrange("(k p) c -> p k c", p=P)[:, r0:r0 + 2, :]).then_inc(sem("wout_in"), 16)
            for two in range(2):
                sp.dma_start(wout[two * DH:(two + 1) * DH, 4:8, :],
                    w_out[512 + 256 * two:768 + 256 * two, :].rearrange("(t d) c -> d t c", d=DH)).then_inc(sem("wout_in"), 16)
            sp.wait_ge(sem("vsum_mm"), B)
            sp.dma_start(x[:, 0:NT, :], xp.rearrange("(t p) d -> p t d", p=P)).then_inc(sem("x2_in"), 16)
            sp.dma_start(x[0:B, NT, :], xs).then_inc(sem("x2_in"), 16)
            sp.wait_ge(sem("mix_ready"), 2)
            sp.wait_ge(sem("mixT_mm"), 4)
            w_up_v = w_up.rearrange("(k p) c -> p k c", p=P)
            w_dn_v = w_down.rearrange("(k p) c -> p k c", p=P)
            for half in range(2):
                with sp.Fori(0, FH // 2) as i:
                    for u in range(2):
                        sp.wait_ge(sem(f"w_lo{u}"), i + (16 * half + W0) + 1)
                        sp.dma_start(w_raw[u], w_up_v[:, :, ds(i * (2 * P) + (u * P + half * FH * P), P)]).then_inc(sem(f"w_in{u}"), 16)
                if half == 0:
                    sp.wait_ge(sem("out_mm"), 2 * T5)
                    sp.dma_start(gfin, A["g_final"].rearrange("(o d) -> o d", o=1).broadcast_to([P, D])).then_inc(sem("gfin_in"), 16)
                with sp.Fori(0, KD) as i:
                    for u in range(2):
                        sp.wait_ge(sem(f"w_lo{u}"), i + (16 * half + 8 + W0) + 1)
                        k = half * FH + u * 8
                        sp.dma_start(w_raw[u], w_dn_v[:, k:k + 8, ds(i * P, P)]).then_inc(sem(f"w_in{u}"), 16)
            for t in range(NT):
                sp.wait_ge(sem("y_ready"), t + 1)
                sp.dma_start(O["y_p"][0].rearrange("(t p) d -> p t d", p=P)[:, t, :], h2[:, t, :]).then_inc(sem("y_out"), 16)
            sp.wait_ge(sem("y_ready"), T5)
            sp.dma_start(O["y_s"].rearrange("b o d -> (b o) d"), h2[0:B, NT, :]).then_inc(sem("y_out"), 16)
            sp.wait_ge(sem("y_out"), 16 * T5)

        @block.tensor
        def _(pe):
            T = nc.tensor
            prime(pe, "pe")

            def mm(out, l, r, start=True, stop=True, **k):
                return T.matmul(out, lhsT=l, rhs=r, start=start, stop=stop, **k)

            def tr(out, in_):
                n = in_.shape[0]
                return T.transpose(out, in_, ident[0:n, 0:n])

            def norm_transposes(src, turn):
                pe.wait_ge(sem("h_ready"), 2 * turn + 1)
                for k in range(KD):
                    if k >= 2:
                        pe.wait_ge(sem("hT_ev"), turn * 9 + k - 1)
                    for t in range(NT):
                        i = tr(bank[k % 2][:, t * P:(t + 1) * P], src[:, t, k * P:(k + 1) * P])
                    i.then_inc(sem("hT_mm"), 1)
                pe.wait_ge(sem("h_ready"), 2 * turn + 2)
                for k in range(KD):
                    i = tr(bank[2][:, k * B:(k + 1) * B], src[0:B, NT, k * P:(k + 1) * P])
                i.then_inc(sem("hT_mm"), 1)

            pe.wait_ge(sem("const_in"), 16)
            pe.wait_ge(sem("vrow_in"), 16 * 7)
            tr(bank[3][:, 0:56], vrow[0:56, :]).then_inc(sem("vcol_mm"), 1)
            norm_transposes(h, 0)
            pe.wait_ge(sem("vcol_ev"), 1)
            pe.wait_ge(sem("hT_ev"), 9)
            with pe.Fori(0, NCB // 2) as i:
                for u in range(2):
                    pe.wait_ge(sem(f"w_lo{u}"), i + 1 + 1)
                    for t in range(T5):
                        pe.wait_ge(sem(f"z_ev{t}"), i * 2 + u + 1)
                        for k in range(KD):
                            for n, (h_, w_) in enumerate(((hT_r, win_hi_r), (hT_r, win_r), (hT_lo1_r, win_hi_r))):
                                ins = mm(bank[t][0:rows[t], 0:CB], h_[:, k, t * P:t * P + rows[t]], w_[u][:, k, :],
                                         k == 0 and n == 0, k == KD - 1 and n == 2)
                        ins.then_inc(sem("z_mm"), 1)
            pe.wait_ge(sem("rope_done"), T5)
            for t in range(T5):
                pe.wait_ge(sem(f"z_ev{t}"), NCB + 1)
            src = [(lambda t, j=j: z[:, t, O_QS + j * P:O_QS + (j + 1) * P]) for j in range(4)]
            src += [(lambda t, j=j: z[:, t, O_KS + j * P:O_KS + (j + 1) * P]) for j in range(4)]
            src += [(lambda t, j=j: z[:, t, O_QN + j * P:O_QN + (j + 1) * P]) for j in range(4)]
            src += [(lambda t, o=o: z[:, t, o:o + P]) for o in (O_S, O_W)]
            for j, s in enumerate(src):
                if j >= 4:
                    pe.wait_ge(sem(f"qkT_ev{j % 2}"), (j - 4) // 2 + 1)
                for t in range(NT):
                    ins = tr(bank[j % 4][:, t * P:(t + 1) * P], s(t))
                ins.then_inc(sem("qkT_mm"), 1)
            for j in range(4):
                ins = tr(bank[4][:, j * B:(j + 1) * B], z[0:B, NT, O_QN + j * P:O_QN + (j + 1) * P])
            ins.then_inc(sem("qkT_mm"), 1)
            pe.wait_ge(sem("cmpw_in"), 64)
            for kv in range(2):
                for m in range(16):
                    ins = mm(bank[6][:, kv:kv + 1], w1[kv][:, m, :], vcol[:, 24 + 16 * kv + m:25 + 16 * kv + m],
                             m == 0, m == 15)
            ins.then_inc(sem("pe_mm"), 1)
            for j in range(2):
                pe.wait_ge(sem(f"qkT_ev{j}"), 7)
            pe.wait_ge(sem("qkT_ev0"), 8)
            pe.wait_ge(sem("pebias"), 2)

            def keys_T(i, u, q):
                n = 5 * u + q
                pe.wait_ge(sem(f"kq_in{n % 2}"), (i * 5 + n // 2 + 1) * 64)
                pe.wait_ge(sem("kq_ev"), i * 10 + n + 1)
                for j in range(4):
                    ins = tr(bank[6][:, j * P:(j + 1) * P], kquad[n % 2][:, j])
                ins.then_inc(sem(f"kq_mm{n % 2}"), 1)

            def key_scores(i, u, q):
                pe.wait_ge(sem("kq_ev"), i * 10 + 5 * u + q + 1 + 1)
                if q == 0:
                    pe.wait_ge(sem("qs_ev"), i * 2 + u + 1)
                for j in range(4):
                    c = (4 * q + j) * H
                    ins = mm(bank[7][:, c:c + H], kqT[:, j, :], qbd[:, ds(i * 2 + u, 1), :].rearrange("p o j -> p (o j)"))
                ins.then_inc(sem("qs_mm"), 1)

            def compress(c, u, i, n, between):
                nb = n - 1
                for kv in range(2):
                    if kv == 0:
                        pe.wait_ge(sem("perm0"), c + 1)
                    else:
                        pe.wait_ge(sem(f"perm1_{u}"), i + 1 + 1)
                    pe.wait_ge(sem(f"hid_ready{kv}"), c + 1)
                    for s in range(5):
                        if s < 4:
                            pe.wait_ge(sem(f"xT_ev{s % 2}"), c * 4 + kv * 2 + s // 2 + 1)
                            for j in range(2):
                                for hh in range(KVH):
                                    m = 2 * s + j
                                    ins = tr(bank[s % 2][:, (2 * j + hh) * P:(2 * j + hh) * P + n],
                                             per(kv, hh)[0:n, 2 * m:2 * m + 2, :].rearrange("p t d -> p (t d)"))
                            ins.then_inc(sem("xT_mm"), 1)
                        if s >= 1:
                            pe.wait_ge(sem(f"xT_ev{(s - 1) % 2}"), c * 4 + kv * 2 + (s - 1) // 2 + 1 + 1)
                            for m in (2 * s - 2, 2 * s - 1):
                                out = bank[2 + kv][:, 0:KVH * nb].rearrange("p (h c) -> p h c", h=KVH)
                                mm(out, w1[kv][:, m, :], xT[kv][:, m, :, 0:nb], m == 0, False)
                                ins = mm(out, w1[kv][:, 8 + m, :], xT[kv][:, m, :, 1:n], False, m == 7)
                            if s == 4:
                                ins.then_inc(sem(f"hid_mm{kv}"), 1)
                        if s in (1, 3):
                            between()
                between()
                between()
                pe.wait_ge(sem("hid_ready0"), c + 1 + 1)
                pe.wait_ge(sem("kvc_ev0"), c + 1)
                for hh in range(KVH):
                    ins = mm(bank[4][DH * hh:DH * (hh + 1), 0:nb], w2[0], hid[2][:, hh, 0:nb])
                ins.then_inc(sem("w2_mm0"), 1)
                pe.wait_ge(sem("hid_ready1"), c + 1 + 1)
                pe.wait_ge(sem("kvc_ev1"), c + 1)
                for hh in range(KVH):
                    ins = mm(bank[5][0:nb, DH * hh:DH * (hh + 1)], hid[3][:, hh, 0:nb], w2[1])
                ins.then_inc(sem("w2_mm1"), 1)

            with pe.Fori(0, 4) as i:
                for u in range(2):
                    todo = [lambda: keys_T(i, u, 0)]
                    for q in range(4):
                        todo.append(lambda q=q: (key_scores(i, u, q), keys_T(i, u, q + 1)))
                    todo.append(lambda: key_scores(i, u, 4))
                    compress(i * 2 + u, u, i, NCH, lambda: todo.pop(0)())
            compress(B, 0, 4, NCP + 1, lambda: None)

            for kv in range(2):
                pe.wait_ge(sem(f"kvc_ev{kv}"), B + 1 + 1)
            pe.wait_ge(sem("qs_ev"), B + 1)

            def cp_qk(i):
                if i >= 1:
                    pe.wait_ge(sem("cp_soft"), i)
                for n in range(H):
                    o = DH * (n // G)
                    ins = mm(bank[4 + n // G][:, (n % G) * NCP:(n % G + 1) * NCP], nqT[o:o + DH, n % G, i * P:(i + 1) * P],
                             kc[o:o + DH, B, 0:NCP])
                ins.then_inc(sem("cp_qk"), 1)

            def cp_tr(i):
                pe.wait_ge(sem("cp_soft"), i + 1)
                if i >= 1:
                    pe.wait_ge(sem("cp_pT"), 2 * i)
                for n in range(H):
                    ins = tr(bank[6 + n // 4][0:NCP, (n % 4) * P:(n % 4 + 1) * P], pbuf[:, 0, n * NCP:(n + 1) * NCP])
                    if n % 4 == 3:
                        ins.then_inc(sem("cp_tr"), 1)

            def cp_pv(i):
                pe.wait_ge(sem("cp_pT"), 2 * i + 2)
                if i >= 2:
                    pe.wait_ge(sem("cp_out"), i - 1)
                for n in range(H):
                    o = DH * (n // G)
                    ins = mm(bank[i % 2][:, place(n) * DH:(place(n) + 1) * DH], ptb[0:NCP].rearrange("p a b -> p (a b)")[:, n * P:(n + 1) * P],
                             vc[0:NCP, B, o:o + DH])
                ins.then_inc(sem("cp_pv"), 1)

            def row_max(br):
                pe.wait_ge(*signal("m_max", br + 1))
                tr(bank[3][0:64, 0:P], s64[:, 7, 0:64]).then_inc(sem("samples_pe"), 1)

            def row_max_over(br):
                pe.wait_ge(*signal("m_diag", br + 1))
                mm(bank[3][:, 0:64], ones[0:64, :], s64[0:64, 7, 64:128]).then_inc(sem("samples_pe"), 1)

            def row_sum_over(br):
                pe.wait_ge(*signal("m_sum", br + 1))
                mm(bank[3][:, 0:64], ones, s64[:, 8, 64:128]).then_inc(sem("samples_pe"), 1)

            for b in range(B):
                ins = mm(bank[2][0:NC, b * H:(b + 1) * H], kc[:, b, 0:NC], qbd[:, b, :])
            ins.then_inc(sem("samples_pe"), 1)
            cp_qk(0)
            row_max(0)
            pe.wait_ge(*signal("c_s", 1))
            tr(bank[2][0:64, 0:NC], s64[0:NC, 0, 0:64]).then_inc(sem("samples_pe"), 1)
            row_max_over(0)
            cp_tr(0)
            pe.wait_ge(*signal("c_p", 1))
            tr(bank[2][0:NC, 0:64], s64[0:64, 2, 0:NC]).then_inc(sem("samples_pe"), 1)
            cp_pv(0)
            cp_qk(1)
            row_sum_over(0)
            pe.wait_ge(*signal("c_pg", 1))
            mm(bank[2][0:16, 0:NSEL], s64[0:NC, 3, 0:16], K("overlap")[0:NC, :]).then_inc(sem("samples_pe"), 1)
            cp_tr(1)
            cp_pv(1)
            cp_qk(2)
            pe.wait_ge(*signal("c_sel", 1))
            tr(bank[2][0:NSEL, 0:16], s64[0:16, 5, 0:NSEL]).then_inc(sem("samples_pe"), 1)
            cp_tr(2)
            pe.wait_ge(*signal("c_selx", 1))
            mm(bank[2][:, 0:272], K("half")[0:NSEL, :], selx[0:NSEL].rearrange("p a b -> p (a b)")).then_inc(sem("samples_pe"), 1)
            cp_pv(2)
            cp_qk(3)
            row_max(1)
            cp_tr(3)
            row_max_over(1)
            cp_pv(3)
            row_sum_over(1)
            pe.wait_ge(sem("cp_pT"), 2 * NT)
            mm(bank[7][:, 0:256], zero, over(zero, 1, 2), True, False, skip_group_check=True)
            for b in range(B):
                mm(bank[7][:, 192 + b * H:192 + (b + 1) * H], vc[0:NC, b, :], pcT[0:NC, b * H:(b + 1) * H], False, False, skip_group_check=True)
            pe.wait_ge(*signal("s_suf", 1))
            pe.wait_ge(*signal("m_rec", 2))
            for c in range(2):
                mm(bank[2 + c][:, 0:512], ntri, sps[:, 4 * c:4 * c + 4].rearrange("p b n j -> p (b n j)"), True, False)
                ins = mm(bank[2 + c][:, 0:512], nones, suf[:, 4 * c:4 * c + 4].rearrange("p b n j -> p (b n j)"), False, True)
            ins.then_inc(sem("samples_pe"), 1)
            pe.wait_ge(sem("cp_out"), NT)
            pe.wait_ge(*signal("s_d", 1))

            def sb_qk(hd, i):
                m = 4 * hd + 3 - i
                if m >= 2:
                    pe.wait_ge(sem("sb_a"), m - 1)
                o = DH * (hd % 2)
                mm(bank[m % 2][:, 0:SEQ - i * P], sbkT[o:o + DH, hd // 2, i * P:(i + 1) * P],
                        sbqT[o:o + DH, hd // 2, i * P:SEQ], True, False, skip_group_check=True).then_inc(sem("sb_qk"), 1)

            def sb_sum(hd, i):
                m = 4 * hd + 3 - i
                pe.wait_ge(sem("sb_sp"), m + 1)
                n = SEQ - i * P
                ins = mm(bank[m % 2][:, 0:n], ntri, spb[:, m % 2, 0:n], False, i == 3, skip_group_check=True)
                if i < 3:
                    pe.wait_ge(sem("sb_run"), m)
                    ins = mm(bank[m % 2][:, P:n], nones, srun[:, (i + 1) * P:SEQ], False, True, skip_group_check=True)
                ins.then_inc(sem("sb_c"), 1)

            def sb_pv(hd, i):
                m = 4 * hd + 3 - i
                pe.wait_ge(sem("sb_am"), m + 1)
                if i == 3 and hd:
                    pe.wait_ge(sem("sb_out"), hd)
                for j in range(i, NT):
                    ins = mm(bank[2][:, j * DH:(j + 1) * DH], abuf[:, m % 2, (j - i) * P:(j - i + 1) * P],
                             z[:, i, O_VS + hd * DH:O_VS + (hd + 1) * DH], i == 3, i == 0, skip_group_check=True)
                ins.then_inc(sem("sb_pv"), 1)

            def n_unit(n):
                hd, br, i = n // 8, (n // 4) % 2, n % 4
                return hd, br, i, DH * (hd // G)

            def n_qk(n):
                hd, br, i, o = n_unit(n)
                if n >= 2:
                    pe.wait_ge(sem("n_exp"), n - 1)
                mm(bank[3 + n % 2][:, 0:(i + 1) * P], nqT[o:o + DH, hd % G, i * P:(i + 1) * P],
                        (ksT, kwT)[br][o:o + DH, 0:(i + 1) * P]).then_inc(sem("n_qk"), 1)

            def n_tr(n):
                hd, br, i, o = n_unit(n)
                pe.wait_ge(sem("n_exp"), n + 1)
                if n >= 1:
                    pe.wait_ge(sem("n_pT"), n)
                for j in range(i + 1):
                    ins = tr(bank[5][:, j * P:(j + 1) * P], pbuf[:, n % 2, j * P:(j + 1) * P])
                ins.then_inc(sem("n_tr"), 1)

            def n_pv(n):
                hd, br, i, o = n_unit(n)
                pe.wait_ge(sem("n_pT"), n + 1)
                if n >= 1:
                    pe.wait_ge(sem("n_out"), n)
                vo = (O_S, O_W)[br] + P + o
                for j in range(i + 1):
                    ins = mm(bank[6][:, 0:DH], ptb[:, n % 2, j * P:(j + 1) * P], z[:, j, vo:vo + DH], j == 0, j == i)
                ins.then_inc(sem("n_pv"), 1)

            def page_values(b):
                pe.wait_ge(sem("ring_free7"), 2 * B + 2 * b + 2 + 1)
                for t in range(4):
                    ins = mm(bank[7][:, t * B + b:t * B + b + 1], vsum[:, b % 2, t * P:(t + 1) * P], ones[:, 0:1],
                             False, False, skip_group_check=True)
                ins.then_inc(sem("vsum_mm"), 1)

            def quad_values(b, q):
                pe.wait_ge(sem(f"quad_in{q}"), (b + 1) * 64)
                for j in range(4):
                    w_, c = (slc[:, b, 4 * q + j, :], 64) if q < 4 else (wsc[:, b, j, :], 128)
                    ins = mm(bank[7][:, c + b * H:c + (b + 1) * H], quad[:, q, j, :], w_, False, False, skip_group_check=True)
                ins.then_inc(sem(f"vq_mm{q}"), 1)

            for n in range(8 * H + 2):
                hd, k = n // 8, n % 8
                if n < 8 * H:
                    n_qk(n)
                    if k == 0:
                        sb_qk(hd, 3)
                        sb_qk(hd, 2)
                    if k in (2, 3):
                        sb_qk(hd, 3 - k)
                    if 1 <= k < 5:
                        sb_sum(hd, 4 - k)
                if 1 <= n < 8 * H + 1:
                    n_tr(n - 1)
                if n < 8 * H and 2 <= k < 6:
                    sb_pv(hd, 5 - k)
                if n >= 2:
                    n_pv(n - 2)
                if n < 8 * H:
                    if n == 0:
                        pe.wait_ge(*signal("m_e", 2))
                    if k == 1 and hd:
                        page_values(hd - 1)
                    if k % 2:
                        quad_values(hd, k // 2)
                    if k == 7:
                        quad_values(hd, 4)
            page_values(B - 1)
            pe.wait_ge(sem("n_out"), 64)

            pe.wait_ge(sem("rows_in"), 16 * 6)
            for br in range(2):
                for b in range(B):
                    w_ = slc[0:1, b, NPG, :] if br == 0 else wsc[0:1, b, NW, :]
                    mm(bank[7][:, 64 + 64 * br + b * H:64 + 64 * br + (b + 1) * H], vnew[0:1, br, b, :], w_, False,
                       br == 1 and b == B - 1, skip_group_check=True)
            pe.wait_ge(*signal("s_sp", 1))
            mm(bank[4][:, 0:B * 24], ones[0:1, :], grow[0:1].rearrange("p b h r -> p (b h r)")).then_inc(sem("samples_pe"), 1)
            pe.wait_ge(*signal("v_sq", 1))
            mm(bank[3][:, 0:64], ones, ofs[:, 9, :]).then_inc(sem("samples_pe"), 1)

            pe.wait_ge(sem("mix_ready"), 1)
            for k in range(KD):
                if k >= 2:
                    pe.wait_ge(sem("mixT_ev"), k - 1)
                for t in range(NT):
                    s = (o_sb, o_n)[k // 4][:, t, (k % 4) * P:(k % 4 + 1) * P]
                    ins = tr(bank[k % 2][:, t * P:(t + 1) * P], s)
                ins.then_inc(sem("mixT_mm"), 1)

            pe.wait_ge(sem("mixT_ev"), KD)
            pe.wait_ge(sem("mix_ready"), 2)
            pe.wait_ge(sem("wout_lo"), 4)
            for t in range(T5):
                for c in range(2):
                    n = 2 * t + c
                    if n >= 4:
                        pe.wait_ge(sem("res_ev"), n - 3)
                    for k in range(KD):
                        for j, (h_, w_) in enumerate(((hT_r, wout_hi_r), (hT_r, wout_r), (hT_lo_r, wout_hi_r))):
                            ins = mm(bank[4 + n % 4][0:rows[t], :], h_[:, k, t * P:t * P + rows[t]],
                                     w_[:, k, c * 512:(c + 1) * 512], k == 0 and j == 0, k == KD - 1 and j == 2)
                    ins.then_inc(sem("out_mm"), 1)
            norm_transposes(h2, 1)
            pe.wait_ge(sem("hT_ev"), 18)
            pe.wait_ge(sem("res_ev"), 10)

            def products(out, u, moving, moving_lo, k0, first, last):
                for k in range(8):
                    for n, (w_, m_) in enumerate(((w_hi_r, moving), (w_hi_r, moving_lo), (w_lo_r, moving))):
                        for half in range(2):
                            ins = mm(out[half][:, 0:HALF], w_[u][:, k, :], m_[:, k0 + k, half * HALF:(half + 1) * HALF],
                                     first and k == 0 and n == 0, last and k == 7 and n == 2)
                ins.then_inc(sem(f"w_used{u}"), 1)

            def down_products(v, i, part):
                pe.wait_ge(sem(f"dn_ev{v}"), i + 4 * part + 1)
                for u in range(2):
                    pe.wait_ge(sem(f"w_lo{u}"), i * 2 + (v + 16 * part + 8 + W0) + 1 + 1)
                    products((bank[v], bank[2 + v]), u, aT_r, aT_lo_r, 8 * u, u == 0, u == 1)

            def down_transposes(v, i, part):
                pe.wait_ge(sem(f"dn_ev{v}"), i + 4 * part + 1 + 1)
                pe.wait_ge(sem(f"y_ev{v}"), i + 4 * part + 1)
                for t in range(NT):
                    tr(bank[4 + v][:, t * P:(t + 1) * P], yT[v][:, t * P:(t + 1) * P])
                tr(bank[6 + v][0:B, 0:P], yT[v][:, SEQ:TOK]).then_inc(sem(f"y_mm{v}"), 1)

            for part in range(2):
                if part:
                    pe.wait_ge(sem("y_ev0"), 4 + 1)
                    pe.wait_ge(sem("y_ev1"), 4 + 1)
                with pe.Fori(0, FH // 2) as i:
                    for u in range(2):
                        pe.wait_ge(sem(f"w_lo{u}"), i + (16 * part + W0) + 1 + 1)
                        pe.wait_ge(sem(f"up_ev{u}"), i + 8 * part + 1)
                        products((bank[4 + u], bank[6 + u]), u, hT_r, hT_lo_r, 0, True, True)
                for u in range(2):
                    pe.wait_ge(sem(f"a_ready{u}"), FH // 2 * (part + 1) + 1)
                last = KD // 2 - 1
                down_products(0, 0, part)
                with pe.Fori(0, last) as i:
                    down_products(1, i, part)
                    down_transposes(0, i, part)
                    down_products(0, i + 1, part)
                    down_transposes(1, i, part)
                down_products(1, last, part)
                down_transposes(0, last, part)
                down_transposes(1, last, part)

        @block.scalar
        def _(act):
            S = nc.scalar
            prime(act, "act")
            chain = Chain(act, sem("act_steps"))

            eps = K("eps")
            act.wait_ge(sem("x_in"), 32)
            act.wait_ge(sem("st_set"), 1)
            for t in (2, 3):
                chain(S.activation(h[:, t, :], x[:, t, :], ACT.Square, accum_out=st[:, t:t + 1]))
            act.wait_ge(sem("const_in"), 16)
            act.wait_ge(sem("ss"), 1)
            S.activation(st[:, 8:13], st[:, 0:5], ACT.Sqrt, bias=eps, scale=1.0 / D).then_inc(sem("rt"), 1)
            def win_high(u, i):
                act.wait_ge(sem(f"win_in{u}"), i * 16 + 16)
                act.wait_ge(sem(f"win_free{u}"), i + 1)
                S.activation(win_hi_r[u], win[u], ACT.Copy).then_inc(sem(f"w_hi{u}"), 1)

            def z_out(u, i, turn, col):
                for t in (1, 3):
                    act.wait_ge(sem("z_mm"), i * (2 * T5) + (2 * T5 * turn + u * T5 + t) + 1)
                    S.activation(z[:, t, ds(i * (2 * CB) + (u * CB + col), CB)], bank[t][:, 0:CB], ACT.Copy).then_inc(sem(f"z_ev{t}"), 1)

            def gained_high(transposed, first, g0):
                for k in range(KD):
                    act.wait_ge(sem(transposed), first + k + 1)
                    S.activation(hT_r[:, k, 0:SEQ], bank[k % 2][:, :], ACT.Copy, scale=vcol[:, g0 + k:g0 + k + 1]).then_inc(sem("hT_high"), 1)

            win_high(0, 0)
            act.wait_ge(sem("vcol_ev"), 1)
            gained_high("hT_mm", 0, 0)
            wb, wo = A["state_nsa_win_kv"][0], O["win_s"][0]
            for b in range(B):
                act.dma_start(wo[b, 0:WIN - 1].rearrange("(o s) k h d -> o (s k h d)", o=1),
                    wb[b, 1:WIN].rearrange("(o s) k h d -> o (s k h d)", o=1)).then_inc(sem("kv_out"), 16)
            for turn, turns, col in COLUMNS:
                more = turn + turns < NCB // 2
                with act.Fori(0, turns if more else turns - 1) as i:
                    win_high(1, i + turn)
                    z_out(0, i, turn, col)
                    win_high(0, i + turn + 1)
                    z_out(1, i, turn, col)
                if not more:
                    win_high(1, NCB // 2 - 1)
                    z_out(0, turns - 1, turn, col)
                    z_out(1, turns - 1, turn, col)
            for t in range(T5):
                act.wait_ge(sem(f"z_ev{t}"), NCB + 1)
            act.dma_start(O["sb_p"][0, 0].rearrange("(t p) k h d -> p t (k h d)", p=P), z[:, 0:NT, O_KS:O_KS + 1024]).then_inc(sem("sb_stored"), 16)
            act.dma_start(O["sb_s"][0].rearrange("b o k h d -> (b o) (k h d)"), z[0:B, NT, O_KS:O_KS + 1024]).then_inc(sem("kv_out"), 16)
            act.wait_ge(sem("rope_done"), T5)
            act.dma_start(O["cmp_p"][0, 0].rearrange("(t p) k h d -> p t (k h d)", p=P), z[:, 0:NT, O_C:O_C + 256]).then_inc(sem("cmp_stored"), 16)
            for nm, o in (("slc_p", O_S), ("win_p", O_W)):
                act.dma_start(O[nm][0, 0].rearrange("(t p) k h d -> p t (k h d)", p=P), z[:, 0:NT, o:o + 256]).then_inc(sem("kv_out"), 16)
            for nm, o in (("cmp_s", O_C), ("slc_s", O_S)):
                act.dma_start(O[nm][0].rearrange("b o k h d -> (b o) (k h d)"), z[0:B, NT, o:o + 256]).then_inc(sem("kv_out"), 16)
            act.dma_start(wo[:, WIN - 1].rearrange("b k h d -> b (k h d)"), z[0:B, NT, O_W:O_W + 256]).then_inc(sem("kv_out"), 16)
            act.wait_ge(sem("qscaled"), 1)
            act.dma_start(sbq_dram, qsc[0:B, :]).then_inc(sem("sbq_out"), 16)
            dst = [sbqT[:, j] for j in range(4)] + [sbkT[:, j] for j in range(4)] + [nqT[:, j] for j in range(4)] + [ksT, kwT]
            for j in range(1, 14, 2):
                act.wait_ge(sem("qkT_mm"), j + 1)
                q = j < 4 or 8 <= j < 12
                S.activation(dst[j], bank[j % 4][:, :], ACT.Copy, scale=SCALE if q else 1.0).then_inc(sem("qkT_ev1"), 1)
            S.activation(z[:, :, O_G:O_G + 24], z[:, :, O_G:O_G + 24], ACT.Exp, scale=-1.0).then_inc(sem("gates_e"), 1)
            act.wait_ge(sem("snew"), 2)
            for br in range(2):
                act.dma_start(newrow[0:1, br].rearrange("p b h -> p (b h)"), snew[0:B, br, :]).then_inc(sem("rows_in"), 16)
            for br, o in enumerate((O_S, O_W)):
                act.dma_start(vnew[0:1, br].rearrange("p b c -> p (b c)"), z[0:B, NT, o + P:o + 2 * P]).then_inc(sem("rows_in"), 16)
            act.wait_ge(sem("gates"), 1)
            act.dma_start(grow[0:1].rearrange("p b h r -> p (b h r)"), z[0:B, NT, O_G:O_G + 24]).then_inc(sem("rows_in"), 16)
            act.dma_start(st[0:1, 208:209], A["g_final"].rearrange("(o d) -> o d", o=1)[:, 0:1]).then_inc(sem("rows_in"), 16)

            act.wait_ge(sem("pebias"), 2)

            def keys_out(i, u, q):
                n = 5 * u + q
                act.wait_ge(sem(f"kq_mm{n % 2}"), i * 5 + n // 2 + 1 + 1)
                act.wait_ge(sem("qs_mm"), i * 10 + n + 1)
                S.activation(kqT.rearrange("p j s -> p (j s)"), bank[6][:, :], ACT.Copy).then_inc(sem("kq_ev"), 1)

            def compress(c, n, between):
                nb = n - 1
                for kv in range(2):
                    for s in range(4):
                        act.wait_ge(sem("xT_mm"), c * 8 + kv * 4 + s + 1)
                        S.activation(xT[kv][:, 2 * s:2 * s + 2, :, 0:n],
                                     bank[s % 2].rearrange("p (m h c) -> p m h c", m=2, h=2)[:, :, :, 0:n],
                                     ACT.Copy).then_inc(sem(f"xT_ev{s % 2}"), 1)
                        if s in (1, 3):
                            between()
                    act.wait_ge(sem(f"hid_mm{kv}"), c + 1)
                    act.wait_ge(sem(f"hid_ready{kv}"), c + 1)
                    S.activation(hid[kv][:, :, 0:nb], bank[2 + kv][:, 0:KVH * nb].rearrange("p (h c) -> p h c", h=KVH),
                                 ACT.Exp, bias=pebias[:, 2 + kv:3 + kv], scale=-1.0).then_inc(sem(f"hid_e{kv}"), 1)

            with act.Fori(0, 4) as i:
                for u in range(2):
                    c = i * 2 + u
                    todo = [lambda q=q: keys_out(i, u, q) for q in range(4)]
                    compress(c, NCH, lambda: todo.pop(0)())
                    keys_out(i, u, 4)
                    act.wait_ge(sem("qs_mm"), i * 10 + 5 * u + 5 + 1)
                    S.activation(slc[:, ds(c, 1), 0:NPG, :].rearrange("p o n j -> p (o n j)"), bank[7][:, 0:NPG * H], ACT.Copy)
                    S.activation(wsc[:, ds(c, 1), 0:NW, :].rearrange("p o n j -> p (o n j)"), bank[7][:, NPG * H:(NPG + NW) * H],
                                 ACT.Copy).then_inc(sem("qs_ev"), 1)
            compress(B, NCP + 1, lambda: None)
            act.wait_ge(sem("kvc_ev0"), B + 1 + 1)
            act.wait_ge(sem("kvc_ev1"), B + 1 + 1)

            def cp_exp(i):
                act.wait_ge(sem("cp_max"), i + 1)
                S.activation(pbuf[:, 0, 0:H * NCP], pbuf[:, 0, 0:H * NCP], ACT.Exp).then_inc(sem("cp_exp"), 1)

            def cp_pT(i):
                for c in range(2):
                    act.wait_ge(sem("cp_tr"), 2 * i + c + 1)
                    if c == 0 and i:
                        act.wait_ge(sem("cp_pv"), i)
                    S.activation(ptb[0:NCP, c, :], bank[6 + c][0:NCP, :], ACT.Copy).then_inc(sem("cp_pT"), 1)

            def samples_exp(br):
                act.wait_ge(*signal("m_sub", br + 1))
                f = (wsc, slc)[br].rearrange("p b n j -> p (b n j)")
                S.activation(f, f, ACT.Exp).then_inc(sem("samples_act"), 1)

            cp_exp(0)
            act.wait_ge(*signal("s_abs", 1))
            f = sps.rearrange("p b n j -> p (b n j)")
            chain(S.activation(f, f, ACT.Exp, scale=-1.0))
            S.activation(f, f, ACT.Ln, bias=K("one")).then_inc(sem("samples_act"), 1)
            act.wait_ge(*signal("c_nm", 1))
            S.activation(s64[0:64, 1, 0:NC], bank[2][0:64, 0:NC], ACT.Exp, bias=st[0:64, 40:41], accum_out=st[0:64, 41:42]).then_inc(sem("samples_act"), 1)
            samples_exp(0)
            cp_pT(0)
            cp_exp(1)
            cp_pT(1)
            cp_exp(2)
            cp_pT(2)
            cp_exp(3)
            cp_pT(3)
            samples_exp(1)
            act.wait_ge(*signal("s_d", 1))
            f = sbs.rearrange("p b n j -> p (b n j)")
            S.activation(f, f, ACT.Exp).then_inc(sem("samples_act"), 1)

            def sb_ln(hd, i):
                m, n = 4 * hd + 3 - i, SEQ - i * P
                act.wait_ge(sem("sb_qk"), m + 1)
                if m >= 2:
                    act.wait_ge(sem("sb_sp"), m - 1)
                e = ebuf[:, m % 2, 0:n]
                chain(S.activation(e, bank[m % 2][:, 0:n], ACT.Abs))
                chain(S.activation(e, e, ACT.Exp, scale=-1.0))
                S.activation(e, e, ACT.Ln, bias=K("one")).then_inc(sem("sb_ln"), 1)

            def sb_exp(hd, i):
                m, n = 4 * hd + 3 - i, SEQ - i * P
                act.wait_ge(sem("sb_c"), m + 1)
                if m >= 2:
                    act.wait_ge(sem("sb_pv"), m - 1)
                S.activation(abuf[:, m % 2, 0:n], bank[m % 2][:, 0:n], ACT.Exp).then_inc(sem("sb_a"), 1)

            def n_exp(n):
                i = n % 4
                act.wait_ge(sem("n_max"), n + 1)
                if n >= 2:
                    act.wait_ge(sem("n_tr"), n - 1)
                if n >= 4:
                    act.wait_ge(sem("n_out"), n - 3)
                S.activation(pbuf[:, n % 2, 0:(i + 1) * P], bank[3 + n % 2][:, 0:(i + 1) * P], ACT.Exp,
                             bias=st[:, 160 + n % 4:161 + n % 4], accum_out=st[:, 164 + n % 4:165 + n % 4]).then_inc(sem("n_exp"), 1)

            def n_pT(n):
                i = n % 4
                act.wait_ge(sem("n_tr"), n + 1)
                if n >= 2:
                    act.wait_ge(sem("n_pv"), n - 1)
                S.activation(ptb[:, n % 2, 0:(i + 1) * P], bank[5][:, 0:(i + 1) * P], ACT.Copy).then_inc(sem("n_pT"), 1)

            act.wait_ge(sem("cp_pv"), NT)
            S.preload_act_table_set("natural_log_exp_and_others")
            for n in range(8 * H + 1):
                hd, k = n // 8, n % 8
                if n < 8 * H:
                    if k == 0:
                        sb_ln(hd, 3)
                    n_exp(n)
                    if k == 0:
                        sb_ln(hd, 2)
                    if k in (2, 3):
                        sb_ln(hd, 3 - k)
                    if 1 <= k < 5:
                        sb_exp(hd, 4 - k)
                if n >= 1:
                    n_pT(n - 1)
                if k == 6:
                    act.wait_ge(sem("sb_pv"), 4 * hd + 4)
                    S.activation(o_sb[:, :, hd * DH:(hd + 1) * DH], bank[2][:, 0:256].rearrange("p (t d) -> p t d", t=NT), ACT.Copy).then_inc(sem("sb_out"), 1)

            act.wait_ge(sem("wout_in"), 64)
            for k in range(0, KD, 2):
                S.activation(wout_hi_r[:, k:k + 2], wout[:, k:k + 2], ACT.Copy).then_inc(sem("wout_hi"), 1)
            act.wait_ge(*signal("v_st", 1))
            S.activation(st[:, 64:80], st[:, 48:64], ACT.Sqrt, bias=eps, scale=1.0 / 512).then_inc(sem("samples_act"), 1)
            act.wait_ge(*signal("mix_ss", 1))
            S.activation(st[:, 96:104], st[:, 88:96], ACT.Sqrt, bias=eps, scale=1.0 / 512).then_inc(sem("samples_act"), 1)
            gained_high("mixT_mm", 0, 16)
            act.wait_ge(sem("ss"), 2)
            S.activation(st[:, 8:12], st[:, 0:4], ACT.Sqrt, bias=eps, scale=1.0 / D).then_inc(sem("rt"), 1)
            act.wait_ge(sem("ss"), 3)
            S.activation(st[0:B, 12:13], st[0:B, 4:5], ACT.Sqrt, bias=eps[0:B], scale=1.0 / D).then_inc(sem("rt"), 1)
            def high_parts(u, n):
                act.wait_ge(sem(f"w_in{u}"), (n + 1) * 16)
                act.wait_ge(sem(f"w_used{u}"), n + 1)
                S.activation(w_hi_r[u], w_raw[u], ACT.Copy).then_inc(sem(f"w_hi{u}"), 1)

            act.wait_ge(sem("mixT_ev"), KD)
            high_parts(0, 0)
            gained_high("hT_mm", 9, 8)
            for part in range(2):
                with act.Fori(0, FH // 2) as i:
                    for u in range(2):
                        high_parts(1 - u, i + (u + 16 * part))
                        act.wait_ge(sem(f"w_used{u}"), i + 16 * part + 1 + 1)
                        act.wait_ge(sem(f"a_ready{u}"), i + 8 * part + 1)
                        S.activation(relu[:, u, 0:HALF], bank[4 + u][:, 0:HALF], ACT.Relu)
                        S.activation(relu[:, u, HALF:TOK], bank[6 + u][:, 0:HALF], ACT.Relu).then_inc(sem(f"up_ev{u}"), 1)
                with act.Fori(0, KD - part) as i:
                    high_parts(1, i + (16 * part + 8))
                    high_parts(0, i + (16 * part + 9))
            high_parts(1, 31)
            for u in range(2):
                act.wait_ge(sem(f"y_ev{u}"), 8 + 1)
            for t in (2, 3):
                chain(S.activation(h2[:, t, :], x[:, t, :], ACT.Square, accum_out=st[:, t:t + 1]))
            act.wait_ge(sem("ss"), 4)
            S.activation(st[:, 8:13], st[:, 0:5], ACT.Sqrt, bias=eps, scale=1.0 / D).then_inc(sem("rt"), 1)
            act.wait_ge(sem("kv_out"), 16 * (B + 6))
            act.wait_ge(sem("cmp_stored"), 16)
            act.wait_ge(sem("sbq_out"), 16)

        @block.vector
        def _(dve):
            V = nc.vector
            prime(dve, "dve")
            chain = Chain(dve, sem("dve_steps"))

            def squares(dst, t, after):
                ins = V.tensor_tensor_reduce(dst[0:rows[t], t, :], x[0:rows[t], t, :], x[0:rows[t], t, :], 1.0, 0.0,
                                             ALU.mult, ALU.add, st[0:rows[t], t:t + 1])
                after(ins)

            def row_scales(dst, tiles, turn):
                lo, hi = tiles[0], tiles[-1] + 1
                dve.wait_ge(sem("rt"), turn)
                chain(V.reciprocal(st[:, 16 + lo:16 + hi], st[:, 8 + lo:8 + hi]))
                for t in tiles:
                    ins = V.tensor_scalar(dst[0:rows[t], t, :], x[0:rows[t], t, :], st[0:rows[t], 16 + t:17 + t], None, ALU.mult)
                    if t < hi - 1:
                        chain(ins)
                return ins

            def gained(g0, turn):
                low = (hT_lo1_r, hT_lo_r)[turn]
                for k in range(KD):
                    dve.wait_ge(sem("hT_high"), 16 * turn + k + 1)
                    V.scalar_tensor_tensor(out=low[:, k, 0:SEQ], in0=bank[k % 2][:, :], scalar=vcol[:, g0 + k:g0 + k + 1],
                                           in1=hT[:, k, 0:SEQ], op0=ALU.mult, op1=ALU.subtract).then_inc(sem("hT_ev"), 1)

            def gained_samples(g0, turn):
                low = (hT_lo1_r, hT_lo_r)[turn]
                dve.wait_ge(sem("hT_mm"), 9 * turn + 9)
                v = act2[:, 0:64].rearrange("p (k b) -> p k b", k=KD)
                chain(V.tensor_tensor(v, bank[2][:, 0:64].rearrange("p (k b) -> p k b", k=KD),
                                      over(vcol[:, g0:g0 + KD], 2, B), ALU.mult))
                chain(V.tensor_copy(hT_r[:, :, SEQ:TOK], v))
                V.tensor_tensor(low[:, :, SEQ:TOK], v, hT[:, :, SEQ:TOK], ALU.subtract).then_inc(sem("hT_ev"), 1)

            chain(V.memset(zero[:, :], 0.0))
            V.memset(st[:, :], 1.0).then_inc(sem("st_set"), 1)
            dve.wait_ge(sem("st_set"), 1)
            dve.wait_ge(sem("x_in"), 32)
            for t in (0, 1):
                squares(h, t, chain)
            squares(h, NT, lambda ins: ins.then_inc(sem("ss"), 1))
            row_scales(h, range(NT), 1).then_inc(sem("h_ready"), 1)
            row_scales(h, [NT], 1).then_inc(sem("h_ready"), 1)
            dve.wait_ge(sem("vcol_mm"), 1)
            V.tensor_copy(vcol[:, :], bank[3][:, 0:56]).then_inc(sem("vcol_ev"), 1)
            dve.wait_ge(sem("vcol_ev"), 1)
            gained(0, 0)
            gained_samples(0, 0)
            dve.wait_ge(sem("z_zero"), 1)
            def win_low(u, i):
                dve.wait_ge(sem(f"w_hi{u}"), i + 1)
                V.tensor_tensor(win_r[u], win[u], win_hi[u], ALU.subtract).then_inc(sem(f"w_lo{u}"), 1)

            def z_out(u, i, turn, col, tiles=(0, 2, 4)):
                for t in tiles:
                    dve.wait_ge(sem("z_mm"), i * (2 * T5) + (2 * T5 * turn + u * T5 + t) + 1)
                    V.tensor_copy(z[0:rows[t], t, ds(i * (2 * CB) + (u * CB + col), CB)], bank[t][0:rows[t], 0:CB]).then_inc(sem(f"z_ev{t}"), 1)
                dve.wait_ge(sem("z_ev4"), i * 2 + (2 * turn + u) + 1 + 1)
                V.memset(st[0:1, 202:203], 0.0).then_inc(sem(f"win_free{u}"), 1)

            def rotary(t):
                dve.wait_ge(sem(f"z_ev{t}"), FIRST + 1)
                cos, sin = (K(n)[:, t * DH:(t + 1) * DH] for n in ("cos", "sin"))
                qn = z[:, t, O_QN:O_QN + 512].rearrange("p (h d) -> p h d", h=H)
                kk = z[:, t, O_C:O_C + 768].rearrange("p (r k h d) -> p r k h d", r=3, k=2, h=2)[:, :, 0]
                a8, b8 = (v.rearrange("p (h d) -> p h d", h=H) for v in (ropeA, ropeB))
                a6, b6 = (v[:, 0:384].rearrange("p (r h d) -> p r h d", r=3, h=2) for v in (ropeA, ropeB))
                chain(V.tensor_tensor(a8, qn, over(cos, 1, H), ALU.mult))
                chain(V.tensor_tensor(b8[:, :, 0:32], qn[:, :, 32:64], over(sin[:, 0:32], 1, H), ALU.mult))
                chain(V.tensor_tensor(b8[:, :, 32:64], qn[:, :, 0:32], over(sin[:, 32:64], 1, H), ALU.mult))
                qp = z[:, t, O_QN:O_QN + 512].rearrange("p (g k d) -> p k g d", g=G, k=KVH)
                chain(V.tensor_tensor(qp, *(v.rearrange("p (k g) d -> p k g d", k=KVH) for v in (a8, b8)), ALU.add))
                cos6, sin6 = over(over(cos, 1, 2), 1, 3), over(over(sin, 1, 2), 1, 3)
                chain(V.tensor_tensor(a6, kk, cos6, ALU.mult))
                chain(V.tensor_tensor(b6[:, :, :, 0:32], kk[:, :, :, 32:64], sin6[:, :, :, 0:32], ALU.mult))
                chain(V.tensor_tensor(b6[:, :, :, 32:64], kk[:, :, :, 0:32], sin6[:, :, :, 32:64], ALU.mult))
                V.tensor_tensor(kk, a6, b6, ALU.add).then_inc(sem("rope_done"), 1)
                dve.wait_ge(sem("rope_done"), t + 1)

            (turn, turns, col), (turn2, turns2, col2) = COLUMNS
            with dve.Fori(0, turns) as i:
                win_low(1, i)
                z_out(0, i, turn, col)
                win_low(0, i + 1)
                z_out(1, i, turn, col)
            for n in range(2 * turns2):
                if n < 2 * turns2 - 1:
                    win_low((n + 1) % 2, turn2 + (n + 1) // 2)
                rotary(n)
                if n == NT - 1:
                    rotary(NT)
                z_out(n % 2, n // 2, turn2, col2)
            chain(V.memset(qbd[:, :, :], 0.0))
            for t in range(T5):
                dve.wait_ge(sem(f"z_ev{t}"), NCB + 1)
            dve.wait_ge(sem("rope_done"), T5)
            zs = z[0:B, NT]
            chain(V.tensor_scalar(qsc[0:B, :], zs[:, O_QS:O_QS + 512], SCALE, None, ALU.mult))
            V.memset(st[0:1, 204:205], 0.0).then_inc(sem("qscaled"), 1)
            for j in range(0, 14, 2):
                dve.wait_ge(sem("qkT_mm"), j + 1)
                q = j < 4 or 8 <= j < 12
                dst = ([sbqT[:, n] for n in range(4)] + [sbkT[:, n] for n in range(4)] + [nqT[:, n] for n in range(4)] + [ksT, kwT])[j]
                if q:
                    ins = V.tensor_scalar(dst, bank[j % 4][:, :], SCALE, None, ALU.mult)
                else:
                    ins = V.tensor_copy(dst, bank[j % 4][:, :])
                ins.then_inc(sem("qkT_ev0"), 1)
            dve.wait_ge(sem("qkT_mm"), 15)
            for kh in range(2):
                lo = kh * DH
                ins = V.tensor_scalar(qbd[lo:lo + DH, :, kh * G:(kh + 1) * G],
                                      bank[4][lo:lo + DH, 0:32].rearrange("p (g b) -> p b g", g=G), SCALE, None, ALU.mult)
                if kh == 0:
                    chain(ins)
            ins.then_inc(sem("qkT_ev0"), 1)
            for br, o in enumerate((O_S, O_W)):
                qn = zs[:, O_QN:O_QN + 512].rearrange("p (g k d) -> p k g d", k=2, g=G)
                kn = over(zs[:, o:o + P].rearrange("p (k d) -> p k d", k=2), 2, G)
                chain(V.tensor_tensor(ropeA[0:B].rearrange("p (k g d) -> p k g d", k=2, g=G), qn, kn, ALU.mult))
                chain(V.tensor_reduce(ropeB[0:B, 0:H], ropeA[0:B].rearrange("p (h d) -> p h d", h=H), AX.X, ALU.add))
                V.tensor_scalar(snew[0:B, br, :], ropeB[0:B, 0:H], SCALE, None, ALU.mult).then_inc(sem("snew"), 1)
                dve.wait_ge(sem("snew"), br + 1)
            dve.wait_ge(sem("gates_e"), 1)
            g = z[:, :, O_G:O_G + 24]
            chain(V.tensor_scalar(g, g, 1.0, None, ALU.add))
            V.reciprocal(g, g).then_inc(sem("gates"), 1)
            dve.wait_ge(sem("pe_mm"), 1)
            V.tensor_copy(pebias[:, 0:2], bank[6][:, 0:2]).then_inc(sem("pebias"), 1)
            V.tensor_scalar(pebias[:, 2:4], bank[6][:, 0:2], -1.0, None, ALU.mult).then_inc(sem("pebias"), 1)
            dve.wait_ge(sem("pebias"), 2)
            dve.wait_ge(sem("gates"), 1)

            def silu(c, kv, n):
                nb = n - 1
                dve.wait_ge(sem(f"hid_e{kv}"), c + 1)
                e = hid[kv][:, :, 0:nb]
                chain(V.tensor_scalar(e, e, 1.0, None, ALU.add))
                chain(V.reciprocal(e, e))
                dve.wait_ge(sem(f"w2_mm{kv}"), c + 1)
                hp = bank[2 + kv][:, 0:KVH * nb].rearrange("p (h c) -> p h c", h=KVH)
                V.scalar_tensor_tensor(out=hid[2 + kv][:, :, 0:nb], in0=hp, scalar=pebias[:, kv:kv + 1], in1=e,
                                       op0=ALU.add, op1=ALU.mult).then_inc(sem(f"hid_ready{kv}"), 1)

            def compressed_out(c, dst_k, dst_v, n):
                dve.wait_ge(sem("w2_mm0"), c + 1 + 1)
                V.tensor_copy(dst_k, bank[4][:, 0:n - 1]).then_inc(sem("kvc_ev0"), 1)
                dve.wait_ge(sem("w2_mm1"), c + 1 + 1)
                V.tensor_copy(dst_v, bank[5][0:n - 1, 0:P]).then_inc(sem("kvc_ev1"), 1)

            def sb_keys(i, u, first, last):
                if first == 0:
                    dve.wait_ge(sem(f"qb_in{u}"), i * 16 + 16)
                for p in range(first, last):
                    k = kring[p % 8]
                    dve.wait_ge(sem(f"ring_in{p % 8}"), (i * 4 + (2 * u + p // 8 + 1)) * 16)
                    if p < NPG - 1:
                        chain(V.tensor_tensor(k, k, qb[:, u, :], ALU.mult))
                    else:
                        V.tensor_tensor(k, k, qb[:, u, :], ALU.mult).then_inc(sem(f"qb_free{u}"), 1)
                        dve.wait_ge(sem(f"qb_free{u}"), i + 1 + 1)
                    V.tensor_reduce(raw_scores(ds(i, 1), u)[:, p, :], k.rearrange("p (h d) -> p h d", h=H),
                                    AX.X, ALU.add).then_inc(sem(f"ring_free{p % 8}"), 1)

            dve.wait_ge(sem("cmp_stored"), 16)
            with Turns(chain, 4, 2 * (NPG - 1 + 4)) as i:
                for u in range(2):
                    c = i * 2 + u
                    sb_keys(i, u, 0, 8)
                    silu(c, 0, NCH)
                    sb_keys(i, u, 8, 14)
                    silu(c, 1, NCH)
                    sb_keys(i, u, 14, 16)
                    compressed_out(c, kc[:, ds(c, 1), 0:NC].rearrange("p o c -> p (o c)"), vc[0:NC, ds(c, 1), :].rearrange("p o c -> p (o c)"), NCH)
            silu(B, 0, NCP + 1)
            silu(B, 1, NCP + 1)
            compressed_out(B, kc[:, B, 0:NCP], vc[0:NCP, B, :], NCP + 1)
            for k in range(8):
                dve.wait_ge(sem(f"ring_free{k}"), 2 * B + 1)

            dve.wait_ge(sem("kvc_ev0"), B + 1 + 1)
            dve.wait_ge(sem("kvc_ev1"), B + 1 + 1)
            dve.wait_ge(sem("qs_ev"), B + 1)
            pc = pbuf[:, 0, 0:H * NCP].rearrange("p (h c) -> p h c", h=H)

            def cp_max(i):
                dve.wait_ge(sem("cp_qk"), i + 1)
                if i:
                    dve.wait_ge(sem("cp_tr"), 2 * i)
                add = over(K("cadd")[:, i * NCP:(i + 1) * NCP], 1, H)
                for kh in range(KVH):
                    hs = slice(G * kh, G * kh + G)
                    chain(V.tensor_tensor(pc[:, hs], bank[4 + kh][:, 0:G * NCP].rearrange("p (h c) -> p h c", h=G), add[:, hs], ALU.add))
                chain(V.tensor_reduce(st[:, 104:112], pc, AX.X, ALU.max))
                V.tensor_tensor(pc, pc, over(st[:, 104:112], 2, NCP), ALU.subtract).then_inc(sem("cp_max"), 1)

            def cp_soft(i):
                dve.wait_ge(sem("cp_exp"), i + 1)
                mul = over(K("cmul")[:, i * NCP:(i + 1) * NCP], 1, H)
                chain(V.tensor_tensor(pc, pc, mul, ALU.mult))
                chain(V.tensor_reduce(st[:, 112:120], pc, AX.X, ALU.add))
                chain(V.tensor_scalar(st[:, 112:120], st[:, 112:120], TINY, None, ALU.max))
                chain(V.reciprocal(st[:, 120:128], st[:, 112:120]))
                gate = z[:, i, O_G:O_G + 24].rearrange("p (h r) -> p h r", r=3)[:, :, 0]
                chain(V.tensor_tensor(st[:, 120:128], st[:, 120:128], gate, ALU.mult))
                V.tensor_tensor(pc, pc, over(st[:, 120:128], 2, NCP), ALU.mult).then_inc(sem("cp_soft"), 1)

            def cp_out(i):
                dve.wait_ge(sem("cp_pv"), i + 1)
                V.tensor_copy(o_n[:, i, :], bank[i % 2][:, :]).then_inc(sem("cp_out"), 1)

            def row_max(br):
                sc = (wsc, slc)[br]
                V.tensor_reduce(s64[:, 7, 0:64].rearrange("p (b j) -> p b j", b=B), sc.rearrange("p b n j -> p b j n"), AX.X, ALU.max).then_inc(sem("samples_dve"), 1)

            def row_max_diagonal(br):
                dve.wait_ge(*signal("m_T", br + 1))
                chain(V.tensor_reduce(st[0:64, 44:45], bank[3][0:64, 0:P], AX.X, ALU.max))
                V.tensor_scalar(s64[0:64, 7, 64:128], ident[0:64, 0:64], st[0:64, 44:45], None, ALU.mult).then_inc(sem("samples_dve"), 1)

            def row_max_subtract(br):
                sc, n = ((wsc, NW + 1), (slc, NPG + 1))[br]
                dve.wait_ge(*signal("m_b", br + 1))
                chain(V.tensor_copy(s64[:, 8, 0:64], bank[3][:, 0:64]))
                V.tensor_tensor(sc, sc, over(s64[:, 8, 0:64].rearrange("p (b j) -> p b j", b=B), 2, n), ALU.subtract).then_inc(sem("samples_dve"), 1)

            def row_sum(br):
                sc = (wsc, slc)[br]
                dve.wait_ge(*signal("m_e", br + 1))
                V.tensor_reduce(s64[:, 8, 64:128].rearrange("p (b j) -> p b j", b=B), sc.rearrange("p b n j -> p b j n"), AX.X, ALU.add).then_inc(sem("samples_dve"), 1)

            def row_reciprocal(br):
                dve.wait_ge(*signal("m_den", br + 1))
                V.reciprocal(ofs[:, 6 - br, :], bank[3][:, 0:64]).then_inc(sem("samples_dve"), 1)

            dve.wait_ge(sem("rows_in"), 96)
            chain(V.memset(slc[:, :, NPG, :], NEG))
            chain(V.memset(wsc[:, :, NW, :], NEG))
            chain(V.tensor_copy(slc[0:1, :, NPG, :], newrow[0:1, 0]))
            chain(V.tensor_copy(wsc[0:1, :, NW, :], newrow[0:1, 1]))
            chain(V.memset(wsc[0:1, :, 0, :], NEG))
            row_max(0)
            dve.wait_ge(*signal("c_sc", 1))
            V.tensor_copy(s64[0:NC, 0, 0:64], bank[2][0:NC, 0:64]).then_inc(sem("samples_dve"), 1)
            cp_max(0)
            row_max_diagonal(0)
            flat = lambda a: a.rearrange("p b n j -> p (b n j)")
            raw = z[:, 0:NT, O_C:O_C + 256]
            chain(V.tensor_copy(flat(sbs).rearrange("p (t c) -> p t c", t=NT), raw))
            V.scalar_tensor_tensor(out=flat(sps), in0=flat(sbs), scalar=-1.0, in1=flat(sbs), op0=ALU.mult, op1=ALU.max).then_inc(sem("samples_dve"), 1)
            dve.wait_ge(*signal("c_scT", 1))
            V.tensor_reduce(st[0:64, 40:41], bank[2][0:64, 0:NC], AX.X, ALU.max, negate=True).then_inc(sem("samples_dve"), 1)
            row_max_subtract(0)
            cp_soft(0)
            dve.wait_ge(*signal("c_e", 1))
            chain(V.tensor_scalar(st[0:64, 41:42], st[0:64, 41:42], TINY, None, ALU.max))
            chain(V.reciprocal(st[0:64, 42:43], st[0:64, 41:42]))
            V.tensor_scalar(s64[0:64, 2, 0:NC], s64[0:64, 1, 0:NC], st[0:64, 42:43], None, ALU.mult).then_inc(sem("samples_dve"), 1)
            dve.wait_ge(*signal("s_ln", 1))
            V.scalar_tensor_tensor(out=flat(sps), in0=flat(sbs), scalar=0.0, in1=flat(sps), op0=ALU.max, op1=ALU.add).then_inc(sem("samples_dve"), 1)
            row_sum(0)
            dve.wait_ge(*signal("c_pT", 1))
            chain(V.tensor_copy(pcT[0:NC, :], bank[2][0:NC, 0:64]))
            V.tensor_reduce(s64[0:NC, 3, 0:16], pcT[0:NC, :].rearrange("p (k g) -> p k g", g=G), AX.X, ALU.add).then_inc(sem("samples_dve"), 1)
            cp_out(0)
            cp_max(1)
            row_reciprocal(0)
            dve.wait_ge(*signal("c_imp", 1))
            imp = s64[0:16, 4, 0:NSEL]
            chain(V.tensor_copy(imp, bank[2][0:16, 0:NSEL]))
            chain(V.memset(imp[:, 0:1], FORCE))
            chain(V.memset(imp[:, NSEL - 2:NSEL], FORCE))
            im_i, im_j = over(imp, 1, NSEL), over(imp, 2, NSEL)
            chain(V.tensor_tensor(rankA[0:16], im_i, im_j, ALU.is_gt))
            chain(V.tensor_tensor(rankB[0:16], im_i, im_j, ALU.is_equal))
            chain(V.tensor_tensor(rankB[0:16], rankB[0:16], K("lower")[0:16].rearrange("p (j i) -> p j i", j=NSEL), ALU.mult))
            chain(V.tensor_tensor(rankA[0:16], rankA[0:16], rankB[0:16], ALU.add))
            chain(V.tensor_reduce(s64[0:16, 6, 0:NSEL], rankA[0:16], AX.X, ALU.add))
            V.tensor_scalar(s64[0:16, 5, 0:NSEL], s64[0:16, 6, 0:NSEL], float(TOPN), None, ALU.is_lt).then_inc(sem("samples_dve"), 1)
            cp_soft(1)
            dve.wait_ge(*signal("s_sp", 1))
            chain(V.memset(suf[:, :, NPG - 1, :], 0.0))
            for n in range(NPG - 2, -1, -1):
                ins = V.tensor_tensor(suf[:, :, n, :], suf[:, :, n + 1, :], sps[:, :, n + 1, :], ALU.add)
                if n:
                    chain(ins)
            ins.then_inc(sem("samples_dve"), 1)
            cp_out(1)
            cp_max(2)
            dve.wait_ge(*signal("c_selT", 1))
            V.tensor_tensor(selx[0:NSEL], over(bank[2][0:NSEL, 0:16], 1, NPG + 1),
                                 K("pagemap")[0:NSEL].rearrange("p (n k) -> p n k", k=16), ALU.mult).then_inc(sem("samples_dve"), 1)
            cp_soft(2)
            dve.wait_ge(*signal("c_mask", 1))
            V.tensor_scalar(selm.rearrange("p n k -> p (n k)"), bank[2][:, 0:272], -1.0, -NEG, ALU.add, ALU.mult).then_inc(sem("samples_dve"), 1)
            dve.wait_ge(*signal("c_selm", 1))
            for b in range(B):
                v = slc[:, b].rearrange("p n (k g) -> p n k g", k=2)
                chain(V.tensor_tensor(v, v, over(selm[:, :, 2 * b:2 * b + 2], 3, G), ALU.add))
            row_max(1)
            cp_out(2)
            cp_max(3)
            row_max_diagonal(1)
            cp_soft(3)
            row_max_subtract(1)
            cp_out(3)
            row_sum(1)
            row_reciprocal(1)
            dve.wait_ge(*signal("s_c", 1))
            for c in range(2):
                f = sbs[:, 4 * c:4 * c + 4].rearrange("p b n j -> p (b n j)")
                ins = V.tensor_tensor(f, f, bank[2 + c][:, :], ALU.add)
                if c == 0:
                    chain(ins)
            ins.then_inc(sem("samples_dve"), 1)
            dve.wait_ge(sem("cp_tr"), 2 * NT)

            def sb_soft(hd, i):
                m, n = 4 * hd + 3 - i, SEQ - i * P
                dve.wait_ge(sem("sb_ln"), m + 1)
                if m >= 2:
                    dve.wait_ge(sem("sb_c"), m - 1)
                    dve.wait_ge(sem("sb_run"), m - 1)
                s = spb[:, m % 2]
                chain(V.scalar_tensor_tensor(out=s[:, 0:n], in0=bank[m % 2][:, 0:n], scalar=0.0, in1=ebuf[:, m % 2, 0:n],
                                             op0=ALU.max, op1=ALU.add))
                V.tensor_tensor(s[:, 0:P], s[:, 0:P], K("before"), ALU.mult).then_inc(sem("sb_sp"), 1)

            def sb_amask(hd, i):
                m = 4 * hd + 3 - i
                dve.wait_ge(sem("sb_a"), m + 1)
                V.tensor_tensor(abuf[:, m % 2, 0:P], abuf[:, m % 2, 0:P], K("before"), ALU.mult).then_inc(sem("sb_am"), 1)

            def n_max(n):
                i = n % 4
                dve.wait_ge(sem("n_qk"), n + 1)
                if n >= 2:
                    dve.wait_ge(sem("n_exp"), n - 1)
                pb = bank[3 + n % 2]
                chain(V.tensor_tensor(pb[:, i * P:(i + 1) * P], pb[:, i * P:(i + 1) * P], K("causal"), ALU.add))
                V.tensor_reduce(st[:, 160 + n % 4:161 + n % 4], pb[:, 0:(i + 1) * P], AX.X, ALU.max, negate=True).then_inc(sem("n_max"), 1)

            def n_gate(n):
                hd, br, i, c = n // 8, (n // 4) % 2, n % 4, 168 + n % 4
                dve.wait_ge(sem("n_exp"), n + 1)
                chain(V.reciprocal(st[:, c:c + 1], st[:, c - 4:c - 3]))
                gate = z[:, i, O_G + 3 * hd + 1 + br:O_G + 3 * hd + 2 + br]
                chain(V.tensor_tensor(st[:, c:c + 1], st[:, c:c + 1], gate, ALU.mult))

            def n_out(n):
                hd, i, c = n // 8, n % 4, 168 + n % 4
                dve.wait_ge(sem("n_pv"), n + 1)
                o = o_n[:, i, place(hd) * DH:(place(hd) + 1) * DH]
                V.scalar_tensor_tensor(out=o, in0=bank[6][:, 0:DH], scalar=st[:, c:c + 1], in1=o, op0=ALU.mult, op1=ALU.add).then_inc(sem("n_out"), 1)
                dve.wait_ge(sem("n_out"), n + 1)

            def page_values(b, n):
                u, r = n % 8, n // 8
                dve.wait_ge(sem(f"ring_in{u}"), (2 * B + 2 * b + r + 1) * 16)
                if n == 0 and b >= 2:
                    dve.wait_ge(sem("vsum_mm"), b - 1)
                if n == 0 and b == 0:
                    dve.wait_ge(*signal("s_a", 1))
                page = ring[:, u, :]
                V.tensor_tensor((page if n else vsum[:, b % 2, :]).rearrange("p (h d) -> p h d", h=H),
                                page.rearrange("p (h d) -> p h d", h=H), over(sbs[:, b, n, :], 2, DH), ALU.mult
                                ).then_inc(sem("weighted" if n else "ring_free0"), 1)

            for n in range(8 * H + 2):
                hd, k = n // 8, n % 8
                if n < 8 * H:
                    if k == 0:
                        sb_soft(hd, 3)
                    n_max(n)
                    if k == 0:
                        sb_soft(hd, 2)
                    if k in (2, 3):
                        sb_soft(hd, 3 - k)
                    if 1 <= k < 5:
                        sb_amask(hd, 4 - k)
                    page_values(hd, 2 * k)
                if 1 <= n < 8 * H + 1:
                    n_gate(n - 1)
                if n >= 2:
                    n_out(n - 2)
                if n < 8 * H:
                    page_values(hd, 2 * k + 1)

            dve.wait_ge(sem("sb_out"), H)
            dve.wait_ge(sem("sb_run"), 4 * H)
            dve.wait_ge(sem("sb_pv"), 4 * H)
            V.memset(st[0:1, 211:212], 0.0).then_inc(sem("samples_dve"), 1)
            dve.wait_ge(*signal("v_mm", 1))
            gb = ofs[:, 0:3, :].rearrange("p a b -> p (a b)")
            chain(V.tensor_copy(gb, bank[4][:, 0:192]))
            g3 = gb.rearrange("p (c r) -> p c r", r=3)
            acc, tmp = ofs[:, 3, :], ofs[:, 4, :]
            chain(V.tensor_tensor(acc, bank[7][:, 192:256], g3[:, :, 0], ALU.mult))
            for br in range(2):
                chain(V.tensor_tensor(tmp, bank[7][:, 64 + 64 * br:128 + 64 * br], ofs[:, 5 + br, :], ALU.mult))
                chain(V.tensor_tensor(tmp, tmp, g3[:, :, 1 + br], ALU.mult))
                chain(V.tensor_tensor(acc, acc, tmp, ALU.add))
            mx = ofs[:, 8, :].rearrange("p (k b) -> p k b", k=KD)
            a3 = acc.rearrange("p (b j) -> p b j", b=B)
            chain(V.tensor_copy(mx[:, 0:4, :], bank[7][:, 0:4 * B].rearrange("p (t b) -> p t b", t=4)))
            for kh in range(2):
                lo = kh * DH
                chain(V.tensor_copy(mx[lo:lo + DH, 4:8, :], a3[lo:lo + DH, :, kh * G:(kh + 1) * G].rearrange("p b g -> p g b")))
            V.tensor_tensor(ofs[:, 9, :], ofs[:, 8, :], ofs[:, 8, :], ALU.mult).then_inc(sem("samples_dve"), 1)
            dve.wait_ge(*signal("v_ss", 1))
            V.tensor_reduce(st[:, 48:64].rearrange("p (a b) -> p a b", a=2), bank[3][:, 0:64].rearrange("p (a t b) -> p a b t", a=2, t=4), AX.X, ALU.add).then_inc(sem("samples_dve"), 1)
            dve.wait_ge(*signal("v_rt", 1))
            chain(V.reciprocal(st[:, 128:144], st[:, 64:80]))
            for a in range(2):
                v = mx[:, 4 * a:4 * a + 4, :]
                chain(V.tensor_tensor(v, v, over(st[:, 128 + 8 * a:136 + 8 * a], 1, 4), ALU.mult))
            v = act2[:, 0:64].rearrange("p (k b) -> p k b", k=KD)
            chain(V.tensor_tensor(v, mx, over(vcol[:, 16:24], 2, B), ALU.mult))
            chain(V.tensor_copy(hT_r[:, :, SEQ:TOK], v))
            chain(V.tensor_tensor(hT_lo_r[:, :, SEQ:TOK], v, hT[:, :, SEQ:TOK], ALU.subtract))
            for a, o in enumerate((o_sb, o_n)):
                for t in range(NT):
                    chain(V.tensor_tensor_reduce(pbuf[:, 0, :], o[:, t, :], o[:, t, :], 1.0, 0.0,
                                                 ALU.mult, ALU.add, st[:, 88 + 4 * a + t:89 + 4 * a + t]))
            V.memset(st[0:1, 213:214], 0.0).then_inc(sem("samples_dve"), 1)
            dve.wait_ge(*signal("mix_rt", 1))
            chain(V.reciprocal(st[:, 144:152], st[:, 96:104]))
            for a, o in enumerate((o_sb, o_n)):
                for t in range(NT):
                    ins = V.tensor_scalar(o[:, t, :], o[:, t, :], st[:, 144 + 4 * a + t:145 + 4 * a + t], None, ALU.mult)
                    if 4 * a + t < 7:
                        chain(ins)
            ins.then_inc(sem("mix_ready"), 1)
            for k in range(KD):
                dve.wait_ge(sem("hT_high"), 8 + k + 1)
                V.scalar_tensor_tensor(out=hT_lo_r[:, k, 0:SEQ], in0=bank[k % 2][:, :], scalar=vcol[:, 16 + k:17 + k],
                                       in1=hT[:, k, 0:SEQ], op0=ALU.mult, op1=ALU.subtract).then_inc(sem("mixT_ev"), 1)
            dve.wait_ge(sem("mixT_ev"), KD)
            V.memset(st[0:1, 214:215], 0.0).then_inc(sem("mix_ready"), 1)
            dve.wait_ge(sem("x2_in"), 32)
            for n in range(2 * T5):
                t, c = n // 2, n % 2
                dve.wait_ge(sem("out_mm"), n + 1)
                xv = x[0:rows[t], t, c * 512:(c + 1) * 512]
                V.tensor_tensor(xv, xv, bank[4 + n % 4][0:rows[t], :], ALU.add).then_inc(sem("res_ev"), 1)
                if c == 1:
                    dve.wait_ge(sem("res_ev"), n + 1)
                    squares(h2, t, chain if t < NT - 1 else lambda ins: ins.then_inc(sem("ss"), 1))
                    if t == NT - 1:
                        row_scales(h2, range(NT), 2).then_inc(sem("h_ready"), 1)
            gained(8, 1)
            row_scales(h2, [NT], 3).then_inc(sem("h_ready"), 1)
            gained_samples(8, 1)
            dve.wait_ge(sem("hT_ev"), 18)

            def low_parts(u, n):
                dve.wait_ge(sem(f"w_hi{u}"), n + W0 + 1)
                V.tensor_tensor(w_lo_r[u], w_raw[u], w_hi[u], ALU.subtract).then_inc(sem(f"w_lo{u}"), 1)

            def down_out(v, i, part):
                dve.wait_ge(sem("w_used1"), i * 2 + (v + 16 * part + 8) + 1 + 1)
                dve.wait_ge(sem(f"y_mm{v}"), i + 4 * part + 1)
                V.tensor_copy(yT[v][:, 0:HALF], bank[v][:, 0:HALF])
                V.tensor_copy(yT[v][:, HALF:TOK], bank[2 + v][:, 0:HALF]).then_inc(sem(f"dn_ev{v}"), 1)

            def down_residual(v, i, part):
                dve.wait_ge(sem(f"y_mm{v}"), i + 4 * part + 1 + 1)
                xv = x[:, 0:NT, ds(i * (2 * P) + v * P, P)]
                V.tensor_tensor(xv, xv, bank[4 + v].rearrange("p (t c) -> p t c", t=NT), ALU.add)
                xv = x[0:B, NT, ds(i * (2 * P) + v * P, P)]
                V.tensor_tensor(xv, xv, bank[6 + v][0:B, 0:P], ALU.add).then_inc(sem(f"y_ev{v}"), 1)

            def ahead(v, i, part, both=True):
                low_parts(1, i * 2 + (v + 16 * part + 8))
                if both:
                    low_parts(0, i * 2 + (v + 16 * part + 9))

            low_parts(0, 0)
            for part in range(2):
                with Turns(chain, FH // 2, 4) as i:
                    for u in range(2):
                        low_parts(1 - u, i + (u + 16 * part))
                        dve.wait_ge(sem(f"up_ev{u}"), i + 8 * part + 1 + 1)
                        hi, lo = (a[:, ds(i * 2 + u, 1), :].rearrange("p o c -> p (o c)") for a in (aT_r, aT_lo_r))
                        chain(V.tensor_tensor(act2, relu[:, u, :], relu[:, u, :], ALU.mult))
                        chain(V.tensor_copy(hi, act2))
                        V.tensor_tensor(lo, act2, aT[:, ds(i * 2 + u, 1), :].rearrange("p o c -> p (o c)"), ALU.subtract).then_inc(sem(f"a_ready{u}"), 1)
                        dve.wait_ge(sem(f"a_ready{u}"), i + 8 * part + 1 + 1)
                last = KD // 2 - 1
                ahead(0, 0, part)
                down_out(0, 0, part)
                with dve.Fori(0, last) as i:
                    ahead(1, i, part)
                    down_out(1, i, part)
                    down_residual(0, i, part)
                    ahead(0, i + 1, part)
                    down_out(0, i + 1, part)
                    down_residual(1, i, part)
                ahead(1, last, part, part == 0)
                down_out(1, last, part)
                down_residual(0, last, part)
                down_residual(1, last, part)
                for u in range(2):
                    dve.wait_ge(sem(f"y_ev{u}"), 4 * part + 4 + 1)
            for t in (0, 1):
                squares(h2, t, chain)
            squares(h2, NT, lambda ins: ins.then_inc(sem("ss"), 1))
            dve.wait_ge(sem("rt"), 4)
            chain(V.reciprocal(st[:, 16:21], st[:, 8:13]))
            dve.wait_ge(sem("gfin_in"), 16)
            for t in range(T5):
                V.scalar_tensor_tensor(out=h2[0:rows[t], t, :], in0=x[0:rows[t], t, :], scalar=st[0:rows[t], 16 + t:17 + t],
                                       in1=gfin[0:rows[t], :], op0=ALU.mult, op1=ALU.mult).then_inc(sem("y_ready"), 1)

        @block.gpsimd
        def _(pool):
            G_ = nc.gpsimd
            prime(pool, "pool")

            G_.memset(z[:, NT, :], 0.0).then_inc(sem("z_zero"), 1)
            pool.wait_ge(sem("w_hi0"), 1)
            G_.tensor_tensor(win_r[0], win[0], win_hi[0], ALU.subtract).then_inc(sem("w_lo0"), 1)
            pool.wait_ge(sem("qkT_mm"), 15)
            pool.wait_ge(sem("sb_stored"), 16)

            def permute(c, u, n):
                for kv in range(2):
                    if c:
                        pool.wait_ge(sem(f"hid_mm{kv}"), c)
                    for hh in range(KVH):
                        ins = G_.tensor_copy(per(kv, hh)[0:n], nat[u][0:n, :, kv, hh, :])
                    ins.then_inc(sem("perm0" if kv == 0 else f"perm1_{u}"), 1)

            for c in range(B):
                pool.wait_ge(sem(f"nat_in{c % 2}"), (c // 2 + 1) * (16 * NPG))
                permute(c, c % 2, NCH)
            pool.wait_ge(sem("nat_in0"), 4 * 16 * NPG + 16)
            permute(B, 0, NCP + 1)
            pool.wait_ge(*signal("s_d", 1))
            def run_zero(hd):
                if hd:
                    pool.wait_ge(sem("sb_c"), 4 * hd)
                    pool.wait_ge(sem("sb_run"), 4 * hd)
                G_.memset(srun[:, :], 0.0).then_inc(sem("run_zero"), 1)
                pool.wait_ge(sem("run_zero"), hd + 1)

            def run_add(hd, i):
                m = 4 * hd + 3 - i
                pool.wait_ge(sem("sb_sp"), m + 1)
                pool.wait_ge(sem("sb_c"), m + 1)
                if i < 3:
                    pool.wait_ge(sem("sb_run"), m)
                G_.tensor_tensor(srun[:, i * P:SEQ], srun[:, i * P:SEQ], spb[:, m % 2, 0:SEQ - i * P], ALU.add).then_inc(sem("sb_run"), 1)

            def page_add(b, n):
                u = n % 8
                pool.wait_ge(sem("weighted"), (NPG - 1) * b + n)
                if n == 1:
                    pool.wait_ge(sem("ring_free0"), 2 * B + 2 * b + 1 + 1)
                else:
                    v = (n - 1) // 8
                    pool.wait_ge(sem(f"ring_free{(n - 1) % 8}"), 2 * B + 2 * b + v + 1 + 1)
                G_.tensor_tensor(vsum[:, b % 2, :], vsum[:, b % 2, :], ring[:, u, :], ALU.add).then_inc(sem(f"ring_free{u}"), 1)

            for n in range(8 * H):
                hd, k = n // 8, n % 8
                if k == 0:
                    run_zero(hd)
                if k in (0, 1, 3, 4):
                    run_add(hd, {0: 3, 1: 2, 3: 1, 4: 0}[k])
                for p in (2 * k, 2 * k + 1):
                    if p:
                        page_add(hd, p)

            for k in range(0, KD, 2):
                pool.wait_ge(sem("wout_hi"), k // 2 + 1)
                G_.tensor_tensor(wout_r[:, k:k + 2], wout[:, k:k + 2], wout_hi[:, k:k + 2], ALU.subtract).then_inc(sem("wout_lo"), 1)

_INS = ["x_prompt", "x_sample", "cache_sb_kv", "cache_nsa_cmp_kv", "cache_nsa_slc_kv", "state_nsa_win_kv", "page_table",
        "w_in", "w_cmp_k1", "w_cmp_k2", "w_cmp_v1", "w_cmp_v2", "pe_cmp_k", "pe_cmp_v", "g_sb_out", "g_nsa_out", "w_out",
        "g_attn_norm", "g_mlp_norm", "w_up", "w_down", "g_final"]
_OUTS = [("y_p", (1, SEQ, D)), ("y_s", (B, 1, D)), ("sb_p", (1, 1, SEQ, 2, H, DH)), ("sb_s", (1, B, 1, 2, H, DH)),
         ("cmp_p", (1, 1, SEQ, 2, KVH, DH)), ("cmp_s", (1, B, 1, 2, KVH, DH)),
         ("slc_p", (1, 1, SEQ, 2, KVH, DH)), ("slc_s", (1, B, 1, 2, KVH, DH)),
         ("win_p", (1, 1, SEQ, 2, KVH, DH)), ("win_s", (1, B, WIN, 2, KVH, DH))]


def build(nc, shapes):
    A = {n: nc.dram_tensor(f"in_{n}_dram", s, d, kind="ExternalInput").ap() for n, (s, d) in shapes.items()}
    O = {n: nc.dram_tensor(f"out_{n}_dram", s, F32, kind="ExternalOutput").ap() for n, s in _OUTS}
    decoder_step(nc, A, O)


def kernel(**inputs):
    import concourse.bacc as bacc
    from concourse.bass_utils import run_bass_kernel_spmd as run

    arrays = {n: np.ascontiguousarray(inputs[n]) for n in _INS}
    arrays["consts"] = shape_constants()
    nc = bacc.Bacc("TRN2", target_bir_lowering=False, num_devices=1)
    build(nc, {n: (a.shape, mybir.dt.from_np(a.dtype)) for n, a in arrays.items()})
    r = run(nc, [{f"in_{n}_dram": a for n, a in arrays.items()}], core_ids=[0])
    return tuple(r.results[0][f"out_{n}_dram"] for n, _ in _OUTS)
```
